# Optimizing a Trainium2 kernel written in Bass

```python
import jax
import jax.numpy as jnp
from jax import lax
import numpy as np

D_MODEL = 1024
BATCH = 1
SEQ = 512
DEPTH = 2
DEC_BATCH = 8
DEC_SEQ = 1
PAST_LEN = 4096
PAGE_SIZE = 128

N_EVEN = (DEPTH + 1) // 2
N_ODD = DEPTH // 2
D_PLE = 256
EPS = 1e-6
CONV_W = 4
D_A = 512
N_BLK_A = 8
BW_A = D_A // N_BLK_A
LRU_C = 8.0
H_B = 8
HD_B = 64
D_B = H_B * HD_B
R_W = 64
R_A = 64
R_G = 128
D_BPROJ = 3 * D_B + R_W + R_A + R_G
GN_EPS_B = 64e-5
IN_AB = 2 * D_A + D_BPROJ
H_C = 8
P_C = 64
D_C = H_C * P_C
G_C = 2
HG_C = H_C // G_C
N_C = 128
D_XBC = D_C + 2 * G_C * N_C
CHUNK_C = 64
H_D = 4
DK_D = 64
DV_D = 128
K_D = H_D * DK_D
V_D = H_D * DV_D
R_ALPHA = 16
GATE_NORM = 16.0
CHUNK_D = 32
IN_CD = D_C + D_XBC + H_C + 2 * K_D + 2 * V_D + R_ALPHA
D_FF = 2816
N_EXP = 8
TOP_K = 2
D_FF_E = 1408

kernel_name = 'hybrid_rglru_rwkv7_ssd_gla_step'

def rmsnorm(x, g):
    xf = x.astype(jnp.float32)
    y = xf * lax.rsqrt(jnp.mean(xf * xf, axis=-1, keepdims=True) + EPS)
    return (y * g.astype(jnp.float32)).astype(x.dtype)

def split_cols(t, sizes):
    idx = [int(s) for s in np.cumsum(sizes)[:-1]]
    return jnp.split(t, idx, axis=-1)

def causal_conv(x, buf, w, b):
    L = x.shape[1]
    xx = jnp.concatenate([buf.astype(x.dtype), x], axis=1)
    y = b + sum(xx[:, k:k + L] * w[k] for k in range(CONV_W))
    return y, xx[:, L:]

def to_chunks(t, q):
    bsz, L = t.shape[:2]
    n = -(-L // q)
    t = jnp.pad(t, [(0, 0), (0, n * q - L)] + [(0, 0)] * (t.ndim - 2))
    return jnp.moveaxis(t.reshape((bsz, n, q) + t.shape[2:]), 1, 0)

def from_chunks(t, L):
    n, bsz, q = t.shape[:3]
    return jnp.moveaxis(t, 0, 1).reshape((bsz, n * q) + t.shape[3:])[:, :L]

def rglru(x, h0, w_r, b_r, w_i, b_i, lam):
    bsz, L, _ = x.shape
    xf = x.astype(jnp.float32)
    xb = xf.reshape(bsz, L, N_BLK_A, BW_A)
    r = jax.nn.sigmoid(jnp.einsum('blni,nij->blnj', xb, w_r).reshape(bsz, L, D_A) + b_r)
    i = jax.nn.sigmoid(jnp.einsum('blni,nij->blnj', xb, w_i).reshape(bsz, L, D_A) + b_i)
    log_a = -LRU_C * r * jax.nn.softplus(-lam)
    a = jnp.exp(log_a)
    u = jnp.sqrt(-jnp.expm1(2.0 * log_a)) * (i * xf)

    def step(h, au):
        h = au[0] * h + au[1]
        return h, h

    hT, hs = lax.scan(step, h0.astype(jnp.float32), (a.swapaxes(0, 1), u.swapaxes(0, 1)))
    return hs.swapaxes(0, 1), hT

def rwkv7(proj, shift0, s0, mu, w0, w2, a0, a2, g2, k_k, k_a, r_k, ln_w, ln_b):
    bsz, L, _ = proj.shape
    prev = jnp.concatenate([shift0[:, None].astype(proj.dtype), proj[:, :-1]], axis=1)
    xs = (proj + (prev - proj) * mu).astype(jnp.float32)
    r, k, v, wl, al, gl = split_cols(xs, [D_B, D_B, D_B, R_W, R_A, R_G])
    w_log = -jax.nn.softplus(-(w0 + jnp.tanh(wl) @ w2)) - 0.5
    decay = jnp.exp(-jnp.exp(w_log))
    a = jax.nn.sigmoid(a0 + al @ a2)
    g = jax.nn.sigmoid(gl) @ g2
    hd = lambda t: t.reshape(bsz, L, H_B, HD_B)
    kk = hd(k * k_k)
    kk = kk * lax.rsqrt(jnp.maximum(jnp.sum(kk * kk, axis=-1, keepdims=True), 1e-12))
    k = hd(k * (1.0 + (a - 1.0) * k_a))
    r, v, decay, a = hd(r), hd(v), hd(decay), hd(a)

    def step(S, inp):
        r_t, k_t, v_t, d_t, kk_t, a_t = inp
        S = (S * d_t[:, :, None, :]
             - jnp.einsum('bhvk,bhk->bhv', S, kk_t)[..., None] * (kk_t * a_t)[:, :, None, :]
             + v_t[..., None] * k_t[:, :, None, :])
        return S, jnp.einsum('bhvk,bhk->bhv', S, r_t)

    sT, y = lax.scan(step, s0.astype(jnp.float32),
                     tuple(t.swapaxes(0, 1) for t in (r, k, v, decay, kk, a)))
    y = y.swapaxes(0, 1)
    mean = jnp.mean(y, axis=-1, keepdims=True)
    var = jnp.mean(jnp.square(y - mean), axis=-1, keepdims=True)
    y = ((y - mean) * lax.rsqrt(var + GN_EPS_B)).reshape(bsz, L, D_B) * ln_w + ln_b
    y = y + (jnp.sum(r * k * r_k, axis=-1, keepdims=True) * v).reshape(bsz, L, D_B)
    return y * g, proj[:, -1], sT

def ssd_scan(x, dt, A, Bm, Cm, s0):
    bsz, L = x.shape[:2]
    q = min(CHUNK_C, L)
    x = x.reshape(bsz, L, G_C, HG_C, P_C)
    dt = dt.reshape(bsz, L, G_C, HG_C)
    la = dt * A.reshape(G_C, HG_C)
    causal = jnp.tril(jnp.ones((q, q), dtype=bool))[None, :, :, None, None]

    def step(S, inp):
        x_c, dt_c, la_c, b_c, c_c = inp
        cum = jnp.cumsum(la_c, axis=1)
        seg = jnp.exp(jnp.where(causal, cum[:, :, None] - cum[:, None, :], -jnp.inf))
        cb = jnp.einsum('bign,bjgn->bijg', c_c, b_c)
        y = jnp.einsum('bijg,bijgh,bjgh,bjghp->bighp', cb, seg, dt_c, x_c)
        y = y + jnp.einsum('bign,bghpn->bighp', c_c, S) * jnp.exp(cum)[..., None]
        w_end = jnp.exp(cum[:, -1:] - cum) * dt_c
        S = (S * jnp.exp(cum[:, -1])[..., None, None]
             + jnp.einsum('bjgh,bjghp,bjgn->bghpn', w_end, x_c, b_c))
        return S, y

    sT, y = lax.scan(step, s0.reshape(bsz, G_C, HG_C, P_C, N_C),
                     tuple(to_chunks(t, q) for t in (x, dt, la, Bm, Cm)))
    return from_chunks(y, L).reshape(bsz, L, H_C, P_C), sT.reshape(bsz, H_C, P_C, N_C)

def gla_scan(q, k, v, la, s0):
    bsz, L = q.shape[:2]
    c = min(CHUNK_D, L)
    causal = jnp.tril(jnp.ones((c, c), dtype=bool))

    def step(S, inp):
        q_c, k_c, v_c, la_c = inp
        b = jnp.cumsum(la_c, axis=1)
        qe = q_c * jnp.exp(b)
        att = jnp.where(causal, jnp.einsum('bihd,bjhd->bhij', qe, k_c * jnp.exp(-b)), 0.0)
        o = jnp.einsum('bhij,bjhv->bihv', att, v_c) + jnp.einsum('bihd,bhdv->bihv', qe, S)
        b_end = b[:, -1]
        S = (S * jnp.exp(b_end)[..., None]
             + jnp.einsum('bjhd,bjhv->bhdv', k_c * jnp.exp(b_end[:, None] - b), v_c))
        return S, o

    sT, o = lax.scan(step, s0, tuple(to_chunks(t, c) for t in (q, k, v, la)))
    return from_chunks(o, L), sT

def mixer_ab(u, conv_buf, h0, shift0, wkv0, w_in, w_out, conv_w, conv_b, w_r, b_r, w_i, b_i, lam,
             mu, w0, w2, a0, a2, g2, k_k, k_a, r_k, ln_w, ln_b):
    xa, ga, pb = split_cols(u @ w_in, [D_A, D_A, D_BPROJ])
    xa, conv_new = causal_conv(xa, conv_buf, conv_w, conv_b)
    ha, h_new = rglru(xa, h0, w_r, b_r, w_i, b_i, lam)
    y_a = jax.nn.gelu(ga.astype(jnp.float32)) * ha
    y_b, shift_new, wkv_new = rwkv7(pb, shift0, wkv0, mu, w0, w2, a0, a2, g2, k_k, k_a, r_k, ln_w, ln_b)
    out = jnp.concatenate([y_a, y_b], axis=-1).astype(u.dtype) @ w_out
    return out, conv_new, h_new, shift_new, wkv_new

def mixer_cd(u, conv_buf, ssd0, gla0, w_in, w_out, conv_w, conv_b, dt_bias, a_log, d_skip, ssd_norm,
             alpha_up, alpha_b, gla_norm):
    bsz, L, _ = u.shape
    z, xbc, dt_raw, q, k, v, g, al = split_cols(
        u @ w_in, [D_C, D_XBC, H_C, K_D, K_D, V_D, V_D, R_ALPHA])
    xbc, conv_new = causal_conv(xbc, conv_buf, conv_w, conv_b)
    xbc = jax.nn.silu(xbc.astype(jnp.float32))
    xs, Bm, Cm = split_cols(xbc, [D_C, G_C * N_C, G_C * N_C])
    xs = xs.reshape(bsz, L, H_C, P_C)
    dt = jax.nn.softplus(dt_raw.astype(jnp.float32) + dt_bias)
    A = -jnp.exp(a_log.astype(jnp.float32))
    y, ssd_new = ssd_scan(xs, dt, A, Bm.reshape(bsz, L, G_C, N_C), Cm.reshape(bsz, L, G_C, N_C),
                          ssd0.astype(jnp.float32))
    y = (y + d_skip[:, None] * xs).reshape(bsz, L, D_C)
    y_c = rmsnorm(y * jax.nn.silu(z.astype(jnp.float32)), ssd_norm)
    la = jax.nn.log_sigmoid((al @ alpha_up + alpha_b).astype(jnp.float32)) / GATE_NORM
    heads = lambda t, d: t.astype(jnp.float32).reshape(bsz, L, H_D, d)
    o, gla_new = gla_scan(heads(q, DK_D) * DK_D ** -0.5, heads(k, DK_D), heads(v, DV_D),
                          heads(la, DK_D), gla0.astype(jnp.float32))
    y_d = rmsnorm(o, gla_norm).reshape(bsz, L, V_D) * jax.nn.silu(g.astype(jnp.float32))
    out = jnp.concatenate([y_c, y_d], axis=-1).astype(u.dtype) @ w_out
    return out, conv_new, ssd_new, gla_new

def swiglu(x, wg, wu, wd):
    return (jax.nn.silu(x @ wg) * (x @ wu)) @ wd

def moe_swiglu(x, w_router, wg, wu, wd):
    bsz, L, D = x.shape
    xt = x.reshape(bsz * L, D)
    probs = jax.nn.softmax((xt @ w_router).astype(jnp.float32), axis=-1)
    top_p, top_i = lax.top_k(probs, TOP_K)
    top_p = top_p / jnp.sum(top_p, axis=-1, keepdims=True)
    gates = jnp.einsum('tk,tke->te', top_p,
                       jax.nn.one_hot(top_i, N_EXP, dtype=jnp.float32)).astype(x.dtype)
    out = jnp.zeros_like(xt)
    for e in range(N_EXP):
        out = out + gates[:, e:e + 1] * swiglu(xt, wg[e], wu[e], wd[e])
    return out.reshape(bsz, L, D)

def trunk(x, p, states, prm):
    lru_conv, lru_h, rwkv_shift, rwkv_wkv, ssd_conv, ssd_st, gla_st = states
    new_ab, new_cd = [], []
    h = x
    for i in range(DEPTH):
        j = i // 2
        u = rmsnorm(h, prm['norm_mix'][i])
        if i % 2 == 0:
            mix, *st = mixer_ab(
                u, lru_conv[j], lru_h[j], rwkv_shift[j], rwkv_wkv[j],
                prm['w_in_ab'][j], prm['w_out_ab'][j], prm['lru_conv_w'][j], prm['lru_conv_b'][j],
                prm['lru_w_r'][j], prm['lru_b_r'][j], prm['lru_w_i'][j], prm['lru_b_i'][j],
                prm['lru_lambda'][j], prm['rwkv_mu'][j], prm['rwkv_w0'][j], prm['rwkv_w2'][j],
                prm['rwkv_a0'][j], prm['rwkv_a2'][j], prm['rwkv_g2'][j], prm['rwkv_k_k'][j],
                prm['rwkv_k_a'][j], prm['rwkv_r_k'][j], prm['rwkv_ln_w'][j], prm['rwkv_ln_b'][j])
            new_ab.append(st)
            h = h + mix
            h = h + swiglu(rmsnorm(h, prm['norm_ffn'][i]), prm['ffn_w_gate'][j],
                           prm['ffn_w_up'][j], prm['ffn_w_down'][j])
        else:
            mix, *st = mixer_cd(
                u, ssd_conv[j], ssd_st[j], gla_st[j],
                prm['w_in_cd'][j], prm['w_out_cd'][j], prm['ssd_conv_w'][j], prm['ssd_conv_b'][j],
                prm['ssd_dt_bias'][j], prm['ssd_a_log'][j], prm['ssd_d'][j], prm['ssd_norm_w'][j],
                prm['gla_alpha_up'][j], prm['gla_alpha_b'][j], prm['gla_norm_w'][j])
            new_cd.append(st)
            h = h + mix
            h = h + moe_swiglu(rmsnorm(h, prm['norm_ffn'][i]), prm['moe_router'][j],
                               prm['moe_w_gate'][j], prm['moe_w_up'][j], prm['moe_w_down'][j])
        gate = jax.nn.sigmoid(rmsnorm(h, prm['norm_ple'][i]) @ prm['w_ple_gate'][i])
        h = h + gate * (p[i] @ prm['w_ple_proj'][i])
    y = rmsnorm(h, prm['norm_final'])
    out_ab = [jnp.stack([st[n] for st in new_ab]).astype(ref.dtype)
              for n, ref in enumerate((lru_conv, lru_h, rwkv_shift, rwkv_wkv))]
    out_cd = [jnp.stack([st[n] for st in new_cd]).astype(ref.dtype)
              for n, ref in enumerate((ssd_conv, ssd_st, gla_st))]
    return y, out_ab + out_cd

def setup_inputs(seed: int = 0) -> dict:
    key = jax.random.key(seed)
    keys = jax.random.split(key, 80)
    count = [0]

    def nk():
        count[0] += 1
        return keys[count[0] - 1]

    def nrm(shape, scale):
        return jax.random.normal(nk(), shape, jnp.float32) * scale

    def unif(shape, lo, hi):
        return jax.random.uniform(nk(), shape, jnp.float32, lo, hi)

    def gain(shape):
        return 1.0 + nrm(shape, 0.02)

    D = D_MODEL
    a_init = unif((N_EVEN, D_A), 0.9, 0.999) ** (1.0 / LRU_C)
    lru_lambda = jnp.log(a_init) - jnp.log1p(-a_init)
    dt0 = jnp.exp(unif((N_ODD, H_C), float(np.log(1e-3)), float(np.log(1e-1))))
    ssd_dt_bias = dt0 + jnp.log(-jnp.expm1(-dt0))
    return {
        'x_prompt': nrm((BATCH, SEQ, D), 1.0),
        'x_sample': nrm((DEC_BATCH, DEC_SEQ, D), 1.0),
        'p_prompt': nrm((DEPTH, BATCH, SEQ, D_PLE), 1.0),
        'p_sample': nrm((DEPTH, DEC_BATCH, DEC_SEQ, D_PLE), 1.0),
        'state_lru_conv': nrm((N_EVEN, DEC_BATCH, CONV_W - 1, D_A), 1.0),
        'state_lru_h': nrm((N_EVEN, DEC_BATCH, D_A), 0.5),
        'state_rwkv_shift': nrm((N_EVEN, DEC_BATCH, D_BPROJ), 1.0),
        'state_rwkv_wkv': nrm((N_EVEN, DEC_BATCH, H_B, HD_B, HD_B), 0.3),
        'state_ssd_conv': nrm((N_ODD, DEC_BATCH, CONV_W - 1, D_XBC), 1.0),
        'state_ssd': nrm((N_ODD, DEC_BATCH, H_C, P_C, N_C), 0.1),
        'state_gla': nrm((N_ODD, DEC_BATCH, H_D, DK_D, DV_D), 0.3),
        'norm_mix': gain((DEPTH, D)),
        'norm_ffn': gain((DEPTH, D)),
        'norm_ple': gain((DEPTH, D)),
        'w_ple_gate': nrm((DEPTH, D, D), D ** -0.5),
        'w_ple_proj': nrm((DEPTH, D_PLE, D), D_PLE ** -0.5),
        'norm_final': gain((D,)),
        'w_in_ab': nrm((N_EVEN, D, IN_AB), D ** -0.5),
        'w_out_ab': nrm((N_EVEN, D_A + D_B, D), (D_A + D_B) ** -0.5),
        'lru_conv_w': nrm((N_EVEN, CONV_W, D_A), CONV_W ** -0.5),
        'lru_conv_b': nrm((N_EVEN, D_A), 0.01),
        'lru_w_r': nrm((N_EVEN, N_BLK_A, BW_A, BW_A), BW_A ** -0.5),
        'lru_b_r': nrm((N_EVEN, D_A), 0.01),
        'lru_w_i': nrm((N_EVEN, N_BLK_A, BW_A, BW_A), BW_A ** -0.5),
        'lru_b_i': nrm((N_EVEN, D_A), 0.01),
        'lru_lambda': lru_lambda,
        'rwkv_mu': unif((N_EVEN, D_BPROJ), 0.0, 1.0),
        'rwkv_w0': unif((N_EVEN, D_B), -6.0, -1.0),
        'rwkv_w2': nrm((N_EVEN, R_W, D_B), 0.1),
        'rwkv_a0': nrm((N_EVEN, D_B), 0.1),
        'rwkv_a2': nrm((N_EVEN, R_A, D_B), 0.1),
        'rwkv_g2': nrm((N_EVEN, R_G, D_B), R_G ** -0.5),
        'rwkv_k_k': 0.85 + nrm((N_EVEN, D_B), 0.02),
        'rwkv_k_a': gain((N_EVEN, D_B)),
        'rwkv_r_k': nrm((N_EVEN, H_B, HD_B), 0.1),
        'rwkv_ln_w': gain((N_EVEN, D_B)),
        'rwkv_ln_b': nrm((N_EVEN, D_B), 0.01),
        'ffn_w_gate': nrm((N_EVEN, D, D_FF), D ** -0.5),
        'ffn_w_up': nrm((N_EVEN, D, D_FF), D ** -0.5),
        'ffn_w_down': nrm((N_EVEN, D_FF, D), D_FF ** -0.5),
        'w_in_cd': nrm((N_ODD, D, IN_CD), D ** -0.5),
        'w_out_cd': nrm((N_ODD, D_C + V_D, D), (D_C + V_D) ** -0.5),
        'ssd_conv_w': nrm((N_ODD, CONV_W, D_XBC), CONV_W ** -0.5),
        'ssd_conv_b': nrm((N_ODD, D_XBC), 0.01),
        'ssd_dt_bias': ssd_dt_bias,
        'ssd_a_log': jnp.log(unif((N_ODD, H_C), 1.0, 16.0)),
        'ssd_d': gain((N_ODD, H_C)),
        'ssd_norm_w': gain((N_ODD, D_C)),
        'gla_alpha_up': nrm((N_ODD, R_ALPHA, K_D), R_ALPHA ** -0.5),
        'gla_alpha_b': nrm((N_ODD, K_D), 0.1),
        'gla_norm_w': gain((N_ODD, DV_D)),
        'moe_router': nrm((N_ODD, D, N_EXP), D ** -0.5),
        'moe_w_gate': nrm((N_ODD, N_EXP, D, D_FF_E), D ** -0.5),
        'moe_w_up': nrm((N_ODD, N_EXP, D, D_FF_E), D ** -0.5),
        'moe_w_down': nrm((N_ODD, N_EXP, D_FF_E, D), D_FF_E ** -0.5),
    }

def reference(x_prompt, x_sample, p_prompt, p_sample, state_lru_conv, state_lru_h, state_rwkv_shift,
              state_rwkv_wkv, state_ssd_conv, state_ssd, state_gla, norm_mix, norm_ffn, norm_ple,
              w_ple_gate, w_ple_proj, norm_final, w_in_ab, w_out_ab, lru_conv_w, lru_conv_b, lru_w_r,
              lru_b_r, lru_w_i, lru_b_i, lru_lambda, rwkv_mu, rwkv_w0, rwkv_w2, rwkv_a0, rwkv_a2,
              rwkv_g2, rwkv_k_k, rwkv_k_a, rwkv_r_k, rwkv_ln_w, rwkv_ln_b, ffn_w_gate, ffn_w_up,
              ffn_w_down, w_in_cd, w_out_cd, ssd_conv_w, ssd_conv_b, ssd_dt_bias, ssd_a_log, ssd_d,
              ssd_norm_w, gla_alpha_up, gla_alpha_b, gla_norm_w, moe_router, moe_w_gate, moe_w_up,
              moe_w_down):
    prm = dict(
        norm_mix=norm_mix, norm_ffn=norm_ffn, norm_ple=norm_ple, w_ple_gate=w_ple_gate,
        w_ple_proj=w_ple_proj, norm_final=norm_final, w_in_ab=w_in_ab, w_out_ab=w_out_ab,
        lru_conv_w=lru_conv_w, lru_conv_b=lru_conv_b, lru_w_r=lru_w_r, lru_b_r=lru_b_r,
        lru_w_i=lru_w_i, lru_b_i=lru_b_i, lru_lambda=lru_lambda, rwkv_mu=rwkv_mu, rwkv_w0=rwkv_w0,
        rwkv_w2=rwkv_w2, rwkv_a0=rwkv_a0, rwkv_a2=rwkv_a2, rwkv_g2=rwkv_g2, rwkv_k_k=rwkv_k_k,
        rwkv_k_a=rwkv_k_a, rwkv_r_k=rwkv_r_k, rwkv_ln_w=rwkv_ln_w, rwkv_ln_b=rwkv_ln_b,
        ffn_w_gate=ffn_w_gate, ffn_w_up=ffn_w_up, ffn_w_down=ffn_w_down, w_in_cd=w_in_cd,
        w_out_cd=w_out_cd, ssd_conv_w=ssd_conv_w, ssd_conv_b=ssd_conv_b, ssd_dt_bias=ssd_dt_bias,
        ssd_a_log=ssd_a_log, ssd_d=ssd_d, ssd_norm_w=ssd_norm_w, gla_alpha_up=gla_alpha_up,
        gla_alpha_b=gla_alpha_b, gla_norm_w=gla_norm_w, moe_router=moe_router,
        moe_w_gate=moe_w_gate, moe_w_up=moe_w_up, moe_w_down=moe_w_down)
    states_s = (state_lru_conv, state_lru_h, state_rwkv_shift, state_rwkv_wkv,
                state_ssd_conv, state_ssd, state_gla)
    n_prompt = x_prompt.shape[0]
    states_p = tuple(jnp.zeros((s.shape[0], n_prompt) + s.shape[2:], s.dtype) for s in states_s)
    y_prompt, st_p = trunk(x_prompt, p_prompt, states_p, prm)
    y_sample, st_s = trunk(x_sample, p_sample, states_s, prm)
    lc_p, lh_p, rs_p, rw_p, sc_p, ss_p, gs_p = st_p
    lc_s, lh_s, rs_s, rw_s, sc_s, ss_s, gs_s = st_s
    return (y_prompt, y_sample, lc_p, lh_p, rs_p, rw_p, sc_p, ss_p, gs_p,
            lc_s, lh_s, rs_s, rw_s, sc_s, ss_s, gs_s)


_drawn_inputs = setup_inputs


def setup_inputs(seed=0):
    import zlib

    import numpy as np

    out = dict(_drawn_inputs(seed))
    spreads = {}
    factors = {'norm_ple': 32.276,
     'norm_final': 24.236,
     'lru_b_r': 22.797,
     'lru_b_i': 17.294,
     'rwkv_k_k': 2.677,
     'rwkv_ln_w': 3.353,
     'rwkv_ln_b': 12.034,
     'gla_norm_w': 24.32,
     'ssd_d': 5.167,
     'ssd_norm_w': 22.672,
     'norm_ffn': 3.403}
    for name, (base, spread) in spreads.items():
        noise = np.random.default_rng([zlib.crc32(name.encode()), seed]).standard_normal(out[name].shape)
        drawn = base * np.exp(spread * noise) if base else spread * noise
        out[name] = jnp.asarray(drawn.astype(out[name].dtype))
    for name, factor in factors.items():
        out[name] = (out[name] * factor).astype(out[name].dtype)
    return out
```

```python
from contextlib import ExitStack

import numpy as np
import concourse.bass as bass
from concourse import mybir

F32 = mybir.dt.float32
ALU = mybir.AluOpType
ACT = mybir.ActivationFunctionType
AX = mybir.AxisListType

P = 128
SEQ = 512
NS = 8
T = SEQ + NS
HALF = T // 2
D = 1024
KD = D // P
EPS = 1e-6
GN_EPS = 64e-5
FF, FFE, NEXP = 2816, 1408, 8
KF, KE = FF // P, FFE // P
PAD = 547
SAMP = 3 + SEQ
SHW = 532
C0 = float(np.exp(-0.5))

RING = 6
SLAB = 1408

VECS = [("norm_mix0", 8), ("norm_ffn0", 8), ("norm_ple0", 8), ("norm_mix1", 8), ("norm_ffn1", 8),
        ("norm_ple1", 8), ("norm_final", 8), ("lru_w", 16), ("lru_b", 4), ("b_r", 4), ("b_i", 4), ("lam", 4),
        ("mu", 14), ("w0", 4), ("a0", 4), ("k_k", 4), ("k_a", 4), ("r_k", 4), ("ln_w", 4), ("ln_b", 4),
        ("ssd_w", 32), ("ssd_b", 8), ("ssd_norm", 4), ("ssd_d", 4), ("alpha_b", 2), ("gla_norm", 1),
        ("dt_bias", 1), ("a_log", 1)]
VCOL, NVEC = {}, 0
for _n, _w in VECS:
    VCOL[_n] = NVEC
    NVEC += _w

AB_TILES = [("xa", i) for i in range(4)] + [("x", 12), ("x", 13)] + [("x", i) for i in (4, 5, 6, 7)] \
    + [("x", i) for i in (0, 1, 2, 3)] + [("x", i) for i in (8, 9, 10, 11)] + [("ga", i) for i in range(4)]
NAB = len(AB_TILES)
NCD = 25
Q_AB = 0
Q_OUT0 = Q_AB + NAB
Q_GU = Q_OUT0 + KD
Q_DN = Q_GU + 2 * KF
Q_PLE0 = Q_DN + 2 * KD
Q_CD = Q_PLE0 + KD
Q_OUT1 = Q_CD + NCD
Q_MOE = Q_OUT1 + KD
PER_E = 2 * KE + KD
Q_PLE1 = Q_MOE + NEXP * PER_E
Q_END = Q_PLE1 + KD


class Signal:

    def __init__(self, sem):
        self.sem, self.count, self.base = sem, 0, 0

    def on(self, ins, by=1):
        ins.then_inc(self.sem, by)
        self.count += by
        return ins

    def add(self, n):
        self.count += n

    def at(self, n):
        return self.base + n


class Serial:

    def __init__(self, engine, signal):
        self.e, self.own = engine, signal

    def __call__(self, ins, signal=None):
        s = signal or self.own
        s.on(ins)
        self.e.wait_ge(s.sem, s.count)
        return ins


def build_program(nc, i, o):
    with ExitStack() as ctx:
        def sb(name, cols):
            return ctx.enter_context(nc.sbuf_tensor(name, [P, cols], F32))

        signals = []

        def signal(name):
            s = Signal(ctx.enter_context(nc.semaphore(name)))
            signals.append(s)
            return s

        def end_of_block():
            for s in signals:
                s.base = s.count

        h_sb, u_sb = sb("resid", KD * T), sb("normed", KD * T)
        h3 = h_sb[:, :].rearrange("p (k t) -> p k t", t=T)
        u3 = u_sb[:, :].rearrange("p (k t) -> p k t", t=T)
        A, B, C = sb("proj", 13796), sb("wide", KF * T), sb("temps", 4 * T + 4 * 548)
        ring = sb("ring", RING * SLAB)
        vec = sb("vecs", NVEC)
        const = sb("consts", 3 * P)
        ident, ones, blk = const[:, 0:P], const[:, P:2 * P], const[:, 2 * P:3 * P]
        Dm = sb("phase", 3500)
        stage = sb("staging", 560)
        small = sb("small", 700)
        ps = [ctx.enter_context(nc.psum_tensor(f"ps{n}", [P, 1024], F32)) for n in range(4)]

        def pt(n, parts=P, p0=0):
            return ps[n % 4][p0:p0 + parts, 512 - HALF:512 + HALF]

        def v(name, k=0, n=1):
            return vec[:, VCOL[name] + k:VCOL[name] + k + n]

        slab_in = [signal(f"slab_in{s}") for s in range(RING)]
        slab_used = signal("slab_used")
        loaded = signal("loaded")
        stored = signal("stored")
        dve_step, act_step, pool_step, pe_step = map(signal, ("dve_step", "act_step", "pool_step", "pe_step"))
        evac = signal("evac")

        def slot(q):
            return ring[:, (q % RING) * SLAB:(q % RING + 1) * SLAB]

        def load_slab(sp, q, src, k=None):
            cols = src.shape[-1]
            if k is None:
                if q >= RING:
                    sp.wait_ge(slab_used.sem, q - RING + 1)
            else:
                turn, per = k
                sp.wait_ge(slab_used.sem, q - RING + 1 + per * turn)
            ins = sp.dma_start(slot(q)[:, 0:cols], src)
            if k is None:
                slab_in[q % RING].on(ins, 16)
            else:
                ins.then_inc(slab_in[q % RING].sem, 16)

        def wait_slab(e, q, k=None):
            n = 16 * (q // RING + 1)
            if k is not None:
                turn, per = k
                n = n + (16 * (per // RING)) * turn
            e.wait_ge(slab_in[q % RING].sem, n)

        def product(pe, dst, slab, kt, rhs, first=True, last=True, width=P, k0=0):
            for k in range(kt):
                for a in (0, HALF):
                    mm = pe.matmul(dst[0:width, a:a + HALF], slab[:, k * width:(k + 1) * width],
                                   rhs(k)[:, a:a + HALF], start=first and k == 0, stop=last and k == kt - 1)
            return mm

        ab_src = lambda m: i["w_in_ab"][m * P:(m + 1) * P, :]
        mixer_small = ["ph_ab"]
        with nc.Block() as block:
            @block.sync
            def _(sp):
                for q in range(RING):
                    load_slab(sp, q, ab_src(q))

            @block.scalar
            def _(act):
                for n in range(2):
                    loaded.on(act.dma_start(h3[:, 4 * n:4 * n + 4, :], i["x"][:, 4 * n:4 * n + 4, :]), 16)
                loaded.on(act.dma_start(const[:, :], i["consts"]), 16)
                loaded.on(act.dma_start(vec[:, :], i["vecs"]), 16)
                loaded.on(act.dma_start(Dm[:, 0:2560], i["ph_ab"]), 16)
                loaded.on(act.dma_start(stage[:, 0:240], i["st_ab"]), 16)
                act.wait_ge(loaded.sem, loaded.count)
        end_of_block()

        sq_done = signal("squares")

        def norm_block(gain, dst3=u3):
            with nc.Block() as block:
                @block.scalar
                def _(act):
                    S = Serial(act, act_step)
                    for k in range(KD):
                        sq_done.on(act.activation(dst3[:, k, :], h3[:, k, :], ACT.Square))
                    act.wait_ge(pe_step.sem, pe_step.at(1))
                    S(act.activation(C[:, 0:T], pt(0), ACT.Sqrt, bias=small[:, 0:1], scale=1.0 / D))

                @block.tensor
                def _(pe):
                    for k in range(KD):
                        pe.wait_ge(sq_done.sem, sq_done.at(k + 1))
                        for a in (0, HALF):
                            mm = pe.matmul(pt(0)[:, a:a + HALF], ones, dst3[:, k, a:a + HALF],
                                           start=k == 0, stop=k == KD - 1)
                    pe_step.on(mm)

                @block.vector
                def _(dve):
                    S = Serial(dve, dve_step)
                    dve.wait_ge(act_step.sem, act_step.at(1))
                    S(dve.reciprocal(C[:, T:2 * T], C[:, 0:T]))
                    for k in range(KD):
                        dve_step.on(dve.scalar_tensor_tensor(
                            out=dst3[:, k, :], in0=h3[:, k, :], scalar=v(gain, k), in1=C[:, T:2 * T],
                            op0=ALU.mult, op1=ALU.mult))
            end_of_block()

        with nc.Block() as block:
            @block.vector
            def _(dve):
                S = Serial(dve, dve_step)
                S(dve.memset(small[:, 0:1], EPS))
                S(dve.memset(small[:, 1:2], GN_EPS))
                S(dve.memset(small[:, 2:3], 1.0))
        end_of_block()

        def softplus_small(dve, act_ready, S, x, e, t0, t1, sign):
            S(dve.tensor_scalar(t0, e, 2.0, None, ALU.add))
            S(dve.reciprocal(t0, t0))
            S(dve.tensor_tensor(e, e, t0, ALU.mult))
            S(dve.tensor_tensor(t0, e, e, ALU.mult))
            S(dve.tensor_scalar(t1, t0, 1.0 / 17, None, ALU.mult))
            for n in (15, 13, 11, 9, 7, 5, 3):
                S(dve.scalar_tensor_tensor(out=t1, in0=t1, scalar=1.0 / n, in1=t0, op0=ALU.add, op1=ALU.mult))
            S(dve.scalar_tensor_tensor(out=t1, in0=t1, scalar=1.0, in1=e, op0=ALU.add, op1=ALU.mult))
            S(dve.tensor_scalar(x, x, sign, 0.0, ALU.mult, ALU.max))
            S(dve.scalar_tensor_tensor(out=x, in0=t1, scalar=2.0, in1=x, op0=ALU.mult, op1=ALU.add))

        norm_block("norm_mix0")

        xa = lambda t: A[:, t * PAD:(t + 1) * PAD]
        ga = lambda t: A[:, 4 * PAD + t * T:4 * PAD + (t + 1) * T]
        X0 = 4 * PAD + 4 * T
        xr = lambda n: A[:, X0 + n * SHW:X0 + (n + 1) * SHW]
        SG0 = X0 + 14 * SHW
        sg = lambda t: A[:, SG0 + t * T:SG0 + (t + 1) * T]
        av = lambda t: A[:, t * PAD:t * PAD + T]
        ha = lambda t: C[:, t * T:(t + 1) * T]
        tm = lambda n: C[:, 4 * T + n * 548:4 * T + (n + 1) * 548]
        tb = lambda n: B[:, 10240 + n * 600:10240 + n * 600 + 544]
        rw4 = B[:, 0:10240].rearrange("p (t c k q) -> p t c k q", t=4, c=8, k=5)
        RB, RK, RR, RKAP, RV = range(5)

        def rw(t, k):
            return rw4[:, t, :, k, :]

        def chunks(ap):
            return ap.rearrange("p (c q) -> p c q", q=64)

        bd_r = lambda t: Dm[:, t * P:(t + 1) * P]
        bd_i = lambda t: Dm[:, 512 + t * P:512 + (t + 1) * P]
        wa2 = Dm[:, 1024:1536]
        g2 = Dm[:, 1536:2048]
        reset64 = Dm[:, 2048:2560]
        st_conv = stage[:, 0:96].rearrange("p (t b k) -> p t b k", t=4, b=NS)
        st_shift = stage[:, 96:208].rearrange("p (t b) -> p t b", t=14)
        st_h0 = stage[:, 208:240].rearrange("p (t b) -> p t b", t=4)
        o_convp = stage[:, 240:252].rearrange("p (t k) -> p t k", t=4)
        o_convs = stage[:, 252:348].rearrange("p (t b k) -> p t b k", t=4, b=NS)
        o_shift = stage[:, 348:474].rearrange("p (t k) -> p t k", t=14)
        o_h = stage[:, 474:510].rearrange("p (t k) -> p t k", t=4)
        ncl, cl, oka = small[:, 4:8], small[:, 8:12], small[:, 12:16]
        sp_t = small[:, 16:32]
        smp = small[:, 32:224].rearrange("p (n t b) -> p n t b", n=6, t=4)
        SD, SKK, SBB, SK, SR, SV = range(6)
        dec = small[:, 224:256].rearrange("p (t c) -> p t c", t=4)

        xc_ready, gates_ready, gates_read = signal("xc_ready"), signal("gates_ready"), signal("gates_read")
        a_ready, m_ready, s_ready, rg_done = map(signal, ("a_ready", "m_ready", "s_ready", "rg_done"))
        x12_ready, wl_ready, wa_ready, wa_read = map(signal, ("x12_ready", "wl_ready", "wa_ready", "wa_read"))
        cs_ready, ex_ready, kk_raw, kk_sq = map(signal, ("cs_ready", "ex_ready", "kk_raw", "kk_sq"))
        kk_sum, kk_max, kk_root, prep_done = map(signal, ("kk_sum", "kk_max", "kk_root", "prep_done"))
        bon_sum, bon_read, gelu_done, setup_done = map(signal, ("bon_sum", "bon_read", "gelu_done", "setup_done"))
        lam_exp = signal("lam_exp")

        with nc.Block() as block:
            @block.sync
            def _(sp):
                for q in range(RING, NAB):
                    load_slab(sp, q, ab_src(q))
                for q in range(RING):
                    load_slab(sp, Q_OUT0 + q, i["w_out_ab"][q * P:(q + 1) * P, :])

            @block.gpsimd
            def _(pool):
                S = Serial(pool, pool_step)
                xa4 = A[:, 0:4 * PAD].rearrange("p (t c) -> p t c", t=4)
                S(pool.memset(xa4[:, :, 0:3], 0.0))
                for t in range(4):
                    S(pool.tensor_copy(xa4[:, t, SAMP:PAD].rearrange("p (b k) -> p b k", k=4)[:, :, 0:3], st_conv[:, t]))
                x14 = A[:, X0:X0 + 14 * SHW].rearrange("p (n c) -> p n c", n=14)
                S(pool.memset(x14[:, :, 0:1], 0.0))
                S(pool.tensor_copy(x14[:, :, 513:513 + 2 * NS:2], st_shift))
                for t in range(4):
                    S(pool.tensor_copy(o_convs[:, t, :, 0:2], st_conv[:, t, :, 1:3]))
                setup_done.on(pool.memset(small[:, 3:4], 0.0))

            @block.tensor
            def _(pe):
                for m in range(NAB):
                    wait_slab(pe, Q_AB + m)
                    if m >= 2:
                        pe.wait_ge(evac.sem, evac.at(m - 1))
                    slab_used.on(product(pe, pt(m % 2), slot(Q_AB + m), KD, lambda k: u3[:, k, :]))
                    if 4 <= m < 8:
                        t = m - 4
                        pe.wait_ge(xc_ready.sem, xc_ready.at(t + 1))
                        if t:
                            pe.wait_ge(gates_read.sem, gates_read.at(t))
                        product(pe, pt(2), bd_r(t), 1, lambda k: xa(t))
                        gates_ready.on(product(pe, pt(3), bd_i(t), 1, lambda k: xa(t)))
                    if 10 <= m < 14:
                        t = m - 10
                        if t:
                            pe.wait_ge(wa_read.sem, wa_read.at(t))
                        else:
                            pe.wait_ge(wl_ready.sem, wl_ready.at(1))
                            pe.wait_ge(gates_read.sem, gates_read.at(4))
                        for n, (p0, dst) in enumerate(((0, pt(2)), (64, pt(3)))):
                            for a in (0, HALF):
                                mm = pe.matmul(dst[:, a:a + HALF], wa2[p0:p0 + 64, t * P:(t + 1) * P],
                                               xr(12)[p0:p0 + 64, a:a + HALF], start=True, stop=True)
                        wa_ready.on(mm)
                    if 14 <= m < 18:
                        t = m - 14
                        pe.wait_ge(kk_sq.sem, kk_sq.at(t + 1))
                        pe.wait_ge(wa_read.sem, wa_read.at(4))
                        if t:
                            pe.wait_ge(kk_max.sem, kk_max.at(t))
                        kk_sum.on(product(pe, pt(2), blk, 1, lambda k: tb(0)))
                    if m >= 18:
                        t = m - 18
                        pe.wait_ge(prep_done.sem, prep_done.at(t + 1))
                        pe.wait_ge(wa_read.sem, wa_read.at(4))
                        if t:
                            pe.wait_ge(bon_read.sem, bon_read.at(t))
                        bon_sum.on(product(pe, pt(3), blk, 1, lambda k: sg(t)))

            @block.scalar
            def _(act):
                S = Serial(act, act_step)
                S(act.activation(sp_t[:, 0:4], v("lam", 0, 4), ACT.Abs))
                S(act.activation(sp_t[:, 4:8], sp_t[:, 0:4], ACT.Exp, scale=-1.0), lam_exp)
                act.wait_ge(setup_done.sem, setup_done.at(1))
                for m in range(NAB):
                    kind, n = AB_TILES[m]
                    act.wait_ge(slab_used.sem, Q_AB + m + 1)
                    src = pt(m % 2)
                    if kind == "xa":
                        act_step.on(act.activation(xa(n)[:, 3:3 + SEQ], src[:, 0:SEQ], ACT.Copy))
                        act_step.on(act.activation(xa(n)[:, SAMP + 3:PAD:4], src[:, SEQ:T], ACT.Copy))
                        act_step.on(act.activation(o_convp[:, n, :], src[:, SEQ - 3:SEQ], ACT.Copy))
                        evac.on(act.activation(o_convs[:, n, :, 2], src[:, SEQ:T], ACT.Copy))
                    elif kind == "x":
                        act_step.on(act.activation(xr(n)[:, 1:1 + SEQ], src[:, 0:SEQ], ACT.Copy))
                        act_step.on(act.activation(xr(n)[:, 514:514 + 2 * NS:2], src[:, SEQ:T], ACT.Copy))
                        evac.on(act.activation(o_shift[:, n, :], src[:, SEQ - 1:T], ACT.Copy))
                    else:
                        evac.on(act.activation(ga(n), src, ACT.Gelu_apprx_tanh))
                    if 5 <= m < 9:
                        t = m - 5
                        act.wait_ge(gates_ready.sem, gates_ready.at(t + 1))
                        if t:
                            act.wait_ge(rg_done.sem, rg_done.at(t))
                        else:
                            act.wait_ge(xc_ready.sem, xc_ready.at(4))
                        S(act.activation(tm(1)[:, 0:T], pt(2), ACT.Sigmoid, bias=v("b_r", t)))
                        S(act.activation(tm(2)[:, 0:T], pt(3), ACT.Sigmoid, bias=v("b_i", t)), gates_read)
                        S(act.activation(tm(3)[:, 0:T], tm(1)[:, 0:T], ACT.Tanh, scale=ncl[:, t:t + 1]))
                        S(act.activation(tm(1)[:, 0:T], tm(1)[:, 0:T], ACT.Exp, scale=cl[:, t:t + 1]), a_ready)
                        act.wait_ge(m_ready.sem, m_ready.at(t + 1))
                        S(act.activation(tm(3)[:, 0:T], tm(0)[:, 0:T], ACT.Sqrt), s_ready)
                    if m == 9:
                        act.wait_ge(x12_ready.sem, x12_ready.at(2))
                        S(act.activation(xr(13)[:, 0:T], xr(13)[:, 0:T], ACT.Sigmoid))
                        S(act.activation(xr(12)[0:64, 0:T], xr(12)[0:64, 0:T], ACT.Tanh), wl_ready)
                    if 10 <= m < 14:
                        t = m - 10
                        act.wait_ge(wa_ready.sem, wa_ready.at(t + 1))
                        S(act.activation(sg(t), pt(2), ACT.Sigmoid, bias=v("w0", t)))
                        S(act.activation(av(t), pt(3), ACT.Sigmoid, bias=v("a0", t)), wa_read)
                    if 14 <= m < 18:
                        t = m - 14
                        act.wait_ge(cs_ready.sem, cs_ready.at(t + 1))
                        S(act.activation(tm(2)[:, 0:SEQ], tm(0)[:, 0:SEQ], ACT.Exp, scale=-C0))
                        S(act.activation(tm(3)[:, 0:SEQ], tm(0)[:, 0:SEQ], ACT.Exp, scale=C0))
                        S(act.activation(tm(1)[:, 0:SEQ], tm(1)[:, 0:SEQ], ACT.Exp, scale=-C0))
                        S(act.activation(smp[:, SD, t, :], sg(t)[:, SEQ:T], ACT.Exp, scale=-C0), ex_ready)
                        act.wait_ge(kk_raw.sem, kk_raw.at(t + 1))
                        S(act.activation(tb(0)[:, 0:T], tb(1)[:, 0:T], ACT.Square), kk_sq)
                        act.wait_ge(kk_max.sem, kk_max.at(t + 1))
                        S(act.activation(tb(0)[:, 0:T], tb(0)[:, 0:T], ACT.Sqrt), kk_root)

            @block.vector
            def _(dve):
                S = Serial(dve, dve_step)
                dve.wait_ge(lam_exp.sem, lam_exp.at(1))
                S(dve.tensor_copy(ncl, v("lam", 0, 4)))
                softplus_small(dve, None, S, ncl, sp_t[:, 4:8], sp_t[:, 8:12], sp_t[:, 12:16], -1.0)
                S(dve.tensor_scalar(cl, ncl, -8.0, None, ALU.mult))
                S(dve.tensor_scalar(ncl, ncl, 8.0, None, ALU.mult))
                S(dve.tensor_scalar(oka, v("k_a", 0, 4), -1.0, 1.0, ALU.mult, ALU.add))
                for t in range(4):
                    w = lambda k: v("lru_w", 4 * k + t)
                    x, y = xa(t), tm(0)
                    dve.wait_ge(evac.sem, evac.at(t + 1))
                    S(dve.tensor_scalar(y[:, 0:544], x[:, 3:547], w(3), v("lru_b", t), ALU.mult, ALU.add))
                    for k in (2, 1):
                        S(dve.scalar_tensor_tensor(out=y[:, 0:544], in0=x[:, k:k + 544], scalar=w(k),
                                                   in1=y[:, 0:544], op0=ALU.mult, op1=ALU.add))
                    S(dve.scalar_tensor_tensor(out=x[:, SEQ:T], in0=x[:, SAMP:PAD:4], scalar=w(0),
                                               in1=y[:, SAMP:544:4], op0=ALU.mult, op1=ALU.add))
                    S(dve.scalar_tensor_tensor(out=x[:, 0:SEQ], in0=x[:, 0:SEQ], scalar=w(0),
                                               in1=y[:, 0:SEQ], op0=ALU.mult, op1=ALU.add), xc_ready)
                for t in range(4):
                    a, gi, th = tm(1)[:, 0:T], tm(2)[:, 0:T], tm(3)[:, 0:T]
                    mm = tm(0)[:, 0:T]
                    dve.wait_ge(a_ready.sem, a_ready.at(t + 1))
                    S(dve.tensor_tensor(mm, a, a, ALU.mult))
                    S(dve.scalar_tensor_tensor(out=mm, in0=mm, scalar=1.0, in1=th, op0=ALU.add, op1=ALU.mult), m_ready)
                    S(dve.tensor_tensor(gi, gi, xa(t)[:, 0:T], ALU.mult))
                    dve.wait_ge(s_ready.sem, s_ready.at(t + 1))
                    S(dve.tensor_tensor(gi, gi, th, ALU.mult))
                    S(dve.tensor_tensor_scan(ha(t)[:, 0:SEQ], a[:, 0:SEQ], gi[:, 0:SEQ], 0.0, ALU.mult, ALU.add))
                    S(dve.tensor_tensor(mm[:, 0:NS], a[:, SEQ:T], st_h0[:, t, :], ALU.mult))
                    S(dve.tensor_tensor(ha(t)[:, SEQ:T], mm[:, 0:NS], gi[:, SEQ:T], ALU.add))
                    S(dve.tensor_copy(o_h[:, t, :], ha(t)[:, SEQ - 1:T]), rg_done)

                def shift(n, s=None):
                    x, d = xr(n), tb(0)
                    dve.wait_ge(evac.sem, evac.at(1 + AB_TILES.index(("x", n))))
                    S(dve.tensor_tensor(d[:, 0:528], x[:, 0:528], x[:, 1:529], ALU.subtract))
                    S(dve.scalar_tensor_tensor(out=x[:, 0:SEQ], in0=d[:, 0:SEQ], scalar=v("mu", n),
                                               in1=x[:, 1:1 + SEQ], op0=ALU.mult, op1=ALU.add))
                    S(dve.scalar_tensor_tensor(out=x[:, SEQ:T], in0=d[:, 513:513 + 2 * NS:2], scalar=v("mu", n),
                                               in1=x[:, 514:514 + 2 * NS:2], op0=ALU.mult, op1=ALU.add), s)

                shift(12, x12_ready)
                shift(13, x12_ready)
                for t in range(4):
                    xk, xv_, kk, e = xr(4 + t), xr(8 + t), tb(1)[:, 0:T], tm
                    dve.wait_ge(wa_read.sem, wa_read.at(t + 1))
                    S(dve.tensor_tensor_scan(tm(0)[:, 0:SEQ], reset64, sg(t)[:, 0:SEQ], 0.0, ALU.mult, ALU.add))
                    S(dve.tensor_tensor(tm(1)[:, 0:SEQ], tm(0)[:, 0:SEQ], sg(t)[:, 0:SEQ], ALU.subtract), cs_ready)
                    shift(4 + t)
                    shift(t)
                    S(dve.tensor_scalar(kk, xk[:, 0:T], v("k_k", t), None, ALU.mult), kk_raw)
                    dve.wait_ge(kk_sum.sem, kk_sum.at(t + 1))
                    S(dve.tensor_scalar(tb(0)[:, 0:T], pt(2), 1e-12, None, ALU.max), kk_max)
                    dve.wait_ge(kk_root.sem, kk_root.at(t + 1))
                    S(dve.reciprocal(tb(0)[:, 0:T], tb(0)[:, 0:T]))
                    S(dve.tensor_tensor(kk, kk, tb(0)[:, 0:T], ALU.mult))
                    S(dve.tensor_scalar(tb(0)[:, 0:T], av(t), v("k_a", t), oka[:, t:t + 1], ALU.mult, ALU.add))
                    S(dve.tensor_tensor(xk[:, 0:T], xk[:, 0:T], tb(0)[:, 0:T], ALU.mult))
                    S(dve.tensor_tensor(av(t), kk, av(t), ALU.mult))
                    S(dve.scalar_tensor_tensor(out=tb(0)[:, 0:T], in0=xr(t)[:, 0:T], scalar=v("r_k", t),
                                               in1=xk[:, 0:T], op0=ALU.mult, op1=ALU.mult))
                    dve.wait_ge(ex_ready.sem, ex_ready.at(t + 1))
                    S(dve.tensor_copy(sg(t), tb(0)[:, 0:T]))
                    S(dve.tensor_tensor(rw(t, RKAP), chunks(kk[:, 0:SEQ]), chunks(tm(1)[:, 0:SEQ]), ALU.mult))
                    S(dve.tensor_tensor(rw(t, RB), chunks(av(t)[:, 0:SEQ]), chunks(tm(3)[:, 0:SEQ]), ALU.mult))
                    S(dve.tensor_tensor(rw(t, RK), chunks(xk[:, 0:SEQ]), chunks(tm(3)[:, 0:SEQ]), ALU.mult))
                    S(dve.tensor_tensor(rw(t, RR), chunks(xr(t)[:, 0:SEQ]), chunks(tm(2)[:, 0:SEQ]), ALU.mult))
                    S(dve.tensor_copy(dec[:, t, :], tm(2)[:, 63:SEQ:64]))
                    S(dve.tensor_copy(smp[:, SKK, t, :], kk[:, SEQ:T]))
                    S(dve.tensor_copy(smp[:, SBB, t, :], av(t)[:, SEQ:T]))
                    S(dve.tensor_copy(smp[:, SK, t, :], xk[:, SEQ:T]))
                    S(dve.tensor_copy(smp[:, SR, t, :], xr(t)[:, SEQ:T]), prep_done)
                for t in range(4):
                    xk, xv_ = xr(4 + t), xr(8 + t)
                    shift(8 + t)
                    S(dve.tensor_copy(rw(t, RV), chunks(xv_[:, 0:SEQ])))
                    S(dve.tensor_copy(smp[:, SV, t, :], xv_[:, SEQ:T]))
                    dve.wait_ge(bon_sum.sem, bon_sum.at(t + 1))
                    S(dve.tensor_tensor(xk[:, 0:T], pt(3), xv_[:, 0:T], ALU.mult), bon_read)
                for t in range(4):
                    dve.wait_ge(evac.sem, evac.at(19 + t))
                    S(dve.tensor_tensor(ga(t), ga(t), ha(t), ALU.mult))
        end_of_block()

        def spread(ap, n, axis):
            shape = list(ap.shape)
            shape.insert(axis, n)
            return ap.unsqueeze(axis).broadcast_to(shape)

        rwmask, level = Dm[:, 0:P], lambda l: Dm[:, P * (1 + l):P * (2 + l)]
        sign, i64 = Dm[:, 7 * P:7 * P + 1], Dm[:, 7 * P + 1:7 * P + 65]
        pairs = lambda ap: ap.rearrange("p (n c) -> p n c", c=P)
        AL, DD, EE, GG = [pairs(u_sb[:, n * 1024:(n + 1) * 1024]) for n in range(4)]
        OO = pairs(C[:, 0:1024])
        AM = C[:, 1024:3072].rearrange("p (c h t q) -> p c h t q", c=2, h=2, t=4)
        BK = C[:, 3072:4096].rearrange("p (h c t q) -> p h c t q", c=2, h=2, t=4)
        PV = B[:, 10240:11264].rearrange("p (h c t q) -> p h c t q", c=2, h=2, t=4)
        Qs = Dm[:, 2560:2816].rearrange("p (t q) -> p t q", t=4)
        Zs = [Dm[:, 2816 + 256 * n:3072 + 256 * n].rearrange("p (t q) -> p t q", t=4) for n in range(2)]
        yr = A[:, X0:X0 + 4 * SHW].rearrange("p (t c) -> p t c", t=4)

        def rk(t, c, k, hh, n=1):
            j = ((t * 8 + c) * 5 + k) * 64
            return B[64 * hh:64 * hh + 64, j:j + 64 * n]

        names = ("ab_mm", "ab_read", "am_mm", "am_read", "bk_mm", "bk_read", "v_mm", "v_read", "d_ready", "e_mm",
                 "e_read", "o_ready", "g_mm", "g_read", "dg_mm", "eg_mm", "de_read", "q_mm", "q_read", "p_mm",
                 "p_read", "z_mm", "y_mm", "y_read", "z_read")
        g = {n: signal("rw_" + n) for n in names}

        def w(e, name, n):
            e.wait_ge(g[name].sem, g[name].at(n))

        with nc.Block() as block:
            @block.sync
            def _(sp):
                loaded.on(sp.dma_start(Dm[:, 0:961], i["ph_rw"]), 16)

            @block.gpsimd
            def _(pool):
                S = Serial(pool, pool_step)
                pool_step.on(pool.memset(B[0:64, 10240:11264], 0.0))
                S(pool.memset(u_sb[:, 0:1024], 0.0))

            @block.tensor
            def _(pe):
                for s in range(4):
                    if s:
                        w(pe, "de_read", 5 * s)
                        w(pe, "z_read", 2 * s)
                        w(pe, "y_read", 2 * s)
                    for cc in range(2):
                        for t in range(4):
                            n = (4 * cc + t) * P
                            for hh in range(2):
                                mm = pe.matmul(ps[0][64 * hh:64 * hh + 64, n + 64 * hh:n + 64 * hh + 64],
                                               rk(t, 2 * s + cc, RKAP, hh), rk(t, 2 * s + cc, RB, hh),
                                               start=True, stop=True)
                    g["ab_mm"].on(mm)
                    for cc in range(2):
                        for t in range(4):
                            for hh in range(2):
                                mm = pe.matmul(ps[1 + cc][:, 512 * hh + t * P:512 * hh + (t + 1) * P],
                                               rk(t, 2 * s + cc, RB, hh, 2), rk(t, 2 * s + cc, RR, hh, 2),
                                               start=True, stop=True)
                        g["am_mm"].on(mm)
                    for cc in range(2):
                        for t in range(4):
                            for hh in range(2):
                                j, n = 64 * hh, 512 * hh + (4 * cc + t) * 64
                                mm = pe.transpose(ps[3][:, n:n + 64], rk(t, 2 * s + cc, RB, hh, 2),
                                                  ident[j:j + 64, j:j + 64])
                    g["bk_mm"].on(mm)
                    w(pe, "ab_read", s + 1)
                    for cc in range(2):
                        for t in range(4):
                            for hh in range(2):
                                j, n = 64 * hh, 512 * hh + (4 * cc + t) * 64
                                mm = pe.transpose(ps[0][:, n:n + 64], rk(t, 2 * s + cc, RKAP, hh, 2),
                                                  ident[j:j + 64, j:j + 64])
                    g["v_mm"].on(mm)
                    w(pe, "d_ready", s + 1)
                    w(pe, "am_read", 2 * s + 2)
                    for n in range(8):
                        mm = pe.transpose(ps[1][:, n * P:(n + 1) * P], DD[:, n, :], ident)
                    g["e_mm"].on(mm)
                    w(pe, "v_read", s + 1)
                    for l in range(5):
                        w(pe, "o_ready", 5 * s + l + 1)
                        if l == 0:
                            w(pe, "e_read", s + 1)
                        else:
                            w(pe, "de_read", 5 * s + l)
                        for n in range(8):
                            mm = pe.matmul(ps[0][:, n * P:(n + 1) * P], OO[:, n, :], EE[:, n, :], start=True, stop=True)
                        g["g_mm"].on(mm)
                        w(pe, "g_read", 5 * s + l + 1)
                        if l < 4:
                            for n in range(8):
                                mm = pe.matmul(ps[1][:, n * P:(n + 1) * P], GG[:, n, :], DD[:, n, :], start=True, stop=True)
                            g["dg_mm"].on(mm)
                        for n in range(8):
                            mm = pe.matmul(ps[2][:, n * P:(n + 1) * P], DD[:, n, :], GG[:, n, :], start=True, stop=True)
                        g["eg_mm"].on(mm)
                    w(pe, "de_read", 5 * s + 5)
                    w(pe, "bk_read", s + 1)
                    for cc in range(2):
                        c = 2 * s + cc
                        z = Zs[(c + 1) % 2]
                        if c:
                            w(pe, "z_read", c)
                        for t in range(4):
                            for hh in range(2):
                                dst = ps[0][64 * hh:64 * hh + 64, 64 * t:64 * t + 64]
                                if c:
                                    pe.matmul(dst, rk(t, c, RKAP, hh), z[64 * hh:64 * hh + 64, t, :], start=True, stop=False)
                                mm = pe.matmul(dst, AM[:, cc, hh, t, 64:P], PV[:, hh, cc, t, :],
                                               start=c == 0, stop=True)
                        g["q_mm"].on(mm)
                        w(pe, "q_read", c + 1)
                        for t in range(4):
                            for hh in range(2):
                                j = 64 * hh
                                mm = pe.matmul(ps[1][0:64, 512 * hh + 64 * t:512 * hh + 64 * t + 64],
                                               EE[j:j + 64, 4 * cc + t, j:j + 64], Qs[j:j + 64, t, :],
                                               start=True, stop=True)
                        g["p_mm"].on(mm)
                        w(pe, "p_read", c + 1)
                        for t in range(4):
                            for hh in range(2):
                                mm = pe.matmul(ps[2][64 * hh:64 * hh + 64, 64 * t:64 * t + 64],
                                               BK[:, hh, cc, t, :], PV[:, hh, cc, t, :], start=True, stop=True)
                        g["z_mm"].on(mm)
                        if c:
                            w(pe, "y_read", c)
                        for t in range(4):
                            for hh in range(2):
                                dst = ps[3][64 * hh:64 * hh + 64, 64 * t:64 * t + 64]
                                if c:
                                    pe.matmul(dst, z[64 * hh:64 * hh + 64, t, :], rk(t, c, RR, hh), start=True, stop=False)
                                mm = pe.matmul(dst, PV[:, hh, cc, t, :], AM[:, cc, hh, t, 0:64],
                                               start=c == 0, stop=True)
                        g["y_mm"].on(mm)

            @block.scalar
            def _(act):
                for s in range(4):
                    w(act, "bk_mm", s + 1)
                    if s == 0:
                        act.wait_ge(loaded.sem, loaded.count)
                    else:
                        w(act, "z_mm", 2 * s)
                    g["bk_read"].on(act.activation(C[:, 3072:4096], ps[3][:, :], ACT.Copy, scale=sign))
                    w(act, "v_mm", s + 1)
                    if s:
                        w(act, "y_mm", 2 * s)
                    g["v_read"].on(act.activation(B[64:P, 10240:11264], ps[0][64:P, :], ACT.Copy))
                    w(act, "e_mm", s + 1)
                    g["e_read"].on(act.activation(u_sb[:, 2048:3072], ps[1][:, :], ACT.Copy))
                    for l in range(5):
                        w(act, "g_mm", 5 * s + l + 1)
                        if l:
                            w(act, "eg_mm", 5 * s + l)
                        g["g_read"].on(act.activation(u_sb[:, 3072:4096], ps[0][:, :], ACT.Copy))
                    for cc in range(2):
                        c = 2 * s + cc
                        w(act, "p_mm", c + 1)
                        for hh in range(2):
                            ins = act.activation(PV[0:64, hh, cc], ps[1][0:64, 512 * hh:512 * hh + 256]
                                                 .rearrange("p (t q) -> p t q", t=4), ACT.Copy)
                            (g["p_read"] if hh else act_step).on(ins)
                        w(act, "y_mm", c + 1)
                        g["y_read"].on(act.activation(yr[:, :, 64 * c:64 * c + 64],
                                                      ps[3][:, 0:256].rearrange("p (t q) -> p t q", t=4), ACT.Copy))

            @block.vector
            def _(dve):
                S = Serial(dve, dve_step)
                dve.wait_ge(loaded.sem, loaded.count)
                dve.wait_ge(pool_step.sem, pool_step.at(2))
                for s in range(4):
                    w(dve, "ab_mm", s + 1)
                    for hh in range(2):
                        j = 64 * hh
                        S(dve.tensor_copy(AL[j:j + 64, :, j:j + 64], pairs(ps[0][j:j + 64, :])[:, :, j:j + 64]),
                          g["ab_read"] if hh else None)
                    S(dve.tensor_tensor(OO, AL, spread(level(0), 8, 1), ALU.mult))
                    S(dve.tensor_tensor(DD, spread(ident, 8, 1), OO, ALU.subtract), g["d_ready"])
                    for cc in range(2):
                        w(dve, "am_mm", 2 * s + cc + 1)
                        if s and cc == 0:
                            w(dve, "y_mm", 2 * s)
                        S(dve.tensor_tensor(pairs(C[:, 1024 * (1 + cc):1024 * (2 + cc)]), pairs(ps[1 + cc][:, :]),
                                            spread(rwmask, 8, 1), ALU.mult), g["am_read"])
                    for l in range(5):
                        if l:
                            w(dve, "g_mm", 5 * s + l)
                        S(dve.tensor_tensor(OO, AL, spread(level(l + 1), 8, 1), ALU.mult), g["o_ready"])
                        if l < 4:
                            w(dve, "eg_mm", 5 * s + l + 1)
                            S(dve.tensor_tensor(DD, DD, pairs(ps[1][:, :]), ALU.subtract))
                        w(dve, "eg_mm", 5 * s + l + 1)
                        S(dve.tensor_tensor(EE, EE, pairs(ps[2][:, :]), ALU.subtract), g["de_read"])
                    for cc in range(2):
                        c = 2 * s + cc
                        z, z1 = Zs[(c + 1) % 2], Zs[c % 2]
                        dc = dec[:, :, c].unsqueeze(2).broadcast_to([P, 4, 64])
                        w(dve, "q_mm", c + 1)
                        S(dve.tensor_copy(Qs, ps[0][:, 0:256].rearrange("p (t q) -> p t q", t=4)), g["q_read"])
                        w(dve, "z_mm", c + 1)
                        if c:
                            w(dve, "y_mm", c)
                        pz = ps[2][:, 0:256].rearrange("p (t q) -> p t q", t=4)
                        if c:
                            S(dve.tensor_tensor(z1, pz, z, ALU.add))
                            S(dve.tensor_tensor(z1, z1, dc, ALU.mult), g["z_read"])
                        else:
                            S(dve.tensor_tensor(z1, pz, dc, ALU.mult), g["z_read"])
        end_of_block()

        S0 = u_sb[:, 0:2048]
        DG = u_sb[:, 2048:4096]
        S1, T1 = B[:, 0:2048], B[:, 2048:4096]
        btk = lambda ap: ap.rearrange("p (n k) -> p n k", k=64)
        row = small[:, 256:288]
        tmpn = small[:, 288:352]

        def per_bt(n):
            return smp[:, n].rearrange("p t b -> p b t").unsqueeze(3).broadcast_to([P, NS, 4, 64])

        b4 = lambda ap: ap.rearrange("p (b t k) -> p b t k", b=NS, t=4)
        dg_ready, bc_mm, bc_read, st_in, norm_a, norm_b = map(signal, (
            "dg_ready", "bc_mm", "bc_read", "st_in", "norm_a", "norm_b"))
        mean_mm, var_mm, g_mm, sq_ready, root_ready, cent, g_read = map(signal, (
            "mean_mm", "var_mm", "g_mm", "sq_ready", "root_ready", "cent", "g_read"))
        ORDER = (SKK, SD, SBB, SK, SR)
        with nc.Block() as block:
            @block.sync
            def _(sp):
                st_in.on(sp.dma_start(S0, i["s_rw"]), 16)
                stored.on(sp.dma_start(o["wkv_p"], Dm[:, 3072:3328]), 16)
                stored.on(sp.dma_start(o["ab_small"], stage[:, 240:510]), 16)
                sp.wait_ge(dve_step.sem, dve_step.at(1))
                stored.on(sp.dma_start(o["wkv_s"], S1), 16)
                sp.wait_ge(stored.sem, stored.count)

            @block.tensor
            def _(pe):
                for n in range(5):
                    pe.wait_ge(dg_ready.sem, dg_ready.at(n + 1))
                    if n:
                        pe.wait_ge(bc_read.sem, bc_read.at(n))
                    for q in range(4):
                        mm = pe.matmul(ps[q // 2][:, 512 * (q % 2):512 * (q % 2) + 512], blk,
                                       DG[:, 512 * q:512 * q + 512], start=True, stop=True)
                    bc_mm.on(mm)
                pe.wait_ge(bc_read.sem, bc_read.at(5))
                for t in range(4):
                    if t == 0:
                        pe.wait_ge(norm_a.sem, norm_a.at(1))
                    else:
                        pe.wait_ge(cent.sem, cent.at(t))
                    mean_mm.on(product(pe, pt(0), blk, 1, lambda k: yr[:, t, 0:T]))
                for t in range(4):
                    pe.wait_ge(sq_ready.sem, sq_ready.at(t + 1))
                    if t:
                        pe.wait_ge(root_ready.sem, root_ready.at(t))
                    var_mm.on(product(pe, pt(1), blk, 1, lambda k: xr(8 + t)[:, 0:T]))
                for t in range(4):
                    if t >= 2:
                        pe.wait_ge(g_read.sem, g_read.at(t - 1))
                    g_mm.on(product(pe, pt(2 + t % 2), g2[:, t * P:(t + 1) * P], 1, lambda k: xr(13)[:, 0:T]))

            @block.scalar
            def _(act):
                for t in range(4):
                    act.wait_ge(cent.sem, cent.at(t + 1))
                    sq_ready.on(act.activation(xr(8 + t)[:, 0:T], yr[:, t, 0:T], ACT.Square))
                for t in range(4):
                    act.wait_ge(var_mm.sem, var_mm.at(t + 1))
                    root_ready.on(act.activation(xr(8 + t)[:, 0:T], pt(1), ACT.Sqrt, bias=small[:, 1:2], scale=1.0 / 64))

            @block.vector
            def _(dve):
                S = Serial(dve, norm_b)

                def diag(n):
                    S(dve.tensor_tensor(b4(DG), i64.unsqueeze(1).unsqueeze(1).broadcast_to([P, NS, 4, 64]),
                                        per_bt(n), ALU.mult), dg_ready)

                def halves():
                    for q in range(2):
                        yield slice(1024 * q, 1024 * q + 1024), ps[q][:, :], slice(16 * q, 16 * q + 16)

                def wait_bc(n):
                    dve.wait_ge(bc_mm.sem, bc_mm.at(n))

                diag(SKK)
                dve.wait_ge(st_in.sem, st_in.count)
                wait_bc(1)
                for c, bc, r in halves():
                    S(dve.tensor_tensor(T1[:, c], S0[:, c], bc, ALU.mult), bc_read if c.start else None)
                S(dve.tensor_reduce(row, btk(T1), AX.X, ALU.add))
                diag(SD)
                wait_bc(2)
                for c, bc, r in halves():
                    S(dve.tensor_tensor(S1[:, c], S0[:, c], bc, ALU.mult), bc_read if c.start else None)
                diag(SBB)
                wait_bc(3)
                for c, bc, r in halves():
                    S(dve.tensor_tensor(btk(T1[:, c]), btk(bc), row[:, r].unsqueeze(2).broadcast_to([P, 16, 64]), ALU.mult),
                      bc_read if c.start else None)
                S(dve.tensor_tensor(S1, S1, T1, ALU.subtract))
                S(dve.tensor_copy(row.rearrange("p (b t) -> p b t", b=NS), smp[:, SV].rearrange("p t b -> p b t")))
                diag(SK)
                wait_bc(4)
                for c, bc, r in halves():
                    S(dve.tensor_tensor(btk(T1[:, c]), btk(bc), row[:, r].unsqueeze(2).broadcast_to([P, 16, 64]), ALU.mult),
                      bc_read if c.start else None)
                S(dve.tensor_tensor(S1, S1, T1, ALU.add), dve_step)
                diag(SR)
                wait_bc(5)
                for c, bc, r in halves():
                    S(dve.tensor_tensor(T1[:, c], S1[:, c], bc, ALU.mult), bc_read if c.start else None)
                S(dve.tensor_reduce(row, btk(T1), AX.X, ALU.add))
                S(dve.tensor_copy(yr[:, :, SEQ:T], row.rearrange("p (b t) -> p t b", b=NS)), norm_a)
                for t in range(4):
                    dve.wait_ge(mean_mm.sem, mean_mm.at(t + 1))
                    S(dve.scalar_tensor_tensor(out=yr[:, t, 0:T], in0=pt(0), scalar=-1.0 / 64, in1=yr[:, t, 0:T],
                                               op0=ALU.mult, op1=ALU.add), cent)
                for t in range(4):
                    y, r = yr[:, t, 0:T], xr(8 + t)[:, 0:T]
                    dve.wait_ge(root_ready.sem, root_ready.at(t + 1))
                    S(dve.reciprocal(r, r))
                    S(dve.tensor_tensor(y, y, r, ALU.mult))
                    S(dve.tensor_scalar(y, y, v("ln_w", t), v("ln_b", t), ALU.mult, ALU.add))
                    S(dve.tensor_tensor(y, y, xr(4 + t)[:, 0:T], ALU.add))
                    dve.wait_ge(g_mm.sem, g_mm.at(t + 1))
                    S(dve.tensor_tensor(y, y, pt(2 + t % 2), ALU.mult), g_read)
        end_of_block()

        silu_done, hid_done = signal("silu_done"), signal("hid_done")
        emb_in = signal("emb_in")
        tmp2 = lambda n: C[:, (n % 2) * T:(n % 2) * T + T]
        hid = lambda k: B[:, k * T:(k + 1) * T]

        def slab_rows(name, n):
            return i[name][bass.ds(n * P, P), :]

        def prefetch(sp, q0, name, count=RING):
            for q in range(count):
                load_slab(sp, q0 + q, slab_rows(name, q))

        def out_block(q0, name, rhs, nxt):
            with nc.Block() as block:
                @block.sync
                def _(sp):
                    for m in range(RING, KD):
                        load_slab(sp, q0 + m, slab_rows(name, m))
                    prefetch(sp, q0 + KD, nxt)

                @block.tensor
                def _(pe):
                    for m in range(KD):
                        wait_slab(pe, q0 + m)
                        if m >= 4:
                            pe.wait_ge(evac.sem, evac.at(m - 3))
                        slab_used.on(product(pe, pt(m), slot(q0 + m), KD, rhs))

                @block.vector
                def _(dve):
                    for m in range(KD):
                        dve.wait_ge(slab_used.sem, q0 + m + 1)
                        evac.on(dve.tensor_tensor(h3[:, m, :], pt(m), h3[:, m, :], ALU.add))
            end_of_block()

        def ffn_block():
            PEEL, PER, TRIPS = 4, 6, 3
            DPEEL, DPER, DTRIPS = 2, 3, 2

            def hidden_tiles(e, body):
                for m in range(PEEL):
                    body(m, None)
                with e.Fori(0, TRIPS) as turn:
                    for j in range(PER):
                        body(PEEL + j, turn)

            def down_tiles(e, body):
                for m in range(DPEEL):
                    body(m, None)
                with e.Fori(0, DTRIPS) as turn:
                    for j in range(DPER):
                        body(DPEEL + j, turn)

            def nth(n, turn, per):
                return n if turn is None else n + per * turn

            with nc.Block() as block:
                @block.sync
                def _(sp):
                    for n in range(RING, 2 * PEEL):
                        load_slab(sp, Q_GU + n, slab_rows("w_gu", n))
                    with sp.Fori(0, TRIPS) as turn:
                        for j in range(2 * PER):
                            n = 2 * PEEL + j
                            load_slab(sp, Q_GU + n, slab_rows("w_gu", n + 2 * PER * turn), (turn, 2 * PER))
                    for n in range(2 * DPEEL):
                        load_slab(sp, Q_DN + n, slab_rows("w_dn", n))
                    with sp.Fori(0, DTRIPS) as turn:
                        for j in range(2 * DPER):
                            n = 2 * DPEEL + j
                            load_slab(sp, Q_DN + n, slab_rows("w_dn", n + 2 * DPER * turn), (turn, 2 * DPER))
                    prefetch(sp, Q_PLE0, "w_ple0")

                @block.tensor
                def _(pe):
                    def hidden(m, turn):
                        k = None if turn is None else (turn, 2 * PER)
                        if m >= 2:
                            pe.wait_ge(hid_done.sem, hid_done.at(nth(m - 1, turn, PER)))
                        for s in range(2):
                            wait_slab(pe, Q_GU + 2 * m + s, k)
                            product(pe, pt(2 * (m % 2) + s), slot(Q_GU + 2 * m + s), KD,
                                    lambda n: u3[:, n, :]).then_inc(slab_used.sem, 1)

                    hidden_tiles(pe, hidden)

                    def down(m, turn):
                        k = None if turn is None else (turn, 2 * DPER)
                        if m < DPEEL:
                            pe.wait_ge(hid_done.sem, hid_done.at(KF))
                        if m >= 2:
                            pe.wait_ge(evac.sem, evac.at(nth(m - 2, turn, DPER)))
                        for s in range(2):
                            wait_slab(pe, Q_DN + 2 * m + s, k)
                            product(pe, pt(m), slot(Q_DN + 2 * m + s), KF // 2, lambda n: hid(s * (KF // 2) + n),
                                    first=s == 0, last=s == 1).then_inc(slab_used.sem, 1)

                    down_tiles(pe, down)

                @block.scalar
                def _(act):
                    def silu(m, turn):
                        act.wait_ge(slab_used.sem, nth(Q_GU + 2 * m + 1, turn, 2 * PER))
                        if m >= 2:
                            act.wait_ge(hid_done.sem, hid_done.at(nth(m - 1, turn, PER)))
                        act.activation(tmp2(m), pt(2 * (m % 2)), ACT.Silu).then_inc(silu_done.sem, 1)

                    hidden_tiles(act, silu)
                    silu_done.add(KF)

                @block.vector
                def _(dve):
                    def gate(m, turn):
                        dve.wait_ge(silu_done.sem, silu_done.at(nth(m + 1, turn, PER)))
                        dve.wait_ge(slab_used.sem, nth(Q_GU + 2 * m + 2, turn, 2 * PER))
                        dst = hid(m) if turn is None else B[:, bass.ds(m * T + (PER * T) * turn, T)]
                        dve.tensor_tensor(dst, tmp2(m), pt(2 * (m % 2) + 1), ALU.mult).then_inc(hid_done.sem, 1)

                    hidden_tiles(dve, gate)
                    hid_done.add(KF)

                    def add(m, turn):
                        dve.wait_ge(slab_used.sem, nth(Q_DN + 2 * m + 2, turn, 2 * DPER))
                        dst = h3[:, m, :] if turn is None else h_sb[:, bass.ds(m * T + (DPER * T) * turn, T)]
                        dve.tensor_tensor(dst, pt(m), dst, ALU.add).then_inc(evac.sem, 1)

                    down_tiles(dve, add)
                    evac.add(KD)
            slab_used.add(2 * KF + 2 * KD)
            for q in range(Q_GU + 2 * PEEL + 2 * PER, Q_DN):
                slab_in[q % RING].add(16)
            for q in range(Q_DN + 2 * DPEEL + 2 * DPER, Q_PLE0):
                slab_in[q % RING].add(16)
            end_of_block()

        def ple_block(q0, layer, nxt):
            emb = A[:, 0:2 * T].rearrange("p (k t) -> p k t", t=T)
            with nc.Block() as block:
                @block.sync
                def _(sp):
                    for m in range(RING, KD):
                        load_slab(sp, q0 + m, slab_rows(f"w_ple{layer}", m))
                    if nxt:
                        prefetch(sp, q0 + KD, nxt)

                @block.gpsimd
                def _(pool):
                    emb_in.on(pool.dma_start(emb, i["p"][layer]), 16)

                @block.tensor
                def _(pe):
                    for m in range(KD):
                        wait_slab(pe, q0 + m)
                        if m >= 2:
                            pe.wait_ge(evac.sem, evac.at(m - 1))
                        product(pe, pt(2 * (m % 2)), slot(q0 + m), KD, lambda k: u3[:, k, :])
                        if m == 0:
                            pe.wait_ge(emb_in.sem, emb_in.at(16))
                        slab_used.on(product(pe, pt(2 * (m % 2) + 1), slot(q0 + m)[:, KD * P:], 2,
                                             lambda k: emb[:, k, :]))

                @block.scalar
                def _(act):
                    for m in range(KD):
                        act.wait_ge(slab_used.sem, q0 + m + 1)
                        if m >= 2:
                            act.wait_ge(evac.sem, evac.at(m - 1))
                        silu_done.on(act.activation(tmp2(m), pt(2 * (m % 2)), ACT.Sigmoid))

                @block.vector
                def _(dve):
                    S = Serial(dve, dve_step)
                    for m in range(KD):
                        dve.wait_ge(silu_done.sem, silu_done.at(m + 1))
                        S(dve.tensor_tensor(tmp2(m), tmp2(m), pt(2 * (m % 2) + 1), ALU.mult))
                        evac.on(dve.tensor_tensor(h3[:, m, :], tmp2(m), h3[:, m, :], ALU.add))
            end_of_block()

        out_block(Q_OUT0, "w_out_ab", lambda k: ga(k) if k < 4 else yr[:, k - 4, 0:T], "w_gu")
        norm_block("norm_ffn0")
        ffn_block()
        norm_block("norm_ple0")
        ple_block(Q_PLE0, 0, "w_in_cd")

        norm_block("norm_mix1")
        G0 = 8 * PAD
        qt = lambda t: A[:, G0 + t * T:G0 + (t + 1) * T]
        kt = lambda t: A[:, G0 + (2 + t) * T:G0 + (3 + t) * T]
        vt = lambda t: A[:, G0 + (4 + t) * T:G0 + (5 + t) * T]
        zt = lambda t: A[:, G0 + (8 + t) * T:G0 + (9 + t) * T]
        gt = lambda t: A[:, G0 + (12 + t) * T:G0 + (13 + t) * T]
        sm = A[:, G0 + 16 * T:G0 + 17 * T]
        KN = lambda t: C[:, t * SEQ:(t + 1) * SEQ]
        tq = lambda n: C[:, 1024 + n * 548:1024 + n * 548 + 548]
        cum, dtr = C[0:8, 3216:3728], C[0:8, 3728:4248]
        col8 = 0
        parts = {}
        for name, width in (("sel8", 1024), ("selp", 512), ("last", P), ("ssdmask", P), ("glamask", P),
                            ("reset128", SEQ), ("reset32", SEQ), ("alpha", 256), ("router", 64), ("reset8", 40)):
            parts[name] = Dm[:, col8:col8 + width]
            col8 += width
        sel8 = lambda n: parts["sel8"][0:8, n * P:(n + 1) * P]
        selp = lambda t: parts["selp"][0:8, t * P:(t + 1) * P]
        s_hist = stage[:, 0:192].rearrange("p (t b k) -> p t b k", t=8, b=NS)
        o2_convp = stage[:, 192:216].rearrange("p (t k) -> p t k", t=8)
        o2_convs = stage[:, 216:408].rearrange("p (t b k) -> p t b k", t=8, b=NS)
        cumT, dtT, cend, ecend, wend = [small[:, 4 + 32 * n:36 + 32 * n] for n in range(5)]
        dts, las = [small[:, 164 + 32 * n:196 + 32 * n].rearrange("p (t b) -> p t b", t=4) for n in range(2)]
        gdec = small[:, 228:260].rearrange("p (t c) -> p t c", t=2)
        gds = small[:, 260:276].rearrange("p (t b) -> p t b", t=2)
        aneg, las8 = small[0:8, 276:277], small[0:8, 277:285]
        sm_mm, conv_done, dt_abs, dt_exp, dt_ready = map(signal, ("sm_mm", "conv_done", "dt_abs", "dt_exp", "dt_ready"))
        al_mm, al_log, al_min, al_read, cs2_ready, ex2_ready, gla_read = map(signal, (
            "al_mm", "al_log", "al_min", "al_read", "cs2_ready", "ex2_ready", "gla_read"))
        X_M = lambda n: 1 + n
        with nc.Block() as block:
            @block.sync
            def _(sp):
                loaded.on(sp.dma_start(Dm[:, 0:col8], i["ph_cd"]), 16)
                loaded.on(sp.dma_start(stage[:, 0:192], i["st_cd"]), 16)
                for m in range(RING, NCD):
                    load_slab(sp, Q_CD + m, slab_rows("w_in_cd", m))
                prefetch(sp, Q_OUT1, "w_out_cd")

            @block.gpsimd
            def _(pool):
                S = Serial(pool, pool_step)
                xa8 = A[:, 0:8 * PAD].rearrange("p (t c) -> p t c", t=8)
                S(pool.memset(xa8[:, :, 0:3], 0.0))
                pool.wait_ge(loaded.sem, loaded.count)
                for t in range(8):
                    S(pool.tensor_copy(xa8[:, t, SAMP:PAD].rearrange("p (b k) -> p b k", k=4)[:, :, 0:3], s_hist[:, t]))
                    S(pool.tensor_copy(o2_convs[:, t, :, 0:2], s_hist[:, t, :, 1:3]))
                setup_done.on(pool.memset(small[:, 3:4], 0.0))

            @block.tensor
            def _(pe):
                for m in range(NCD):
                    wait_slab(pe, Q_CD + m)
                    if m >= 2:
                        pe.wait_ge(evac.sem, evac.at(m - 1))
                    slab_used.on(product(pe, pt(m % 2), slot(Q_CD + m), KD, lambda k: u3[:, k, :],
                                         width=48 if m == 0 else P))
                    if m in (10, 13):
                        t = (m - 10) // 3
                        pe.wait_ge(evac.sem, evac.at(1))
                        if t:
                            pe.wait_ge(al_read.sem, al_read.at(t))
                        for a in (0, HALF):
                            mm = pe.matmul(pt(2)[:, a:a + HALF], parts["alpha"][32:48, t * P:(t + 1) * P],
                                           sm[32:48, a:a + HALF], start=True, stop=True)
                        al_mm.on(mm)

            @block.scalar
            def _(act):
                S = Serial(act, act_step)
                act.wait_ge(setup_done.sem, setup_done.at(1))
                S(act.activation(aneg, v("a_log")[0:8], ACT.Exp))
                for m in range(NCD):
                    act.wait_ge(slab_used.sem, Q_CD + m + 1)
                    src = pt(m % 2)
                    if m == 0:
                        S(act.activation(sm[0:48], src[0:48], ACT.Copy), evac)
                        S(act.activation(dtr, sm[0:8], ACT.Identity, bias=v("dt_bias")[0:8]))
                        S(act.activation(tq(0)[0:8, 0:T], dtr, ACT.Abs))
                        S(act.activation(tq(0)[0:8, 0:T], tq(0)[0:8, 0:T], ACT.Exp, scale=-1.0), dt_exp)
                    elif m < 9:
                        n = m - 1
                        act_step.on(act.activation(xa(n)[:, 3:3 + SEQ], src[:, 0:SEQ], ACT.Copy))
                        act_step.on(act.activation(xa(n)[:, SAMP + 3:PAD:4], src[:, SEQ:T], ACT.Copy))
                        act_step.on(act.activation(o2_convp[:, n, :], src[:, SEQ - 3:SEQ], ACT.Copy))
                        evac.on(act.activation(o2_convs[:, n, :, 2], src[:, SEQ:T], ACT.Copy))
                    elif m < 17:
                        evac.on(act.activation(A[:, G0 + (m - 9) * T:G0 + (m - 8) * T], src, ACT.Copy))
                    else:
                        evac.on(act.activation(A[:, G0 + (m - 9) * T:G0 + (m - 8) * T], src, ACT.Silu))
                    if m in (11, 14):
                        t = (m - 11) // 3
                        if t:
                            act.wait_ge(gla_read.sem, gla_read.at(t))
                        else:
                            act.wait_ge(dt_ready.sem, dt_ready.at(1))
                        act.wait_ge(al_mm.sem, al_mm.at(t + 1))
                        S(act.activation(tq(2)[:, 0:T], pt(2), ACT.Abs, bias=v("alpha_b", t)))
                        S(act.activation(tq(2)[:, 0:T], tq(2)[:, 0:T], ACT.Exp, scale=-1.0))
                        S(act.activation(tq(2)[:, 0:T], tq(2)[:, 0:T], ACT.Ln, bias=small[:, 2:3]), al_log)
                        act.wait_ge(cs2_ready.sem, cs2_ready.at(t + 1))
                        S(act.activation(tq(3)[:, 0:SEQ], tq(1)[:, 0:SEQ], ACT.Exp, scale=1.0 / 16))
                        S(act.activation(tq(1)[:, 0:SEQ], tq(1)[:, 0:SEQ], ACT.Exp, scale=-1.0 / 16))
                        S(act.activation(gds[:, t, :], tq(2)[:, SEQ:T], ACT.Exp, scale=1.0 / 16))
                        S(act.activation(tq(2)[:, 0:SEQ], tq(2)[:, 0:SEQ], ACT.Exp, scale=1.0 / 16), ex2_ready)
                    if 3 <= m < 9 or m == 9 or m == 10:
                        n = m - 3
                        act.wait_ge(conv_done.sem, conv_done.at(n + 1))
                        S(act.activation(xa(n)[:, 0:T], xa(n)[:, 0:T], ACT.Silu))

            @block.vector
            def _(dve):
                S = Serial(dve, dve_step)
                dve.wait_ge(dt_exp.sem, dt_exp.at(1))
                softplus_small(dve, None, S, dtr, tq(0)[0:8, 0:T], tq(1)[0:8, 0:T], tq(2)[0:8, 0:T], 1.0)
                S(dve.tensor_scalar(aneg, aneg, -1.0, None, ALU.mult))
                S(dve.tensor_scalar(tq(0)[0:8, 0:T], dtr, aneg, None, ALU.mult))
                S(dve.tensor_copy(las8, tq(0)[0:8, SEQ:T]))
                S(dve.tensor_tensor_scan(cum, parts["reset128"][0:8, :], tq(0)[0:8, 0:SEQ], 0.0, ALU.mult, ALU.add), dt_ready)

                def conv(n):
                    w = lambda k: v("ssd_w", 8 * k + n)
                    x, y = xa(n), tq(0)
                    dve.wait_ge(evac.sem, evac.at(n + 2))
                    S(dve.tensor_scalar(y[:, 0:544], x[:, 3:547], w(3), v("ssd_b", n), ALU.mult, ALU.add))
                    for k in (2, 1):
                        S(dve.scalar_tensor_tensor(out=y[:, 0:544], in0=x[:, k:k + 544], scalar=w(k),
                                                   in1=y[:, 0:544], op0=ALU.mult, op1=ALU.add))
                    S(dve.scalar_tensor_tensor(out=x[:, SEQ:T], in0=x[:, SAMP:PAD:4], scalar=w(0),
                                               in1=y[:, SAMP:544:4], op0=ALU.mult, op1=ALU.add))
                    S(dve.scalar_tensor_tensor(out=x[:, 0:SEQ], in0=x[:, 0:SEQ], scalar=w(0),
                                               in1=y[:, 0:SEQ], op0=ALU.mult, op1=ALU.add), conv_done)

                def decay(t):
                    la, cs, to_end = tq(2)[:, 0:T], tq(1)[:, 0:SEQ], tq(2)[:, 0:SEQ]
                    dve.wait_ge(al_log.sem, al_log.at(t + 1))
                    S(dve.tensor_scalar(tq(3)[:, 0:T], pt(2), v("alpha_b", t), 0.0, ALU.add, ALU.min), al_read)
                    S(dve.tensor_tensor(la, tq(3)[:, 0:T], la, ALU.subtract))
                    S(dve.tensor_tensor_scan(cs, parts["reset32"], la[:, 0:SEQ], 0.0, ALU.mult, ALU.add))
                    c32 = cs.rearrange("p (c q) -> p c q", q=32)
                    S(dve.tensor_tensor(to_end.rearrange("p (c q) -> p c q", q=32),
                                        c32[:, :, 31:32].broadcast_to([P, 16, 32]), c32, ALU.subtract), cs2_ready)

                def gla_ready(t):
                    dve.wait_ge(ex2_ready.sem, ex2_ready.at(t + 1))
                    dve.wait_ge(evac.sem, evac.at(12 + t))
                    S(dve.tensor_copy(gdec[:, t, :], tq(3)[:, 31:SEQ:32]))
                    S(dve.tensor_tensor(KN(t), kt(t)[:, 0:SEQ], tq(2)[:, 0:SEQ], ALU.mult))
                    S(dve.tensor_tensor(kt(t)[:, 0:SEQ], kt(t)[:, 0:SEQ], tq(1)[:, 0:SEQ], ALU.mult))
                    S(dve.scalar_tensor_tensor(out=qt(t)[:, 0:SEQ], in0=qt(t)[:, 0:SEQ], scalar=0.125,
                                               in1=tq(3)[:, 0:SEQ], op0=ALU.mult, op1=ALU.mult))
                    S(dve.tensor_scalar(qt(t)[:, SEQ:T], qt(t)[:, SEQ:T], 0.125, None, ALU.mult), gla_read)

                for n in range(4):
                    conv(n)
                for n in range(4, 8):
                    conv(n)
                decay(0)
                gla_ready(0)
                decay(1)
                gla_ready(1)
        end_of_block()

        NC = SEQ // P
        BT0, CT0 = 4, 6
        XD = B[:, 0:2048].rearrange("p (c h q) -> p c h q", c=NC, h=8)
        WX = B[:, 2048:4096].rearrange("p (c h q) -> p c h q", c=NC, h=8)
        BTt = B[:, 4096:5120].rearrange("p (g c n) -> p g c n", g=2, c=NC)
        CB = B[:, 5120:6144].rearrange("p (g c n) -> p g c n", g=2, c=NC)
        ST = B[:, 6144:8192].rearrange("p (c h q) -> p c h q", c=NC, h=8)
        EB = lambda n: B[:, 8192 + 512 * (n % 2):8704 + 512 * (n % 2)]
        SG2 = lambda n: B[:, 9216 + 512 * (n % 2):9728 + 512 * (n % 2)]
        CE = lambda n: B[:, 10240 + 512 * (n % 2):10752 + 512 * (n % 2)]
        c4 = lambda ap: ap.rearrange("p (c n) -> p c n", c=NC)
        names = ("x_tr", "xd", "b_tr", "b_cp", "cb_mm", "cb_cp", "t_tr", "t_cp", "end_mm", "end_ex", "wx", "s_mm",
                 "s_up", "bc", "eb", "dif", "seg", "m", "y_mm", "y_cp", "smp_mm", "smp_cp")
        q = {n: signal("ssd_" + n) for n in names}

        def wq(e, name, n):
            e.wait_ge(q[name].sem, q[name].at(n))

        def head_y(pe, n):
            t, hh = n // 2, n % 2
            wq(pe, "m", n + 1)
            wq(pe, "s_up", NC)
            if n >= 4:
                wq(pe, "y_cp", n // 2 - 1)
            bank = 512 * (t % 2)
            for c in range(NC):
                dst = ps[2][64 * hh:64 * hh + 64, bank + c * P:bank + (c + 1) * P]
                mm = pe.matmul(dst, XD[:, c, n, :], SG2(n)[:, c * P:(c + 1) * P], start=True, stop=c == 0)
                if c:
                    mm = pe.matmul(dst, ST[:, c - 1, n, :], CE(n)[:, c * P:(c + 1) * P], start=False, stop=True)
            q["y_mm"].on(mm)

        with nc.Block() as block:
            @block.sync
            def _(sp):
                st_in.on(sp.dma_start(u_sb[:, 0:4096], i["s_ssd"]), 16)

            @block.tensor
            def _(pe):
                for n, src in enumerate((cum, dtr)):
                    for c in range(NC):
                        mm = pe.transpose(ps[3][:, 32 * n + 8 * c:32 * n + 8 * c + 8], src[:, c * P:(c + 1) * P],
                                          ident[0:8, 0:8])
                q["t_tr"].on(mm)
                for c in range(NC):
                    if c >= 2:
                        wq(pe, "xd", c - 1)
                    for t in range(4):
                        mm = pe.transpose(ps[0][:, 512 * (c % 2) + t * P:512 * (c % 2) + (t + 1) * P],
                                          xa(t)[:, c * P:(c + 1) * P], ident)
                    q["x_tr"].on(mm)
                for gq in range(2):
                    for c in range(NC):
                        mm = pe.transpose(ps[1][:, 512 * gq + c * P:512 * gq + (c + 1) * P],
                                          xa(BT0 + gq)[:, c * P:(c + 1) * P], ident)
                q["b_tr"].on(mm)
                for gq in range(2):
                    for c in range(NC):
                        mm = pe.matmul(ps[2][:, 512 * gq + c * P:512 * gq + (c + 1) * P],
                                       xa(BT0 + gq)[:, c * P:(c + 1) * P], xa(CT0 + gq)[:, c * P:(c + 1) * P],
                                       start=True, stop=True)
                q["cb_mm"].on(mm)
                wq(pe, "t_cp", 2)
                q["end_mm"].on(pe.matmul(ps[3][:, 64:96], parts["last"], cumT, start=True, stop=True))
                wq(pe, "end_ex", 2)
                for n, src in enumerate((las8, dtr[:, SEQ:T])):
                    for t in range(4):
                        mm = pe.matmul(ps[3][:, 512 + 32 * n + 8 * t:512 + 32 * n + 8 * t + 8], selp(t), src,
                                       start=True, stop=True)
                q["smp_mm"].on(mm)
                wq(pe, "b_cp", 1)
                for c in range(NC):
                    wq(pe, "wx", c + 2)
                    if c >= 2:
                        wq(pe, "s_up", c - 1)
                    elif c == 0:
                        wq(pe, "xd", NC)
                    for gq in range(2):
                        mm = pe.matmul(ps[0][:, 512 * (c % 2) + 256 * gq:512 * (c % 2) + 256 * gq + 256],
                                       BTt[:, gq, c, :], B[:, 2048 + 512 * c + 256 * gq:2048 + 512 * c + 256 * gq + 256],
                                       start=True, stop=True)
                    q["s_mm"].on(mm)
                wq(pe, "cb_cp", 1)
                wq(pe, "smp_cp", 1)
                for n in range(8):
                    t, hh, gq = n // 2, n % 2, n // 4
                    if n >= 2:
                        wq(pe, "seg", n - 1)
                        wq(pe, "eb", n - 1)
                        wq(pe, "dif", n - 1)
                    q["bc"].on(pe.matmul(ps[1][:, 512 * (n % 2):512 * (n % 2) + 512], sel8(n), cum, start=True, stop=True))
                    if n == 0:
                        continue
                    head_y(pe, n - 1)
                head_y(pe, 7)

            @block.scalar
            def _(act):
                S = Serial(act, act_step)
                wq(act, "t_tr", 1)
                S(act.activation(cumT, ps[3][:, 0:32], ACT.Copy), q["t_cp"])
                S(act.activation(dtT, ps[3][:, 32:64], ACT.Copy), q["t_cp"])
                wq(act, "b_tr", 1)
                S(act.activation(B[:, 4096:5120], ps[1][:, :], ACT.Copy), q["b_cp"])
                wq(act, "cb_mm", 1)
                S(act.activation(B[:, 5120:6144], ps[2][:, :], ACT.Copy), q["cb_cp"])
                wq(act, "end_mm", 1)
                S(act.activation(cend, ps[3][:, 64:96], ACT.Copy), q["end_ex"])
                S(act.activation(ecend, ps[3][:, 64:96], ACT.Exp), q["end_ex"])
                wq(act, "wx", 1)
                S(act.activation(wend, wend, ACT.Exp), q["end_ex"])
                wq(act, "smp_mm", 1)
                S(act.activation(small[:, 196:228], ps[3][:, 512:544], ACT.Exp))
                S(act.activation(small[:, 164:196], ps[3][:, 544:576], ACT.Copy), q["smp_cp"])
                for n in range(8):
                    wq(act, "bc", n + 1)
                    if n >= 2:
                        wq(act, "m", n - 1)
                    q["eb"].on(act.activation(EB(n), ps[1][:, 512 * (n % 2):512 * (n % 2) + 512], ACT.Exp))
                    wq(act, "dif", n + 1)
                    q["seg"].on(act.activation(SG2(n), SG2(n), ACT.Exp))

            @block.vector
            def _(dve):
                S = Serial(dve, dve_step)
                wq(dve, "t_cp", 2)
                for c in range(NC):
                    wq(dve, "x_tr", c + 1)
                    S(dve.tensor_tensor(XD[:, c], ps[0][:, 512 * (c % 2):512 * (c % 2) + 512].rearrange("p (h q) -> p h q", h=8),
                                        dtT[:, 8 * c:8 * c + 8].unsqueeze(2).broadcast_to([P, 8, 64]), ALU.mult), q["xd"])
                wq(dve, "end_ex", 2)
                S(dve.tensor_tensor(wend, cend, cumT, ALU.subtract), q["wx"])
                wq(dve, "end_ex", 3)
                for c in range(NC):
                    S(dve.tensor_tensor(WX[:, c], XD[:, c], wend[:, 8 * c:8 * c + 8].unsqueeze(2).broadcast_to([P, 8, 64]),
                                        ALU.mult), q["wx"] if c < 3 else q["wx"])
                for c in range(NC):
                    wq(dve, "s_mm", c + 1)
                    inc = ps[0][:, 512 * (c % 2):512 * (c % 2) + 512].rearrange("p (h q) -> p h q", h=8)
                    if c:
                        S(dve.tensor_tensor(ST[:, c], ST[:, c - 1], ecend[:, 8 * c:8 * c + 8].unsqueeze(2).broadcast_to([P, 8, 64]), ALU.mult))
                        S(dve.tensor_tensor(ST[:, c], ST[:, c], inc, ALU.add), q["s_up"])
                    else:
                        S(dve.tensor_copy(ST[:, c], inc), q["s_up"])
                for n in range(9):
                    if n < 8:
                        t, gq = n // 2, n // 4
                        bank = ps[1][:, 512 * (n % 2):512 * (n % 2) + 512]
                        wq(dve, "eb", n + 1)
                        if n >= 2:
                            wq(dve, "y_mm", n - 1)
                        for c in range(NC):
                            ins = dve.scalar_tensor_tensor(
                                out=SG2(n)[:, c * P:(c + 1) * P], in0=bank[:, c * P:(c + 1) * P],
                                scalar=cumT[:, 8 * c + n:8 * c + n + 1], in1=parts["ssdmask"], op0=ALU.subtract, op1=ALU.min)
                            S(ins, q["dif"] if c == NC - 1 else None)
                        S(dve.tensor_tensor(CE(n), EB(n), xa(CT0 + gq)[:, 0:SEQ], ALU.mult))
                        wq(dve, "seg", n + 1)
                        S(dve.tensor_tensor(SG2(n), SG2(n), B[:, 5120 + 512 * gq:5632 + 512 * gq], ALU.mult), q["m"])
                    if n >= 2 and n % 2 == 0:
                        t = n // 2 - 1
                        wq(dve, "y_mm", n)
                        S(dve.scalar_tensor_tensor(out=xa(t)[:, 0:SEQ], in0=xa(t)[:, 0:SEQ], scalar=v("ssd_d", t),
                                                   in1=ps[2][:, 512 * (t % 2):512 * (t % 2) + 512],
                                                   op0=ALU.mult, op1=ALU.add), q["y_cp"])
        end_of_block()

        SS = u_sb[:, 0:4096]
        ss_b = SS.rearrange("p (b t n) -> p b t n", b=NS, t=4)
        SDG, ST2 = B[:, 0:2048], B[:, 2048:4096]
        srow = small[:, 300:332].rearrange("p (b t) -> p b t", b=NS)
        dtx = small[:, 332:364].rearrange("p (t b) -> p t b", t=4)
        with nc.Block() as block:
            @block.sync
            def _(sp):
                stored.on(sp.dma_start(o["ssd_p"], B[:, 6144 + 3 * 512:8192]), 16)
                stored.on(sp.dma_start(o["cd_small"], stage[:, 192:408]), 16)
                sp.wait_ge(dve_step.sem, dve_step.at(1))
                stored.on(sp.dma_start(o["ssd_s"], SS), 16)
                sp.wait_ge(stored.sem, stored.count)

            @block.tensor
            def _(pe):
                for n in range(2):
                    pe.wait_ge(dg_ready.sem, dg_ready.at(n + 1))
                    if n:
                        pe.wait_ge(bc_read.sem, bc_read.at(n))
                    for r in range(4):
                        mm = pe.matmul(ps[r // 2][:, 512 * (r % 2):512 * (r % 2) + 512], ones,
                                       SDG[:, 512 * r:512 * r + 512], start=True, stop=True)
                    bc_mm.on(mm)

            @block.vector
            def _(dve):
                S = Serial(dve, norm_b)
                dve.wait_ge(st_in.sem, st_in.count)
                for n, tile0 in enumerate((BT0, CT0)):
                    for gq in range(2):
                        S(dve.tensor_tensor(SDG[:, 1024 * gq:1024 * gq + 1024].rearrange("p (b n) -> p b n", b=NS),
                                            ident.unsqueeze(1).broadcast_to([P, NS, P]),
                                            xa(tile0 + gq)[:, SEQ:T].unsqueeze(2).broadcast_to([P, NS, P]), ALU.mult),
                          dg_ready if gq else None)
                    if n == 0:
                        S(dve.tensor_tensor(dtx, dts, A[:, 0:4 * PAD].rearrange("p (t c) -> p t c", t=4)[:, :, SEQ:T], ALU.mult))
                        for b in range(2):
                            c = slice(4 * b, 4 * b + 4)
                            S(dve.tensor_tensor(SS[:, 2048 * b:2048 * b + 2048].rearrange("p (b t n) -> p b t n", b=4, t=4),
                                                SS[:, 2048 * b:2048 * b + 2048].rearrange("p (b t n) -> p b t n", b=4, t=4),
                                                las[:, :, c].rearrange("p t b -> p b t").unsqueeze(3).broadcast_to([P, 4, 4, P]), ALU.mult))
                    dve.wait_ge(bc_mm.sem, bc_mm.at(n + 1))
                    for t in range(4):
                        bc = ps[t // 2][:, :].rearrange("p (b n) -> p b n", b=NS)
                        tmp = ST2[:, 0:1024].rearrange("p (b n) -> p b n", b=NS)
                        if n == 0:
                            S(dve.tensor_tensor(tmp, bc, dtx[:, t, :].unsqueeze(2).broadcast_to([P, NS, P]), ALU.mult),
                              bc_read if t == 3 else None)
                            S(dve.tensor_tensor(ss_b[:, :, t, :], ss_b[:, :, t, :], tmp, ALU.add), dve_step if t == 3 else None)
                        else:
                            S(dve.tensor_tensor(tmp, bc, ss_b[:, :, t, :], ALU.mult), bc_read if t == 3 else None)
                            S(dve.tensor_reduce(srow[:, :, t], tmp, AX.X, ALU.add))
                for t in range(4):
                    S(dve.scalar_tensor_tensor(out=xa(t)[:, SEQ:T], in0=xa(t)[:, SEQ:T], scalar=v("ssd_d", t),
                                               in1=srow[:, :, t], op0=ALU.mult, op1=ALU.add))
        end_of_block()

        VT = B[:, 0:2048].rearrange("p (c h n) -> p c h n", c=NC, h=4)
        KT = B[:, 2048:3072].rearrange("p (c t n) -> p c t n", c=NC, t=2)
        ATT = lambda h: B[:, 3072 + 512 * h:3584 + 512 * h]
        GS = B[:, 5120:9216].rearrange("p (t s n) -> p t s n", t=2, s=16)
        bank = lambda n: ps[n // 2][:, 512 * (n % 2):512 * (n % 2) + 512]
        ATT_BANK, O_BANK = (6, 7, 4, 5), (0, 1, 2, 3)
        v_tr, v_cp, k_tr, k_cp, att_mm, att_cp, inc_mm, state_up, o_mm = (
            q["x_tr"], q["xd"], q["b_tr"], q["b_cp"], q["cb_mm"], q["cb_cp"], q["s_mm"], q["s_up"], q["y_mm"])
        with nc.Block() as block:
            @block.sync
            def _(sp):
                st_in.on(sp.dma_start(u_sb[:, 0:2048], i["s_gla"]), 16)

            @block.tensor
            def _(pe):
                for c in range(NC):
                    for h in range(4):
                        mm = pe.transpose(bank(c)[:, h * P:(h + 1) * P], vt(h)[:, c * P:(c + 1) * P], ident)
                    v_tr.on(mm)
                for t in range(2):
                    for c in range(NC):
                        mm = pe.transpose(ps[2][:, (2 * c + t) * P:(2 * c + t + 1) * P], KN(t)[:, c * P:(c + 1) * P], ident)
                k_tr.on(mm)
                for h in range(4):
                    t, r = h // 2, slice(64 * (h % 2), 64 * (h % 2) + 64)
                    if h >= 2:
                        pe.wait_ge(k_cp.sem, k_cp.at(1))
                    for c in range(NC):
                        cc = slice(c * P, (c + 1) * P)
                        mm = pe.matmul(bank(ATT_BANK[h])[:, cc], kt(t)[r, cc], qt(t)[r, cc], start=True, stop=True)
                    att_mm.on(mm)
                pe.wait_ge(v_cp.sem, v_cp.at(4))
                for t in range(2):
                    if t:
                        pe.wait_ge(att_cp.sem, att_cp.at(4))
                    for s in range(16):
                        c, r = s // 4, slice(32 * (s % 4), 32 * (s % 4) + 32)
                        for hh in range(2):
                            mm = pe.matmul(bank(4 * t + s % 4)[64 * hh:64 * hh + 64, c * P:(c + 1) * P],
                                           KT[r, c, t, 64 * hh:64 * hh + 64], VT[r, c, 2 * t + hh, :], start=True, stop=True)
                    inc_mm.on(mm)
                for h in range(4):
                    t, r = h // 2, slice(64 * (h % 2), 64 * (h % 2) + 64)
                    pe.wait_ge(state_up.sem, state_up.at(t + 1))
                    for c in range(NC):
                        dst = bank(O_BANK[h])
                        pe.matmul(dst[:, c * P:(c + 1) * P], VT[:, c, h, :], ATT(h)[:, c * P:(c + 1) * P],
                                  start=True, stop=False)
                        for s in range(4 * c, 4 * c + 4):
                            if s:
                                mm = pe.matmul(dst[:, 32 * s:32 * s + 32], GS[r, t, s - 1, :], qt(t)[r, 32 * s:32 * s + 32],
                                               start=False, stop=s % 4 == 3)
                    o_mm.on(mm)

            @block.scalar
            def _(act):
                for c in range(NC):
                    act.wait_ge(v_tr.sem, v_tr.at(c + 1))
                    v_cp.on(act.activation(B[:, 512 * c:512 * c + 512], bank(c), ACT.Copy))
                for h in range(4):
                    act.wait_ge(o_mm.sem, o_mm.at(h + 1))
                    act_step.on(act.activation(vt(h)[:, 0:SEQ], bank(O_BANK[h]), ACT.Copy))

            @block.vector
            def _(dve):
                S = Serial(dve, dve_step)
                dve.wait_ge(k_tr.sem, k_tr.at(1))
                k_cp.on(dve.tensor_copy(B[:, 2048:3072], ps[2][:, :]))
                for h in range(4):
                    dve.wait_ge(att_mm.sem, att_mm.at(h + 1))
                    att_cp.on(dve.tensor_tensor(c4(ATT(h)), c4(bank(ATT_BANK[h])),
                                                parts["glamask"].unsqueeze(1).broadcast_to([P, NC, P]), ALU.mult))
                for t in range(2):
                    for s in range(16):
                        inc = bank(4 * t + s % 4)[:, (s // 4) * P:(s // 4 + 1) * P]
                        if s == 0:
                            dve.wait_ge(inc_mm.sem, inc_mm.at(t + 1))
                        if s == 0:
                            S(dve.tensor_copy(GS[:, t, 0, :], inc))
                        else:
                            S(dve.scalar_tensor_tensor(out=GS[:, t, s, :], in0=GS[:, t, s - 1, :], scalar=gdec[:, t, s:s + 1],
                                                       in1=inc, op0=ALU.mult, op1=ALU.add), state_up if s == 15 else None)
        end_of_block()

        SG = u_sb[:, 0:2048]
        sg4 = SG.rearrange("p (b t n) -> p b t n", b=NS, t=2)
        VD = lambda hh: B[:, 2048 * hh:2048 * hh + 2048]
        KV = u_sb[:, 2048:4096].rearrange("p (b t n) -> p b t n", b=NS, t=2)
        vk = lambda t0, n: A[:, G0 + t0 * T:G0 + (t0 + n) * T].rearrange("p (t c) -> p t c", c=T)
        per_b = lambda ap: ap.rearrange("p t b -> p b t").unsqueeze(3).broadcast_to([P, NS, 2, P])
        with nc.Block() as block:
            @block.sync
            def _(sp):
                for t in range(2):
                    stored.on(sp.dma_start(o["gla_p"][:, t * P:(t + 1) * P], GS[:, t, 15, :]), 16)
                sp.wait_ge(dve_step.sem, dve_step.at(1))
                stored.on(sp.dma_start(o["gla_s"], SG), 16)
                sp.wait_ge(stored.sem, stored.count)

            @block.tensor
            def _(pe):
                for hh in range(2):
                    pe.wait_ge(dg_ready.sem, dg_ready.at(hh + 1))
                    for r in range(4):
                        mm = pe.matmul(bank(r)[64 * hh:64 * hh + 64, :], ones[:, 0:64], VD(hh)[:, 512 * r:512 * r + 512],
                                       start=True, stop=True)
                    bc_mm.on(mm)
                pe.wait_ge(dve_step.sem, dve_step.at(1))
                for hh in range(2):
                    r = slice(64 * hh, 64 * hh + 64)
                    for t in range(2):
                        for b in range(NS):
                            mm = pe.matmul(bank(4 + hh)[:, NS * t + b:NS * t + b + 1], sg4[r, b, t, :],
                                           qt(t)[r, SEQ + b:SEQ + b + 1], start=True, stop=True)
                o_mm.on(mm)

            @block.vector
            def _(dve):
                S = Serial(dve, norm_b)
                for hh in range(2):
                    for t in range(2):
                        S(dve.tensor_tensor(VD(hh).rearrange("p (b t n) -> p b t n", b=NS, t=2)[:, :, t, :],
                                            ident.unsqueeze(1).broadcast_to([P, NS, P]),
                                            vt(2 * t + hh)[:, SEQ:T].unsqueeze(2).broadcast_to([P, NS, P]), ALU.mult),
                          dg_ready if t else None)
                dve.wait_ge(st_in.sem, st_in.count)
                S(dve.tensor_tensor(sg4, sg4, per_b(gds), ALU.mult))
                dve.wait_ge(bc_mm.sem, bc_mm.at(2))
                for n in range(2):
                    bs = slice(4 * n, 4 * n + 4)
                    S(dve.tensor_tensor(KV[:, bs], ps[n][:, :].rearrange("p (b t n) -> p b t n", b=4, t=2),
                                        per_b(vk(2, 2)[:, :, SEQ:T])[:, bs], ALU.mult))
                S(dve.tensor_tensor(sg4, sg4, KV, ALU.add), dve_step)
                dve.wait_ge(o_mm.sem, o_mm.at(1))
                for h in range(4):
                    t, hh = h // 2, h % 2
                    S(dve.tensor_copy(vt(h)[:, SEQ:T], bank(4 + hh)[:, NS * t:NS * t + NS]))
        end_of_block()

        SQ = lambda n: B[:, n * T:n * T + T]
        RT = lambda n: B[:, (8 + n) * T:(9 + n) * T]
        yz, ysq, ysum, yroot = q["bc"], q["eb"], q["dif"], q["seg"]
        with nc.Block() as block:
            @block.tensor
            def _(pe):
                for n in range(8):
                    pe.wait_ge(ysq.sem, ysq.at(n + 1))
                    if n == 7:
                        pe.wait_ge(yroot.sem, yroot.at(1))
                    mm = product(pe, pt(0) if n < 4 else pt(n - 3), ones, 1, lambda k: SQ(n), first=n == 0 or n > 3,
                                 last=n >= 3)
                    if n >= 3:
                        ysum.on(mm)

            @block.scalar
            def _(act):
                for n in range(8):
                    if n < 4:
                        act.wait_ge(yz.sem, yz.at(n + 1))
                    ysq.on(act.activation(SQ(n), xa(n)[:, 0:T] if n < 4 else vt(n - 4), ACT.Square))
                for n in range(5):
                    act.wait_ge(ysum.sem, ysum.at(n + 1))
                    yroot.on(act.activation(RT(n), pt(n), ACT.Sqrt, bias=small[:, 0:1], scale=1.0 / (512 if n == 0 else P)))

            @block.vector
            def _(dve):
                S = Serial(dve, dve_step)
                for t in range(4):
                    yz.on(dve.tensor_tensor(xa(t)[:, 0:T], xa(t)[:, 0:T], zt(t), ALU.mult))
                dve.wait_ge(ysq.sem, ysq.at(4))
                for n in range(5):
                    dve.wait_ge(yroot.sem, yroot.at(n + 1))
                    S(dve.reciprocal(RT(n), RT(n)))
                    if n == 0:
                        for t in range(4):
                            dve_step.on(dve.scalar_tensor_tensor(out=xa(t)[:, 0:T], in0=xa(t)[:, 0:T],
                                                                 scalar=v("ssd_norm", t), in1=RT(0), op0=ALU.mult, op1=ALU.mult))
                    else:
                        if n == 1:
                            dve.wait_ge(ysq.sem, ysq.at(8))
                        o_h = vt(n - 1)
                        S(dve.scalar_tensor_tensor(out=o_h, in0=o_h, scalar=v("gla_norm"), in1=RT(n), op0=ALU.mult, op1=ALU.mult))
                        S(dve.tensor_tensor(o_h, o_h, gt(n - 1), ALU.mult))
        end_of_block()

        out_block(Q_OUT1, "w_out_cd", lambda k: xa(k)[:, 0:T] if k < 4 else vt(k - 4), "w_moe_gu")
        norm_block("norm_ffn1")

        NT = 5
        e3 = lambda n: small[:, 300 + 40 * n:340 + 40 * n]
        r5 = lambda n: small[:, 660 + 5 * n:665 + 5 * n]
        by_e = lambda ap: ap.rearrange("p (t e) -> p t e", e=NEXP)
        logit, prob, first1, first2, rest, scan = [e3(n) for n in range(6)]
        top, tot, top2 = r5(0), r5(1), r5(2)
        row8 = lambda ap: ap.unsqueeze(2).broadcast_to([P, NT, NEXP])
        gates_t = A[0:8, 4160:4160 + T]
        gate_of = lambda e: A[:, e * T:(e + 1) * T]
        rt_mm, rt_exp, rt_sub, rt_gate, rt_tr, rt_cp, rt_bc = (q[n] for n in ("bc", "eb", "dif", "seg", "m", "y_mm", "y_cp"))
        with nc.Block() as block:
            @block.tensor
            def _(pe):
                for tt in range(NT):
                    w = P if tt < 4 else NS
                    for k in range(KD):
                        mm = pe.matmul(ps[0][0:w, 8 * tt:8 * tt + 8], u3[:, k, tt * P:tt * P + w],
                                       parts["router"][:, 8 * k:8 * k + 8], start=k == 0, stop=k == KD - 1)
                rt_mm.on(mm)
                pe.wait_ge(rt_gate.sem, rt_gate.at(1))
                for tt in range(NT):
                    w = P if tt < 4 else NS
                    mm = pe.transpose(ps[1][0:8, tt * P:tt * P + w], prob[0:w, 8 * tt:8 * tt + 8], ident[0:w, 0:w])
                rt_tr.on(mm)
                pe.wait_ge(rt_cp.sem, rt_cp.at(1))
                for e in range(NEXP):
                    if e >= 4:
                        pe.wait_ge(rt_bc.sem, rt_bc.at(e - 3))
                    evac.on(product(pe, pt(e), sel8(e), 1, lambda k: gates_t))

            @block.scalar
            def _(act):
                act.wait_ge(rt_sub.sem, rt_sub.at(1))
                rt_exp.on(act.activation(prob, logit, ACT.Exp))
                for e in range(NEXP):
                    act.wait_ge(evac.sem, evac.at(e + 1))
                    rt_bc.on(act.activation(gate_of(e), pt(e), ACT.Copy))

            @block.vector
            def _(dve):
                S = Serial(dve, dve_step)

                def first_of(dst, src, peak):
                    S(dve.tensor_tensor(by_e(dst), by_e(src), row8(peak), ALU.is_equal))
                    S(dve.tensor_tensor_scan(scan, parts["reset8"], dst, 0.0, ALU.mult, ALU.add))
                    S(dve.scalar_tensor_tensor(out=dst, in0=scan, scalar=1.0, in1=dst, op0=ALU.is_equal, op1=ALU.mult))

                S(dve.memset(logit, 0.0))
                dve.wait_ge(rt_mm.sem, rt_mm.at(1))
                S(dve.tensor_copy(logit[:, 0:32], ps[0][:, 0:32]))
                S(dve.tensor_copy(logit[0:NS, 32:40], ps[0][0:NS, 32:40]))
                S(dve.tensor_reduce(top, by_e(logit), AX.X, ALU.max))
                S(dve.tensor_tensor(by_e(logit), by_e(logit), row8(top), ALU.subtract), rt_sub)
                dve.wait_ge(rt_exp.sem, rt_exp.at(1))
                S(dve.tensor_reduce(tot, by_e(prob), AX.X, ALU.add))
                S(dve.reciprocal(tot, tot))
                S(dve.tensor_tensor(by_e(prob), by_e(prob), row8(tot), ALU.mult))
                S(dve.tensor_reduce(top, by_e(prob), AX.X, ALU.max))
                first_of(first1, prob, top)
                S(dve.scalar_tensor_tensor(out=rest, in0=first1, scalar=-2.0, in1=prob, op0=ALU.mult, op1=ALU.add))
                S(dve.tensor_reduce(top2, by_e(rest), AX.X, ALU.max))
                first_of(first2, rest, top2)
                S(dve.tensor_tensor(tot, top, top2, ALU.add))
                S(dve.reciprocal(tot, tot))
                S(dve.tensor_tensor(first1, first1, first2, ALU.add))
                S(dve.tensor_tensor(prob, prob, first1, ALU.mult))
                S(dve.tensor_tensor(by_e(prob), by_e(prob), row8(tot), ALU.mult), rt_gate)
                dve.wait_ge(rt_tr.sem, rt_tr.at(1))
                S(dve.tensor_copy(gates_t, ps[1][0:8, 0:T]), rt_cp)
        end_of_block()

        def moe_src(n, e):
            if n < 2 * KE:
                return i["w_moe_gu"][bass.ds(n * P + (2 * KE * P) * e, P), :]
            return i["w_moe_dn"][bass.ds((n - 2 * KE) * P + (KD * P) * e, P), :]

        down_pt = lambda m: pt(m + 2)
        with nc.Block() as block:
            @block.sync
            def _(sp):
                with sp.Fori(0, NEXP - 1) as e:
                    for n in range(RING, PER_E):
                        load_slab(sp, Q_MOE + n, moe_src(n, e), (e, PER_E))
                    for n in range(RING):
                        load_slab(sp, Q_MOE + PER_E + n, moe_src(n, e + 1), (e, PER_E))
                for n in range(RING, PER_E):
                    load_slab(sp, Q_MOE + (NEXP - 1) * PER_E + n, moe_src(n, NEXP - 1))
                prefetch(sp, Q_PLE1, "w_ple1")

            @block.tensor
            def _(pe):
                with pe.Fori(0, NEXP) as e:
                    turn = (e, PER_E)
                    for m in range(KE):
                        if m < 2:
                            pe.wait_ge(evac.sem, evac.at(KD * e))
                        else:
                            pe.wait_ge(hid_done.sem, hid_done.at(m - 1) + KE * e)
                        for s in range(2):
                            wait_slab(pe, Q_MOE + 2 * m + s, turn)
                            product(pe, pt(2 * (m % 2) + s), slot(Q_MOE + 2 * m + s), KD,
                                    lambda k: u3[:, k, :]).then_inc(slab_used.sem, 1)
                    for m in range(KD):
                        wait_slab(pe, Q_MOE + 2 * KE + m, turn)
                        if m >= 4:
                            pe.wait_ge(evac.sem, evac.at(m - 3) + KD * e)
                        if m == 0:
                            pe.wait_ge(hid_done.sem, hid_done.at(KE - 1) + KE * e)
                            product(pe, down_pt(m), slot(Q_MOE + 2 * KE + m), KE - 1, hid, last=False)
                            pe.wait_ge(hid_done.sem, hid_done.at(KE) + KE * e)
                            ins = product(pe, down_pt(m), slot(Q_MOE + 2 * KE + m)[:, (KE - 1) * P:], 1,
                                          lambda k: hid(KE - 1), first=False)
                        else:
                            ins = product(pe, down_pt(m), slot(Q_MOE + 2 * KE + m), KE, hid)
                        ins.then_inc(slab_used.sem, 1)

            @block.scalar
            def _(act):
                with act.Fori(0, NEXP) as e:
                    for m in range(KE):
                        act.wait_ge(slab_used.sem, Q_MOE + 2 * m + 1 + PER_E * e)
                        if m != 1:
                            act.wait_ge(hid_done.sem, hid_done.at(max(m - 1, 0)) + KE * e)
                        act.activation(tmp2(m), pt(2 * (m % 2)), ACT.Silu).then_inc(silu_done.sem, 1)

            @block.vector
            def _(dve):
                with dve.Fori(0, NEXP) as e:
                    for m in range(KE):
                        dve.wait_ge(silu_done.sem, silu_done.at(m + 1) + KE * e)
                        dve.tensor_tensor(tmp2(m), tmp2(m), A[:, bass.ds(T * e, T)], ALU.mult).then_inc(dve_step.sem, 1)
                        dve.wait_ge(dve_step.sem, dve_step.at(m + 1) + KE * e)
                        dve.wait_ge(slab_used.sem, Q_MOE + 2 * m + 2 + PER_E * e)
                        dve.tensor_tensor(hid(m), tmp2(m), pt(2 * (m % 2) + 1), ALU.mult).then_inc(hid_done.sem, 1)
                    for m in range(KD):
                        dve.wait_ge(slab_used.sem, Q_MOE + 2 * KE + m + 1 + PER_E * e)
                        if m == 0:
                            dve.wait_ge(evac.sem, evac.at(0) + KD * e)
                        dve.tensor_tensor(h3[:, m, :], down_pt(m), h3[:, m, :], ALU.add).then_inc(evac.sem, 1)
        slab_used.add(NEXP * PER_E)
        for n in range(RING):
            slab_in[n].add(16 * (PER_E // RING) * (NEXP - 1))
        for s, n in ((silu_done, KE), (hid_done, KE), (dve_step, KE), (evac, KD)):
            s.add(n * NEXP)
        end_of_block()

        norm_block("norm_ple1")
        ple_block(Q_PLE1, 1, None)
        norm_block("norm_final")
        with nc.Block() as block:
            @block.sync
            def _(sp):
                for n in range(2):
                    stored.on(sp.dma_start(o["y"][:, 4 * T * n:4 * T * (n + 1)], u_sb[:, 4 * T * n:4 * T * (n + 1)]), 16)
                sp.wait_ge(stored.sem, stored.count)


def slabs(w, tiles=None):
    k, m = w.shape
    return np.ascontiguousarray(w.reshape(k // P, P, m // P, P).transpose(2, 1, 0, 3).reshape(m // P, P, k))


def fm(a):
    return a.reshape(a.shape[0], -1, P).transpose(2, 1, 0)


def col(a):
    return a.reshape(-1, P).T


def shape_constants():
    eye = np.eye(P, dtype=np.float32)
    one = np.ones((P, P), np.float32)
    blk = np.kron(np.eye(2, dtype=np.float32), np.ones((64, 64), np.float32))
    out = {"consts": np.concatenate([eye, one, blk], 1)}
    r64 = np.ones((P, SEQ), np.float32)
    r64[:, ::64] = 0
    out["reset64"] = r64
    s, t = np.meshgrid(np.arange(64), np.arange(64), indexing="ij")
    incl, strict = (s <= t).astype(np.float32), (s < t).astype(np.float32)
    rwmask = np.block([[-incl, 0 * strict], [incl, strict]])
    levels = []
    r = np.arange(P)
    for l in range(6):
        m = 1 << l
        ti, si = r[:, None], r[None, :]
        levels.append(((ti // (2 * m) == si // (2 * m)) & ((ti // m) % 2 == 1) & ((si // m) % 2 == 0)).astype(np.float32))
    sign = np.where(np.arange(P) < 64, -1.0, 1.0).astype(np.float32)[:, None]
    i64 = np.tile(np.eye(64, dtype=np.float32), (2, 1))
    out["ph_rw"] = np.concatenate([rwmask] + levels + [sign, i64], 1)
    sel8 = np.zeros((P, 8, P), np.float32)
    selp = np.zeros((P, 4, P), np.float32)
    for n in range(8):
        sel8[n, n] = 1
        selp[n, n // 2, 64 * (n % 2):64 * (n % 2) + 64] = 1
    last = np.zeros((P, P), np.float32)
    last[P - 1] = 1
    j, t = np.meshgrid(np.arange(P), np.arange(P), indexing="ij")
    ssdmask = np.where(j <= t, 0.0, -1e30)
    glamask = ((j <= t) & (j // 32 == t // 32)).astype(np.float32)
    rs = lambda n, w: np.where(np.arange(w) % n == 0, 0.0, 1.0)[None].repeat(P, 0)
    out["cd"] = (np.concatenate([sel8.reshape(P, -1), selp.reshape(P, -1), last, ssdmask, glamask,
                                 rs(128, SEQ), rs(32, SEQ)], 1), rs(8, 40))
    return {k: np.ascontiguousarray(a, np.float32) if k != "cd" else [y.astype(np.float32) for y in a] for k, a in out.items()}


def pack(x):
    c = shape_constants()
    a = {}
    a["x"] = fm(np.concatenate([x["x_prompt"][0], x["x_sample"][:, 0]], 0))
    z = lambda n: np.zeros(n, np.float32)
    pad1 = lambda y: np.concatenate([y.reshape(-1), z(P - y.size)])[:, None]
    vecs = {
        "norm_mix0": col(x["norm_mix"][0]), "norm_mix1": col(x["norm_mix"][1]),
        "norm_ffn0": col(x["norm_ffn"][0]), "norm_ffn1": col(x["norm_ffn"][1]),
        "norm_ple0": col(x["norm_ple"][0]), "norm_ple1": col(x["norm_ple"][1]), "norm_final": col(x["norm_final"]),
        "lru_w": col(x["lru_conv_w"][0]), "lru_b": col(x["lru_conv_b"][0]), "b_r": col(x["lru_b_r"][0]),
        "b_i": col(x["lru_b_i"][0]), "lam": col(x["lru_lambda"][0]), "mu": col(x["rwkv_mu"][0]),
        "w0": col(x["rwkv_w0"][0]), "a0": col(x["rwkv_a0"][0]), "k_k": col(x["rwkv_k_k"][0]),
        "k_a": col(x["rwkv_k_a"][0]), "r_k": col(x["rwkv_r_k"][0]), "ln_w": col(x["rwkv_ln_w"][0]),
        "ln_b": col(x["rwkv_ln_b"][0]), "ssd_w": col(x["ssd_conv_w"][0]), "ssd_b": col(x["ssd_conv_b"][0]),
        "ssd_norm": col(x["ssd_norm_w"][0]), "ssd_d": col(np.repeat(x["ssd_d"][0], 64)),
        "alpha_b": col(x["gla_alpha_b"][0]), "gla_norm": col(x["gla_norm_w"][0]),
        "dt_bias": pad1(x["ssd_dt_bias"][0]), "a_log": pad1(x["ssd_a_log"][0]),
    }
    a["vecs"] = np.concatenate([vecs[n] for n, _ in VECS], 1)
    a["consts"] = c["consts"]

    bd = np.zeros((2, P, 4, P), np.float32)
    for n, w in enumerate((x["lru_w_r"][0], x["lru_w_i"][0])):
        for t in range(4):
            bd[n, 0:64, t, 0:64] = w[2 * t]
            bd[n, 64:, t, 64:] = w[2 * t + 1]
    a["ph_ab"] = np.concatenate([bd[0].reshape(P, 512), bd[1].reshape(P, 512),
                                 np.concatenate([x["rwkv_w2"][0], x["rwkv_a2"][0]], 0), x["rwkv_g2"][0],
                                 c["reset64"]], 1)
    hist = x["state_lru_conv"][0].reshape(NS, 3, 4, P).transpose(3, 2, 0, 1)
    shift = x["state_rwkv_shift"][0].reshape(NS, 14, P).transpose(2, 1, 0)
    h0 = x["state_lru_h"][0].reshape(NS, 4, P).transpose(2, 1, 0)
    a["st_ab"] = np.concatenate([hist.reshape(P, 96), shift.reshape(P, 112), h0.reshape(P, 32)], 1)
    w = x["w_in_ab"][0]
    order = [n if k == "xa" else 4 + n if k == "ga" else 8 + n for k, n in AB_TILES]
    a["w_in_ab"] = slabs(w)[order]
    a["w_out_ab"] = slabs(x["w_out_ab"][0])
    a["ph_rw"] = c["ph_rw"]
    a["s_rw"] = x["state_rwkv_wkv"][0].reshape(NS, 4, 2 * 64, 64).transpose(2, 0, 1, 3).reshape(P, 2048)
    flat = lambda y: y.reshape(-1, y.shape[-1])
    for n in ("w_in_ab", "w_out_ab"):
        a[n] = flat(a[n])
    g, u = slabs(x["ffn_w_gate"][0]), slabs(x["ffn_w_up"][0])
    a["w_gu"] = flat(np.stack([g, u], 1))
    a["w_dn"] = slabs(x["ffn_w_down"][0]).reshape(KD * P, 2, SLAB).reshape(KD, P, 2, SLAB).transpose(0, 2, 1, 3).reshape(-1, SLAB)
    for l in range(2):
        a[f"w_ple{l}"] = flat(np.concatenate([slabs(x["w_ple_gate"][l]), slabs(x["w_ple_proj"][l])], 2))
    a["p"] = np.stack([fm(np.concatenate([x["p_prompt"][l, 0], x["p_sample"][l, :, 0]], 0)) for l in range(2)])
    w = x["w_in_cd"][0]
    z_, xbc, dt, q, k, v_, g, al = np.split(w, np.cumsum([512, 1024, 8, 256, 256, 512, 512]), 1)
    tail = np.concatenate([dt, np.zeros((D, 24), np.float32), al], 1)
    body = slabs(np.concatenate([xbc, q, k, v_, z_, g], 1))
    tail = tail.reshape(KD, P, 48).transpose(1, 0, 2).reshape(1, P, KD * 48)
    a["w_in_cd"] = flat(np.concatenate([np.concatenate([tail, np.zeros((1, P, D - KD * 48), np.float32)], 2), body], 0))
    alpha = np.zeros((P, 256), np.float32)
    alpha[32:48] = x["gla_alpha_up"][0]
    router = x["moe_router"][0].reshape(KD, P, NEXP).transpose(1, 0, 2).reshape(P, -1)
    a["ph_cd"] = np.concatenate([c["cd"][0], alpha, router, c["cd"][1]], 1)
    a["st_cd"] = x["state_ssd_conv"][0].reshape(NS, 3, 8, P).transpose(3, 2, 0, 1).reshape(P, -1)
    a["s_ssd"] = x["state_ssd"][0].reshape(NS, 4, P, P).transpose(2, 0, 1, 3).reshape(P, -1)
    a["s_gla"] = x["state_gla"][0].reshape(NS, 2, P, P).transpose(2, 0, 1, 3).reshape(P, -1)
    a["w_out_cd"] = flat(slabs(x["w_out_cd"][0]))
    g, u = [x[n][0].reshape(NEXP, KD, P, KE, P).transpose(0, 3, 2, 1, 4).reshape(NEXP, KE, P, D)
            for n in ("moe_w_gate", "moe_w_up")]
    a["w_moe_gu"] = np.stack([g, u], 2).reshape(-1, D)
    a["w_moe_dn"] = x["moe_w_down"][0].reshape(NEXP, KE, P, KD, P).transpose(0, 3, 2, 1, 4).reshape(-1, FFE)
    return {k: np.ascontiguousarray(y) for k, y in a.items()}


def unpack(r):
    tok = lambda a, f: a.reshape(P, f, -1).transpose(2, 1, 0).reshape(a.size // (P * f), f * P)
    y = tok(r["y"], KD)
    small = r["ab_small"]
    conv_p, conv_s = small[:, 0:12].reshape(P, 4, 3), small[:, 12:108].reshape(P, 4, NS, 3)
    shift, lru_h = tok(small[:, 108:234], 14), tok(small[:, 234:270], 4)
    wkv_p = r["wkv_p"].reshape(2, 64, 4, 64).transpose(2, 0, 3, 1).reshape(8, 64, 64)
    wkv_s = r["wkv_s"].reshape(2, 64, NS, 4, 64).transpose(2, 3, 0, 1, 4).reshape(NS, 8, 64, 64)
    c2 = r["cd_small"]
    conv2_p, conv2_s = c2[:, 0:24].reshape(P, 8, 3), c2[:, 24:216].reshape(P, 8, NS, 3)
    ssd_p = r["ssd_p"].reshape(P, 8, 64).transpose(1, 2, 0)
    ssd_s = r["ssd_s"].reshape(P, NS, 4, P).transpose(1, 2, 0, 3).reshape(NS, 8, 64, P)
    gla_p = r["gla_p"].reshape(2, 64, 2, P).transpose(2, 0, 1, 3).reshape(4, 64, P)
    gla_s = r["gla_s"].reshape(2, 64, NS, 2, P).transpose(2, 3, 0, 1, 4).reshape(NS, 4, 64, P)
    hist_p = lambda c: c.transpose(2, 1, 0).reshape(3, -1)
    hist_s = lambda c: c.transpose(2, 3, 1, 0).reshape(NS, 3, -1)
    outs = (y[:SEQ][None], y[SEQ:][:, None],
            hist_p(conv_p)[None, None], lru_h[0:1][None], shift[0:1][None], wkv_p[None, None],
            hist_p(conv2_p)[None, None], ssd_p[None, None], gla_p[None, None],
            hist_s(conv_s)[None], lru_h[1:][None], shift[1:][None], wkv_s[None],
            hist_s(conv2_s)[None], ssd_s[None], gla_s[None])
    return tuple(np.ascontiguousarray(a) for a in outs)


OUTPUTS = {"wkv_p": 256, "wkv_s": 2048, "ab_small": 270, "ssd_p": 512, "cd_small": 216, "ssd_s": 4096,
           "gla_p": 256, "gla_s": 2048, "y": KD * T}


def kernel(**inputs):
    import concourse.bacc as _bacc
    from concourse.bass_utils import run_bass_kernel_spmd as _run

    arrays = pack({k: np.asarray(a) for k, a in inputs.items()})
    nc = _bacc.Bacc("TRN2", target_bir_lowering=False, num_devices=1)
    i = {k: nc.dram_tensor("in_" + k, a.shape, F32, kind="ExternalInput").ap() for k, a in arrays.items()}
    o = {k: nc.dram_tensor("out_" + k, [P, c], F32, kind="ExternalOutput").ap() for k, c in OUTPUTS.items()}
    build_program(nc, i, o)
    r = _run(nc, [{"in_" + k: a for k, a in arrays.items()}], core_ids=[0])
    return unpack({k: r.results[0]["out_" + k] for k in OUTPUTS})
```

```python
from contextlib import ExitStack

import numpy as np
import concourse.bass as bass
from concourse import mybir

F32 = mybir.dt.float32
ALU = mybir.AluOpType
ACT = mybir.ActivationFunctionType
AX = mybir.AxisListType

P = 128
SEQ = 512
NS = 8
T = SEQ + NS
HALF = T // 2
D = 1024
KD = D // P
EPS = 1e-6
GN_EPS = 64e-5
FF, FFE, NEXP = 2816, 1408, 8
KF, KE = FF // P, FFE // P
PAD = 547
SAMP = 3 + SEQ
SHW = 532
C0 = float(np.exp(-0.5))

RING = 6
SLAB = 1408

VECS = [("norm_mix0", 8), ("norm_ffn0", 8), ("norm_ple0", 8), ("norm_mix1", 8), ("norm_ffn1", 8),
        ("norm_ple1", 8), ("norm_final", 8), ("lru_w", 16), ("lru_b", 4), ("b_r", 4), ("b_i", 4), ("lam", 4),
        ("mu", 14), ("w0", 4), ("a0", 4), ("k_k", 4), ("k_a", 4), ("r_k", 4), ("ln_w", 4), ("ln_b", 4),
        ("ssd_w", 32), ("ssd_b", 8), ("ssd_norm", 4), ("ssd_d", 4), ("alpha_b", 2), ("gla_norm", 1),
        ("dt_bias", 1), ("a_log", 1)]
VCOL, NVEC = {}, 0
for _n, _w in VECS:
    VCOL[_n] = NVEC
    NVEC += _w

AB_TILES = [("xa", i) for i in range(4)] + [("x", 12), ("x", 13)] + [("x", i) for i in (4, 5, 6, 7)] \
    + [("x", i) for i in (0, 1, 2, 3)] + [("x", i) for i in (8, 9, 10, 11)] + [("ga", i) for i in range(4)]
NAB = len(AB_TILES)
NCD = 25
Q_AB = 0
Q_OUT0 = Q_AB + NAB
Q_GU = Q_OUT0 + KD
Q_DN = Q_GU + 2 * KF
Q_PLE0 = Q_DN + 2 * KD
Q_CD = Q_PLE0 + KD
Q_OUT1 = Q_CD + NCD
Q_MOE = Q_OUT1 + KD
PER_E = 2 * KE + KD
MAXB = (2 * T - NEXP) // P + NEXP
Q_PLE1 = Q_MOE + MAXB * PER_E
Q_END = Q_PLE1 + KD


class Signal:

    def __init__(self, sem):
        self.sem, self.count, self.base = sem, 0, 0

    def on(self, ins, by=1):
        ins.then_inc(self.sem, by)
        self.count += by
        return ins

    def add(self, n):
        self.count += n

    def at(self, n):
        return self.base + n


class Serial:

    def __init__(self, engine, signal):
        self.e, self.own = engine, signal

    def __call__(self, ins, signal=None):
        s = signal or self.own
        s.on(ins)
        self.e.wait_ge(s.sem, s.count)
        return ins


def build_program(nc, i, o):
    with ExitStack() as ctx:
        def sb(name, cols):
            return ctx.enter_context(nc.sbuf_tensor(name, [P, cols], F32))

        signals = []

        def signal(name):
            s = Signal(ctx.enter_context(nc.semaphore(name)))
            signals.append(s)
            return s

        def end_of_block():
            for s in signals:
                s.base = s.count

        h_sb, u_sb = sb("resid", KD * T), sb("normed", KD * T)
        h3 = h_sb[:, :].rearrange("p (k t) -> p k t", t=T)
        u3 = u_sb[:, :].rearrange("p (k t) -> p k t", t=T)
        A, B, C = sb("proj", 13796), sb("wide", KF * T), sb("temps", 4 * T + 4 * 548)
        ring = sb("ring", RING * SLAB)
        vec = sb("vecs", NVEC)
        const = sb("consts", 3 * P)
        ident, ones, blk = const[:, 0:P], const[:, P:2 * P], const[:, 2 * P:3 * P]
        Dm = sb("phase", 3500)
        stage = sb("staging", 560)
        small = sb("small", 700)
        expert_of = ctx.enter_context(nc.sbuf_tensor("expert_of", [P, MAXB + 1], mybir.dt.int32))
        ps = [ctx.enter_context(nc.psum_tensor(f"ps{n}", [P, 1024], F32)) for n in range(4)]

        def pt(n, parts=P, p0=0):
            return ps[n % 4][p0:p0 + parts, 512 - HALF:512 + HALF]

        def v(name, k=0, n=1):
            return vec[:, VCOL[name] + k:VCOL[name] + k + n]

        slab_in = [signal(f"slab_in{s}") for s in range(RING)]
        slab_used = signal("slab_used")
        loaded = signal("loaded")
        resid_in = signal("resid_in")
        stored = signal("stored")
        dve_step, act_step, pool_step, pe_step = map(signal, ("dve_step", "act_step", "pool_step", "pe_step"))
        evac = signal("evac")

        def slot(q):
            return ring[:, (q % RING) * SLAB:(q % RING + 1) * SLAB]

        def load_slab(sp, q, src, k=None):
            cols = src.shape[-1]
            if k is None:
                if q >= RING:
                    sp.wait_ge(slab_used.sem, q - RING + 1)
            else:
                turn, per = k
                sp.wait_ge(slab_used.sem, q - RING + 1 + per * turn)
            ins = sp.dma_start(slot(q)[:, 0:cols], src)
            if k is None:
                slab_in[q % RING].on(ins, 16)
            else:
                ins.then_inc(slab_in[q % RING].sem, 16)

        def wait_slab(e, q, k=None):
            n = 16 * (q // RING + 1)
            if k is not None:
                turn, per = k
                n = n + (16 * (per // RING)) * turn
            e.wait_ge(slab_in[q % RING].sem, n)

        def product(pe, dst, slab, kt, rhs, first=True, last=True, width=P, k0=0):
            for k in range(kt):
                x = rhs(k)
                for a in (0, HALF):
                    mm = pe.matmul(dst[0:width, a:a + HALF], slab[:, k * width:(k + 1) * width],
                                   x[:, a:a + HALF], start=first and k == 0, stop=last and k == kt - 1)
            return mm

        ab_src = lambda m: i["w_in_ab"][m * P:(m + 1) * P, :]
        mixer_small = ["ph_ab"]
        with nc.Block() as block:
            @block.sync
            def _(sp):
                for n in range(2):
                    resid_in.on(sp.dma_start(h3[:, 4 * n:4 * n + 4, :], i["x"][:, 4 * n:4 * n + 4, :]), 16)
                sp.wait_ge(resid_in.sem, resid_in.count)
                for q in range(RING):
                    load_slab(sp, q, ab_src(q))

            @block.scalar
            def _(act):
                loaded.on(act.dma_start(const[:, :], i["consts"]), 16)
                loaded.on(act.dma_start(vec[:, :], i["vecs"]), 16)
                loaded.on(act.dma_start(Dm[:, 0:2560], i["ph_ab"]), 16)
                loaded.on(act.dma_start(stage[:, 0:240], i["st_ab"]), 16)
                act.wait_ge(loaded.sem, loaded.count)
                act.wait_ge(resid_in.sem, resid_in.count)
        end_of_block()

        sq_done, sq_added, norm_sum, norm_root, u_ready = map(signal, (
            "squares", "sq_added", "norm_sum", "norm_root", "u_ready"))
        sq_tmp = lambda m: C[:, (2 + m % 3) * T:(3 + m % 3) * T]
        SQ_SUM, ROOT, RINV = [C[:, (5 + n) * T:(6 + n) * T] for n in range(3)]

        def square(act, m, src=None, more=0, in_loop=False):
            if m >= 4 or in_loop:
                act.wait_ge(sq_added.sem, sq_added.at(m - 3) + more)
            act.activation(SQ_SUM if m == 0 else sq_tmp(m), h3[:, m, :] if src is None else src,
                           ACT.Square).then_inc(sq_done.sem, 1)

        def add_square(dve, m, more=0, in_loop=False):
            if m >= 2 or in_loop:
                dve.wait_ge(sq_added.sem, sq_added.at(m - 1) + more)
            dve.wait_ge(sq_done.sem, sq_done.at(m + 1) + more)
            dve.tensor_tensor(SQ_SUM, SQ_SUM, sq_tmp(m), ALU.add).then_inc(sq_added.sem, 1)

        def squares_counted():
            sq_done.add(KD)
            sq_added.add(KD - 1)

        def norm_pe(pe):
            norm_sum.on(product(pe, pt(0), ones, 1, lambda k: SQ_SUM))

        def norm_act(act):
            act.wait_ge(norm_sum.sem, norm_sum.at(1))
            norm_root.on(act.activation(ROOT, pt(0), ACT.Sqrt, bias=small[:, 0:1], scale=1.0 / D))

        def norm_dve(dve, gain):
            dve.wait_ge(norm_root.sem, norm_root.at(1))
            dve_step.on(dve.reciprocal(RINV, ROOT))
            dve.wait_ge(dve_step.sem, dve_step.count)
            for k in range(KD):
                u_ready.on(dve.scalar_tensor_tensor(out=u3[:, k, :], in0=h3[:, k, :], scalar=v(gain, k), in1=RINV,
                                                    op0=ALU.mult, op1=ALU.mult))

        def normed(pe):
            def tile(k):
                pe.wait_ge(u_ready.sem, u_ready.at(k + 1))
                return u3[:, k, :]
            return tile

        def square_block():
            with nc.Block() as block:
                @block.scalar
                def _(act):
                    for m in range(KD):
                        square(act, m)

                @block.vector
                def _(dve):
                    for m in range(1, KD):
                        add_square(dve, m)
            squares_counted()
            end_of_block()

        with nc.Block() as block:
            @block.vector
            def _(dve):
                S = Serial(dve, dve_step)
                S(dve.memset(small[:, 0:1], EPS))
                S(dve.memset(small[:, 1:2], GN_EPS))
                S(dve.memset(small[:, 2:3], 1.0))
        end_of_block()

        def softplus_small(dve, act_ready, S, x, e, t0, t1, sign):
            S(dve.tensor_scalar(t0, e, 2.0, None, ALU.add))
            S(dve.reciprocal(t0, t0))
            S(dve.tensor_tensor(e, e, t0, ALU.mult))
            S(dve.tensor_tensor(t0, e, e, ALU.mult))
            S(dve.tensor_scalar(t1, t0, 1.0 / 17, None, ALU.mult))
            for n in (15, 13, 11, 9, 7, 5, 3):
                S(dve.scalar_tensor_tensor(out=t1, in0=t1, scalar=1.0 / n, in1=t0, op0=ALU.add, op1=ALU.mult))
            S(dve.scalar_tensor_tensor(out=t1, in0=t1, scalar=1.0, in1=e, op0=ALU.add, op1=ALU.mult))
            S(dve.tensor_scalar(x, x, sign, 0.0, ALU.mult, ALU.max))
            S(dve.scalar_tensor_tensor(out=x, in0=t1, scalar=2.0, in1=x, op0=ALU.mult, op1=ALU.add))

        square_block()

        xa = lambda t: A[:, t * PAD:(t + 1) * PAD]
        ga = lambda t: A[:, 4 * PAD + t * T:4 * PAD + (t + 1) * T]
        X0 = 4 * PAD + 4 * T
        xr = lambda n: A[:, X0 + n * SHW:X0 + (n + 1) * SHW]
        SG0 = X0 + 14 * SHW
        sg = lambda t: A[:, SG0 + t * T:SG0 + (t + 1) * T]
        av = lambda t: A[:, t * PAD:t * PAD + T]
        ha = lambda t: C[:, t * T:(t + 1) * T]
        tm = lambda n: C[:, 4 * T + n * 548:4 * T + (n + 1) * 548]
        tb = lambda n: B[:, 10240 + n * 600:10240 + n * 600 + 544]
        rw4 = B[:, 0:10240].rearrange("p (t c k q) -> p t c k q", t=4, c=8, k=5)
        RB, RK, RR, RKAP, RV = range(5)

        def rw(t, k):
            return rw4[:, t, :, k, :]

        def chunks(ap):
            return ap.rearrange("p (c q) -> p c q", q=64)

        bd_r = lambda t: Dm[:, t * P:(t + 1) * P]
        bd_i = lambda t: Dm[:, 512 + t * P:512 + (t + 1) * P]
        wa2 = Dm[:, 1024:1536]
        g2 = Dm[:, 1536:2048]
        reset64 = Dm[:, 2048:2560]
        td = Dm[:, 2560:3104]
        st_conv = stage[:, 0:96].rearrange("p (t b k) -> p t b k", t=4, b=NS)
        st_shift = stage[:, 96:208].rearrange("p (t b) -> p t b", t=14)
        st_h0 = stage[:, 208:240].rearrange("p (t b) -> p t b", t=4)
        o_convp = stage[:, 240:252].rearrange("p (t k) -> p t k", t=4)
        o_convs = stage[:, 252:348].rearrange("p (t b k) -> p t b k", t=4, b=NS)
        o_shift = stage[:, 348:474].rearrange("p (t k) -> p t k", t=14)
        o_h = stage[:, 474:510].rearrange("p (t k) -> p t k", t=4)
        ncl, cl, oka = small[:, 4:8], small[:, 8:12], small[:, 12:16]
        sp_t = small[:, 16:32]
        smp = small[:, 32:224].rearrange("p (n t b) -> p n t b", n=6, t=4)
        SD, SKK, SBB, SK, SR, SV = range(6)
        dec = small[:, 224:256].rearrange("p (t c) -> p t c", t=4)

        xc_ready, gates_ready, gates_read = signal("xc_ready"), signal("gates_ready"), signal("gates_read")
        a_ready, m_ready, s_ready, rg_done = map(signal, ("a_ready", "m_ready", "s_ready", "rg_done"))
        x12_ready, wl_ready, wa_ready, wa_read = map(signal, ("x12_ready", "wl_ready", "wa_ready", "wa_read"))
        cs_ready, ex_ready, kk_raw, kk_sq = map(signal, ("cs_ready", "ex_ready", "kk_raw", "kk_sq"))
        kk_sum, kk_max, kk_root, rk_ready = map(signal, ("kk_sum", "kk_max", "kk_root", "rk_ready"))
        k_ready, r_ready, rr_done = map(signal, ("k_ready", "r_ready", "rr_done"))
        bon_sum, bon_read, gelu_done, setup_done = map(signal, ("bon_sum", "bon_read", "gelu_done", "setup_done"))
        lam_exp = signal("lam_exp")

        with nc.Block() as block:
            @block.sync
            def _(sp):
                for q in range(RING, NAB):
                    load_slab(sp, q, ab_src(q))
                for q in range(RING):
                    load_slab(sp, Q_OUT0 + q, i["w_out_ab"][q * P:(q + 1) * P, :])

            @block.gpsimd
            def _(pool):
                S = Serial(pool, pool_step)
                xa4 = A[:, 0:4 * PAD].rearrange("p (t c) -> p t c", t=4)
                S(pool.memset(xa4[:, :, 0:3], 0.0))
                for t in range(4):
                    S(pool.tensor_copy(xa4[:, t, SAMP:PAD].rearrange("p (b k) -> p b k", k=4)[:, :, 0:3], st_conv[:, t]))
                x14 = A[:, X0:X0 + 14 * SHW].rearrange("p (n c) -> p n c", n=14)
                S(pool.memset(x14[:, :, 0:1], 0.0))
                S(pool.tensor_copy(x14[:, :, 513:513 + 2 * NS:2], st_shift))
                for t in range(4):
                    S(pool.tensor_copy(o_convs[:, t, :, 0:2], st_conv[:, t, :, 1:3]))
                setup_done.on(pool.memset(small[:, 3:4], 0.0))
                for t in range(4):
                    pool.wait_ge(k_ready.sem, k_ready.at(t + 1))
                    pool.wait_ge(r_ready.sem, r_ready.at(t + 1))
                    pool.wait_ge(ex_ready.sem, ex_ready.at(t + 1))
                    pool_step.on(pool.tensor_copy(smp[:, SK, t, :], xr(4 + t)[:, SEQ:T]))
                    pool_step.on(pool.tensor_copy(smp[:, SR, t, :], xr(t)[:, SEQ:T]))
                    pool_step.on(pool.tensor_copy(dec[:, t, :], tm(2)[:, 63:SEQ:64]))
                    rr_done.on(pool.tensor_tensor(rw(t, RR), chunks(xr(t)[:, 0:SEQ]), chunks(tm(2)[:, 0:SEQ]), ALU.mult))

            @block.tensor
            def _(pe):
                norm_pe(pe)
                for m in range(NAB):
                    wait_slab(pe, Q_AB + m)
                    if m >= 2:
                        pe.wait_ge(evac.sem, evac.at(m - 1))
                    slab_used.on(product(pe, pt(m % 2), slot(Q_AB + m), KD, lambda k: u3[:, k, :] if m else normed(pe)(k)))
                    if 4 <= m < 8:
                        t = m - 4
                        pe.wait_ge(xc_ready.sem, xc_ready.at(t + 1))
                        if t:
                            pe.wait_ge(gates_read.sem, gates_read.at(t))
                        product(pe, pt(2), bd_r(t), 1, lambda k: xa(t))
                        gates_ready.on(product(pe, pt(3), bd_i(t), 1, lambda k: xa(t)))
                    if 11 <= m < 15:
                        t = m - 11
                        pe.wait_ge(kk_sq.sem, kk_sq.at(t + 1))
                        pe.wait_ge(wa_read.sem, wa_read.at(t + 1))
                        kk_sum.on(product(pe, pt(2), blk, 1, lambda k: tb(0)))
                    if 10 <= m < 14:
                        t = m - 10
                        if t:
                            pe.wait_ge(kk_max.sem, kk_max.at(t))
                        else:
                            pe.wait_ge(wl_ready.sem, wl_ready.at(1))
                            pe.wait_ge(gates_read.sem, gates_read.at(4))
                        for n, (p0, dst) in enumerate(((0, pt(2)), (64, pt(3)))):
                            for a in (0, HALF):
                                mm = pe.matmul(dst[:, a:a + HALF], wa2[p0:p0 + 64, t * P:(t + 1) * P],
                                               xr(12)[p0:p0 + 64, a:a + HALF], start=True, stop=True)
                        wa_ready.on(mm)
                    if 16 <= m < 20:
                        t = m - 16
                        pe.wait_ge(rk_ready.sem, rk_ready.at(t + 1))
                        pe.wait_ge(wa_read.sem, wa_read.at(4))
                        if t:
                            pe.wait_ge(bon_read.sem, bon_read.at(t))
                        bon_sum.on(product(pe, pt(3), blk, 1, lambda k: sg(t)))

            @block.scalar
            def _(act):
                S = Serial(act, act_step)
                S(act.activation(sp_t[:, 0:4], v("lam", 0, 4), ACT.Abs))
                S(act.activation(sp_t[:, 4:8], sp_t[:, 0:4], ACT.Exp, scale=-1.0), lam_exp)
                norm_act(act)
                act.wait_ge(setup_done.sem, setup_done.at(1))
                for m in range(NAB):
                    kind, n = AB_TILES[m]
                    act.wait_ge(slab_used.sem, Q_AB + m + 1)
                    src = pt(m % 2)
                    if kind == "xa":
                        act_step.on(act.activation(xa(n)[:, 3:3 + SEQ], src[:, 0:SEQ], ACT.Copy))
                        act_step.on(act.activation(xa(n)[:, SAMP + 3:PAD:4], src[:, SEQ:T], ACT.Copy))
                        act_step.on(act.activation(o_convp[:, n, :], src[:, SEQ - 3:SEQ], ACT.Copy))
                        evac.on(act.activation(o_convs[:, n, :, 2], src[:, SEQ:T], ACT.Copy))
                    elif kind == "x":
                        act_step.on(act.activation(xr(n)[:, 1:1 + SEQ], src[:, 0:SEQ], ACT.Copy))
                        act_step.on(act.activation(xr(n)[:, 514:514 + 2 * NS:2], src[:, SEQ:T], ACT.Copy))
                        evac.on(act.activation(o_shift[:, n, :], src[:, SEQ - 1:T], ACT.Copy))
                    else:
                        evac.on(act.activation(ga(n), src, ACT.Gelu_apprx_tanh))
                    if 5 <= m < 9:
                        t = m - 5
                        act.wait_ge(gates_ready.sem, gates_ready.at(t + 1))
                        if t:
                            act.wait_ge(rg_done.sem, rg_done.at(t))
                        else:
                            act.wait_ge(xc_ready.sem, xc_ready.at(4))
                        S(act.activation(tm(1)[:, 0:T], pt(2), ACT.Sigmoid, bias=v("b_r", t)))
                        S(act.activation(tm(2)[:, 0:T], pt(3), ACT.Sigmoid, bias=v("b_i", t)), gates_read)
                        S(act.activation(tm(3)[:, 0:T], tm(1)[:, 0:T], ACT.Tanh, scale=ncl[:, t:t + 1]))
                        S(act.activation(tm(1)[:, 0:T], tm(1)[:, 0:T], ACT.Exp, scale=cl[:, t:t + 1]), a_ready)
                        act.wait_ge(m_ready.sem, m_ready.at(t + 1))
                        S(act.activation(tm(3)[:, 0:T], tm(0)[:, 0:T], ACT.Sqrt), s_ready)
                    if m == 9:
                        act.wait_ge(x12_ready.sem, x12_ready.at(2))
                        S(act.activation(xr(13)[:, 0:T], xr(13)[:, 0:T], ACT.Sigmoid))
                        S(act.activation(xr(12)[0:64, 0:T], xr(12)[0:64, 0:T], ACT.Tanh), wl_ready)
                    if 11 <= m < 15:
                        t = m - 11
                        act.wait_ge(kk_raw.sem, kk_raw.at(t + 1))
                        S(act.activation(tb(0)[:, 0:T], tb(1)[:, 0:T], ACT.Square), kk_sq)
                        act.wait_ge(cs_ready.sem, cs_ready.at(t + 1))
                        if t:
                            act.wait_ge(rr_done.sem, rr_done.at(t))
                        S(act.activation(tm(2)[:, 0:SEQ], tm(0)[:, 0:SEQ], ACT.Exp, scale=-C0))
                        S(act.activation(tm(3)[:, 0:SEQ], tm(0)[:, 0:SEQ], ACT.Exp, scale=C0))
                        S(act.activation(tm(1)[:, 0:SEQ], tm(1)[:, 0:SEQ], ACT.Exp, scale=-C0))
                        S(act.activation(smp[:, SD, t, :], sg(t)[:, SEQ:T], ACT.Exp, scale=-C0), ex_ready)
                    if 10 <= m < 14:
                        t = m - 10
                        act.wait_ge(wa_ready.sem, wa_ready.at(t + 1))
                        S(act.activation(sg(t), pt(2), ACT.Sigmoid, bias=v("w0", t)))
                        S(act.activation(av(t), pt(3), ACT.Sigmoid, bias=v("a0", t)), wa_read)
                    if 11 <= m < 15:
                        t = m - 11
                        act.wait_ge(kk_max.sem, kk_max.at(t + 1))
                        S(act.activation(tb(0)[:, 0:T], tb(0)[:, 0:T], ACT.Sqrt), kk_root)

            @block.vector
            def _(dve):
                S = Serial(dve, dve_step)
                norm_dve(dve, "norm_mix0")
                dve.wait_ge(lam_exp.sem, lam_exp.at(1))
                S(dve.tensor_copy(ncl, v("lam", 0, 4)))
                softplus_small(dve, None, S, ncl, sp_t[:, 4:8], sp_t[:, 8:12], sp_t[:, 12:16], -1.0)
                S(dve.tensor_scalar(cl, ncl, -8.0, None, ALU.mult))
                S(dve.tensor_scalar(ncl, ncl, 8.0, None, ALU.mult))
                S(dve.tensor_scalar(oka, v("k_a", 0, 4), -1.0, 1.0, ALU.mult, ALU.add))
                for t in range(4):
                    w = lambda k: v("lru_w", 4 * k + t)
                    x, y = xa(t), tm(0)
                    dve.wait_ge(evac.sem, evac.at(t + 1))
                    S(dve.tensor_scalar(y[:, 0:544], x[:, 3:547], w(3), v("lru_b", t), ALU.mult, ALU.add))
                    for k in (2, 1):
                        S(dve.scalar_tensor_tensor(out=y[:, 0:544], in0=x[:, k:k + 544], scalar=w(k),
                                                   in1=y[:, 0:544], op0=ALU.mult, op1=ALU.add))
                    S(dve.scalar_tensor_tensor(out=x[:, SEQ:T], in0=x[:, SAMP:PAD:4], scalar=w(0),
                                               in1=y[:, SAMP:544:4], op0=ALU.mult, op1=ALU.add))
                    S(dve.scalar_tensor_tensor(out=x[:, 0:SEQ], in0=x[:, 0:SEQ], scalar=w(0),
                                               in1=y[:, 0:SEQ], op0=ALU.mult, op1=ALU.add), xc_ready)
                for t in range(4):
                    a, gi, th = tm(1)[:, 0:T], tm(2)[:, 0:T], tm(3)[:, 0:T]
                    mm = tm(0)[:, 0:T]
                    dve.wait_ge(a_ready.sem, a_ready.at(t + 1))
                    S(dve.tensor_tensor(mm, a, a, ALU.mult))
                    S(dve.scalar_tensor_tensor(out=mm, in0=mm, scalar=1.0, in1=th, op0=ALU.add, op1=ALU.mult), m_ready)
                    S(dve.tensor_tensor(gi, gi, xa(t)[:, 0:T], ALU.mult))
                    dve.wait_ge(s_ready.sem, s_ready.at(t + 1))
                    S(dve.tensor_tensor(gi, gi, th, ALU.mult))
                    S(dve.tensor_tensor_scan(ha(t)[:, 0:SEQ], a[:, 0:SEQ], gi[:, 0:SEQ], 0.0, ALU.mult, ALU.add))
                    S(dve.tensor_tensor(mm[:, 0:NS], a[:, SEQ:T], st_h0[:, t, :], ALU.mult))
                    S(dve.tensor_tensor(ha(t)[:, SEQ:T], mm[:, 0:NS], gi[:, SEQ:T], ALU.add))
                    S(dve.tensor_copy(o_h[:, t, :], ha(t)[:, SEQ - 1:T]), rg_done)

                def shift(n, s=None):
                    x, d = xr(n), td
                    dve.wait_ge(evac.sem, evac.at(1 + AB_TILES.index(("x", n))))
                    S(dve.tensor_tensor(d[:, 0:528], x[:, 0:528], x[:, 1:529], ALU.subtract))
                    S(dve.scalar_tensor_tensor(out=x[:, 0:SEQ], in0=d[:, 0:SEQ], scalar=v("mu", n),
                                               in1=x[:, 1:1 + SEQ], op0=ALU.mult, op1=ALU.add))
                    S(dve.scalar_tensor_tensor(out=x[:, SEQ:T], in0=d[:, 513:513 + 2 * NS:2], scalar=v("mu", n),
                                               in1=x[:, 514:514 + 2 * NS:2], op0=ALU.mult, op1=ALU.add), s)

                shift(12, x12_ready)
                shift(13, x12_ready)
                for t in range(4):
                    xk, xv_, kk, e = xr(4 + t), xr(8 + t), tb(1)[:, 0:T], tm
                    shift(4 + t)
                    S(dve.tensor_scalar(kk, xk[:, 0:T], v("k_k", t), None, ALU.mult), kk_raw)
                    dve.wait_ge(wa_read.sem, wa_read.at(t + 1))
                    S(dve.tensor_tensor_scan(tm(0)[:, 0:SEQ], reset64, sg(t)[:, 0:SEQ], 0.0, ALU.mult, ALU.add))
                    S(dve.tensor_tensor(tm(1)[:, 0:SEQ], tm(0)[:, 0:SEQ], sg(t)[:, 0:SEQ], ALU.subtract), cs_ready)
                    shift(t, r_ready)
                    S(dve.tensor_scalar(td[:, 0:T], av(t), v("k_a", t), oka[:, t:t + 1], ALU.mult, ALU.add))
                    S(dve.tensor_tensor(xk[:, 0:T], xk[:, 0:T], td[:, 0:T], ALU.mult), k_ready)
                    dve.wait_ge(ex_ready.sem, ex_ready.at(t + 1))
                    S(dve.scalar_tensor_tensor(out=sg(t), in0=xr(t)[:, 0:T], scalar=v("r_k", t),
                                               in1=xk[:, 0:T], op0=ALU.mult, op1=ALU.mult), rk_ready)
                    dve.wait_ge(kk_sum.sem, kk_sum.at(t + 1))
                    S(dve.tensor_scalar(tb(0)[:, 0:T], pt(2), 1e-12, None, ALU.max), kk_max)
                    S(dve.tensor_tensor(rw(t, RK), chunks(xk[:, 0:SEQ]), chunks(tm(3)[:, 0:SEQ]), ALU.mult))
                    dve.wait_ge(kk_root.sem, kk_root.at(t + 1))
                    S(dve.reciprocal(tb(0)[:, 0:T], tb(0)[:, 0:T]))
                    S(dve.tensor_tensor(kk, kk, tb(0)[:, 0:T], ALU.mult))
                    S(dve.tensor_tensor(av(t), kk, av(t), ALU.mult))
                    S(dve.tensor_tensor(rw(t, RKAP), chunks(kk[:, 0:SEQ]), chunks(tm(1)[:, 0:SEQ]), ALU.mult))
                    S(dve.tensor_tensor(rw(t, RB), chunks(av(t)[:, 0:SEQ]), chunks(tm(3)[:, 0:SEQ]), ALU.mult))
                    S(dve.tensor_copy(smp[:, SKK, t, :], kk[:, SEQ:T]))
                    S(dve.tensor_copy(smp[:, SBB, t, :], av(t)[:, SEQ:T]))
                for t in range(4):
                    xk, xv_ = xr(4 + t), xr(8 + t)
                    shift(8 + t)
                    S(dve.tensor_copy(rw(t, RV), chunks(xv_[:, 0:SEQ])))
                    S(dve.tensor_copy(smp[:, SV, t, :], xv_[:, SEQ:T]))
                    dve.wait_ge(bon_sum.sem, bon_sum.at(t + 1))
                    dve.wait_ge(rr_done.sem, rr_done.at(t + 1))
                    S(dve.tensor_tensor(xk[:, 0:T], pt(3), xv_[:, 0:T], ALU.mult), bon_read)
                for t in range(4):
                    dve.wait_ge(evac.sem, evac.at(19 + t))
                    S(dve.tensor_tensor(ga(t), ga(t), ha(t), ALU.mult))
        end_of_block()

        def spread(ap, n, axis):
            shape = list(ap.shape)
            shape.insert(axis, n)
            return ap.unsqueeze(axis).broadcast_to(shape)

        rwmask, level = Dm[:, 0:P], lambda l: Dm[:, P * (1 + l):P * (2 + l)]
        sign, i64 = Dm[:, 7 * P:7 * P + 1], Dm[:, 7 * P + 1:7 * P + 65]
        pairs = lambda ap: ap.rearrange("p (n c) -> p n c", c=P)
        AL, DD, EE, GG = [pairs(u_sb[:, n * 1024:(n + 1) * 1024]) for n in range(4)]
        OO = pairs(C[:, 0:1024])
        AM = C[:, 1024:3072].rearrange("p (c h t q) -> p c h t q", c=2, h=2, t=4)
        BK = C[:, 3072:4096].rearrange("p (h c t q) -> p h c t q", c=2, h=2, t=4)
        PV = B[:, 10240:11264].rearrange("p (h c t q) -> p h c t q", c=2, h=2, t=4)
        Qs = Dm[:, 2560:2816].rearrange("p (t q) -> p t q", t=4)
        Zs = [Dm[:, 2816 + 256 * n:3072 + 256 * n].rearrange("p (t q) -> p t q", t=4) for n in range(2)]
        yr = A[:, X0:X0 + 4 * SHW].rearrange("p (t c) -> p t c", t=4)

        def rk(t, c, k, hh, n=1):
            j = ((t * 8 + c) * 5 + k) * 64
            return B[64 * hh:64 * hh + 64, j:j + 64 * n]

        names = ("ab_mm", "ab_read", "am_mm", "am_read", "bk_mm", "bk_read", "v_mm", "v_read", "d_ready", "e_mm",
                 "e_read", "o_ready", "g_mm", "g_read", "eg_mm", "de_read", "q_mm", "q_read", "p_mm",
                 "p_read", "z_mm", "y_mm", "y_read", "z_read")
        g = {n: signal("rw_" + n) for n in names}

        def w(e, name, n):
            e.wait_ge(g[name].sem, g[name].at(n))

        def nth(s, l, cc):
            return 10 * s + 2 * l + cc + 1

        with nc.Block() as block:
            @block.sync
            def _(sp):
                loaded.on(sp.dma_start(Dm[:, 0:961], i["ph_rw"]), 16)

            @block.gpsimd
            def _(pool):
                S = Serial(pool, pool_step)
                pool_step.on(pool.memset(B[0:64, 10240:11264], 0.0))
                S(pool.memset(u_sb[:, 0:1024], 0.0))

            @block.tensor
            def _(pe):
                for s in range(4):
                    if s:
                        w(pe, "de_read", 10 * s)
                        w(pe, "z_read", 2 * s)
                        w(pe, "y_read", 2 * s)
                    for cc in range(2):
                        for t in range(4):
                            n = (4 * cc + t) * P
                            for hh in range(2):
                                mm = pe.matmul(ps[0][64 * hh:64 * hh + 64, n + 64 * hh:n + 64 * hh + 64],
                                               rk(t, 2 * s + cc, RKAP, hh), rk(t, 2 * s + cc, RB, hh),
                                               start=True, stop=True)
                    g["ab_mm"].on(mm)
                    for cc in range(2):
                        for t in range(4):
                            for hh in range(2):
                                mm = pe.matmul(ps[1 + cc][:, 512 * hh + t * P:512 * hh + (t + 1) * P],
                                               rk(t, 2 * s + cc, RB, hh, 2), rk(t, 2 * s + cc, RR, hh, 2),
                                               start=True, stop=True)
                        g["am_mm"].on(mm)
                    for cc in range(2):
                        for t in range(4):
                            for hh in range(2):
                                j, n = 64 * hh, 512 * hh + (4 * cc + t) * 64
                                mm = pe.transpose(ps[3][:, n:n + 64], rk(t, 2 * s + cc, RB, hh, 2),
                                                  ident[j:j + 64, j:j + 64])
                    g["bk_mm"].on(mm)
                    w(pe, "ab_read", s + 1)
                    for cc in range(2):
                        for t in range(4):
                            for hh in range(2):
                                j, n = 64 * hh, 512 * hh + (4 * cc + t) * 64
                                mm = pe.transpose(ps[0][:, n:n + 64], rk(t, 2 * s + cc, RKAP, hh, 2),
                                                  ident[j:j + 64, j:j + 64])
                    g["v_mm"].on(mm)
                    w(pe, "d_ready", s + 1)
                    w(pe, "am_read", 2 * s + 2)
                    for n in range(8):
                        mm = pe.transpose(ps[1][:, n * P:(n + 1) * P], DD[:, n, :], ident)
                    g["e_mm"].on(mm)
                    w(pe, "v_read", s + 1)
                    for l in range(5):
                        for cc in range(2):
                            w(pe, "o_ready", nth(s, l, cc))
                            if l == 0:
                                w(pe, "e_read", s + 1)
                            else:
                                w(pe, "de_read", nth(s, l - 1, cc))
                            for n in range(4 * cc, 4 * cc + 4):
                                mm = pe.matmul(ps[0][:, n * P:(n + 1) * P], OO[:, n, :], EE[:, n, :], start=True, stop=True)
                            g["g_mm"].on(mm)
                        for cc in range(2):
                            w(pe, "g_read", nth(s, l, cc))
                            for n in range(4 * cc, 4 * cc + 4):
                                if l < 4:
                                    pe.matmul(ps[1][:, n * P:(n + 1) * P], GG[:, n, :], DD[:, n, :], start=True, stop=True)
                                mm = pe.matmul(ps[2][:, n * P:(n + 1) * P], DD[:, n, :], GG[:, n, :], start=True, stop=True)
                            g["eg_mm"].on(mm)
                    w(pe, "de_read", 10 * s + 10)
                    w(pe, "bk_read", s + 1)
                    for cc in range(2):
                        c = 2 * s + cc
                        z = Zs[(c + 1) % 2]
                        if c:
                            w(pe, "z_read", c)
                        for t in range(4):
                            for hh in range(2):
                                dst = ps[0][64 * hh:64 * hh + 64, 64 * t:64 * t + 64]
                                if c:
                                    pe.matmul(dst, rk(t, c, RKAP, hh), z[64 * hh:64 * hh + 64, t, :], start=True, stop=False)
                                mm = pe.matmul(dst, AM[:, cc, hh, t, 64:P], PV[:, hh, cc, t, :],
                                               start=c == 0, stop=True)
                        g["q_mm"].on(mm)
                        w(pe, "q_read", c + 1)
                        for t in range(4):
                            for hh in range(2):
                                j = 64 * hh
                                mm = pe.matmul(ps[1][0:64, 512 * hh + 64 * t:512 * hh + 64 * t + 64],
                                               EE[j:j + 64, 4 * cc + t, j:j + 64], Qs[j:j + 64, t, :],
                                               start=True, stop=True)
                        g["p_mm"].on(mm)
                        w(pe, "p_read", c + 1)
                        for t in range(4):
                            for hh in range(2):
                                mm = pe.matmul(ps[2][64 * hh:64 * hh + 64, 64 * t:64 * t + 64],
                                               BK[:, hh, cc, t, :], PV[:, hh, cc, t, :], start=True, stop=True)
                        g["z_mm"].on(mm)
                        if c:
                            w(pe, "y_read", c)
                        for t in range(4):
                            for hh in range(2):
                                dst = ps[3][64 * hh:64 * hh + 64, 64 * t:64 * t + 64]
                                if c:
                                    pe.matmul(dst, z[64 * hh:64 * hh + 64, t, :], rk(t, c, RR, hh), start=True, stop=False)
                                mm = pe.matmul(dst, PV[:, hh, cc, t, :], AM[:, cc, hh, t, 0:64],
                                               start=c == 0, stop=True)
                        g["y_mm"].on(mm)

            @block.scalar
            def _(act):
                for s in range(4):
                    w(act, "bk_mm", s + 1)
                    if s == 0:
                        act.wait_ge(loaded.sem, loaded.count)
                    else:
                        w(act, "z_mm", 2 * s)
                    g["bk_read"].on(act.activation(C[:, 3072:4096], ps[3][:, :], ACT.Copy, scale=sign))
                    w(act, "v_mm", s + 1)
                    if s:
                        w(act, "y_mm", 2 * s)
                    g["v_read"].on(act.activation(B[64:P, 10240:11264], ps[0][64:P, :], ACT.Copy))
                    w(act, "e_mm", s + 1)
                    g["e_read"].on(act.activation(u_sb[:, 2048:3072], ps[1][:, :], ACT.Copy))
                    for l in range(5):
                        for cc in range(2):
                            w(act, "g_mm", nth(s, l, cc))
                            if l:
                                w(act, "eg_mm", nth(s, l - 1, cc))
                            g["g_read"].on(act.activation(u_sb[:, 3072 + 512 * cc:3584 + 512 * cc],
                                                          ps[0][:, 512 * cc:512 * cc + 512], ACT.Copy))
                    for cc in range(2):
                        c = 2 * s + cc
                        w(act, "p_mm", c + 1)
                        for hh in range(2):
                            ins = act.activation(PV[0:64, hh, cc], ps[1][0:64, 512 * hh:512 * hh + 256]
                                                 .rearrange("p (t q) -> p t q", t=4), ACT.Copy)
                            (g["p_read"] if hh else act_step).on(ins)
                        w(act, "y_mm", c + 1)
                        g["y_read"].on(act.activation(yr[:, :, 64 * c:64 * c + 64],
                                                      ps[3][:, 0:256].rearrange("p (t q) -> p t q", t=4), ACT.Copy))

            @block.vector
            def _(dve):
                S = Serial(dve, dve_step)
                dve.wait_ge(loaded.sem, loaded.count)
                dve.wait_ge(pool_step.sem, pool_step.at(2))
                for s in range(4):
                    w(dve, "ab_mm", s + 1)
                    for hh in range(2):
                        j = 64 * hh
                        S(dve.tensor_copy(AL[j:j + 64, :, j:j + 64], pairs(ps[0][j:j + 64, :])[:, :, j:j + 64]),
                          g["ab_read"] if hh else None)
                    S(dve.tensor_tensor(OO, AL, spread(level(0), 8, 1), ALU.mult))
                    S(dve.tensor_tensor(DD, spread(ident, 8, 1), OO, ALU.subtract), g["d_ready"])
                    for cc in range(2):
                        n = slice(4 * cc, 4 * cc + 4)
                        S(dve.tensor_tensor(OO[:, n], AL[:, n], spread(level(1), 4, 1), ALU.mult), g["o_ready"])
                    for cc in range(2):
                        w(dve, "am_mm", 2 * s + cc + 1)
                        if s and cc == 0:
                            w(dve, "y_mm", 2 * s)
                        S(dve.tensor_tensor(pairs(C[:, 1024 * (1 + cc):1024 * (2 + cc)]), pairs(ps[1 + cc][:, :]),
                                            spread(rwmask, 8, 1), ALU.mult), g["am_read"])
                    for l in range(5):
                        for cc in range(2):
                            n, half = slice(4 * cc, 4 * cc + 4), slice(512 * cc, 512 * cc + 512)
                            w(dve, "eg_mm", nth(s, l, cc))
                            if l < 4:
                                S(dve.tensor_tensor(DD[:, n], DD[:, n], pairs(ps[1][:, half]), ALU.subtract))
                            S(dve.tensor_tensor(EE[:, n], EE[:, n], pairs(ps[2][:, half]), ALU.subtract), g["de_read"])
                            if l < 4:
                                S(dve.tensor_tensor(OO[:, n], AL[:, n], spread(level(l + 2), 4, 1), ALU.mult), g["o_ready"])
                    for cc in range(2):
                        c = 2 * s + cc
                        z, z1 = Zs[(c + 1) % 2], Zs[c % 2]
                        dc = dec[:, :, c].unsqueeze(2).broadcast_to([P, 4, 64])
                        w(dve, "q_mm", c + 1)
                        S(dve.tensor_copy(Qs, ps[0][:, 0:256].rearrange("p (t q) -> p t q", t=4)), g["q_read"])
                        w(dve, "z_mm", c + 1)
                        if c:
                            w(dve, "y_mm", c)
                        pz = ps[2][:, 0:256].rearrange("p (t q) -> p t q", t=4)
                        if c:
                            S(dve.tensor_tensor(z1, pz, z, ALU.add))
                            S(dve.tensor_tensor(z1, z1, dc, ALU.mult), g["z_read"])
                        else:
                            S(dve.tensor_tensor(z1, pz, dc, ALU.mult), g["z_read"])
        end_of_block()

        S0 = u_sb[:, 0:2048]
        DG = u_sb[:, 2048:4096]
        S1, T1 = B[:, 0:2048], B[:, 2048:4096]
        btk = lambda ap: ap.rearrange("p (n k) -> p n k", k=64)
        row = small[:, 256:288]
        tmpn = small[:, 288:352]

        def per_bt(n):
            return smp[:, n].rearrange("p t b -> p b t").unsqueeze(3).broadcast_to([P, NS, 4, 64])

        b4 = lambda ap: ap.rearrange("p (b t k) -> p b t k", b=NS, t=4)
        dg_ready, bc_mm, bc_read, st_in, norm_a, norm_b = map(signal, (
            "dg_ready", "bc_mm", "bc_read", "st_in", "norm_a", "norm_b"))
        mean_mm, var_mm, g_mm, sq_ready, root_ready, cent, g_read = map(signal, (
            "mean_mm", "var_mm", "g_mm", "sq_ready", "root_ready", "cent", "g_read"))
        ORDER = (SKK, SD, SBB, SK, SR)
        with nc.Block() as block:
            @block.sync
            def _(sp):
                st_in.on(sp.dma_start(S0, i["s_rw"]), 16)
                stored.on(sp.dma_start(o["wkv_p"], Dm[:, 3072:3328]), 16)
                stored.on(sp.dma_start(o["ab_small"], stage[:, 240:510]), 16)
                sp.wait_ge(dve_step.sem, dve_step.at(1))
                stored.on(sp.dma_start(o["wkv_s"], S1), 16)
                sp.wait_ge(stored.sem, stored.count)

            @block.tensor
            def _(pe):
                for n in range(5):
                    pe.wait_ge(dg_ready.sem, dg_ready.at(n + 1))
                    if n:
                        pe.wait_ge(bc_read.sem, bc_read.at(n))
                    for q in range(4):
                        mm = pe.matmul(ps[q // 2][:, 512 * (q % 2):512 * (q % 2) + 512], blk,
                                       DG[:, 512 * q:512 * q + 512], start=True, stop=True)
                    bc_mm.on(mm)
                pe.wait_ge(bc_read.sem, bc_read.at(5))
                for t in range(4):
                    if t == 0:
                        pe.wait_ge(norm_a.sem, norm_a.at(1))
                    else:
                        pe.wait_ge(cent.sem, cent.at(t))
                    mean_mm.on(product(pe, pt(0), blk, 1, lambda k: yr[:, t, 0:T]))
                for t in range(4):
                    pe.wait_ge(sq_ready.sem, sq_ready.at(t + 1))
                    if t:
                        pe.wait_ge(root_ready.sem, root_ready.at(t))
                    var_mm.on(product(pe, pt(1), blk, 1, lambda k: xr(8 + t)[:, 0:T]))
                for t in range(4):
                    if t >= 2:
                        pe.wait_ge(g_read.sem, g_read.at(t - 1))
                    g_mm.on(product(pe, pt(2 + t % 2), g2[:, t * P:(t + 1) * P], 1, lambda k: xr(13)[:, 0:T]))

            @block.scalar
            def _(act):
                for t in range(4):
                    act.wait_ge(cent.sem, cent.at(t + 1))
                    sq_ready.on(act.activation(xr(8 + t)[:, 0:T], yr[:, t, 0:T], ACT.Square))
                for t in range(4):
                    act.wait_ge(var_mm.sem, var_mm.at(t + 1))
                    root_ready.on(act.activation(xr(8 + t)[:, 0:T], pt(1), ACT.Sqrt, bias=small[:, 1:2], scale=1.0 / 64))

            @block.vector
            def _(dve):
                S = Serial(dve, norm_b)

                def diag(n):
                    S(dve.tensor_tensor(b4(DG), i64.unsqueeze(1).unsqueeze(1).broadcast_to([P, NS, 4, 64]),
                                        per_bt(n), ALU.mult), dg_ready)

                def halves():
                    for q in range(2):
                        yield slice(1024 * q, 1024 * q + 1024), ps[q][:, :], slice(16 * q, 16 * q + 16)

                def wait_bc(n):
                    dve.wait_ge(bc_mm.sem, bc_mm.at(n))

                diag(SKK)
                dve.wait_ge(st_in.sem, st_in.count)
                wait_bc(1)
                for c, bc, r in halves():
                    S(dve.tensor_tensor(T1[:, c], S0[:, c], bc, ALU.mult), bc_read if c.start else None)
                S(dve.tensor_reduce(row, btk(T1), AX.X, ALU.add))
                diag(SD)
                wait_bc(2)
                for c, bc, r in halves():
                    S(dve.tensor_tensor(S1[:, c], S0[:, c], bc, ALU.mult), bc_read if c.start else None)
                diag(SBB)
                wait_bc(3)
                for c, bc, r in halves():
                    S(dve.tensor_tensor(btk(T1[:, c]), btk(bc), row[:, r].unsqueeze(2).broadcast_to([P, 16, 64]), ALU.mult),
                      bc_read if c.start else None)
                S(dve.tensor_tensor(S1, S1, T1, ALU.subtract))
                S(dve.tensor_copy(row.rearrange("p (b t) -> p b t", b=NS), smp[:, SV].rearrange("p t b -> p b t")))
                diag(SK)
                wait_bc(4)
                for c, bc, r in halves():
                    S(dve.tensor_tensor(btk(T1[:, c]), btk(bc), row[:, r].unsqueeze(2).broadcast_to([P, 16, 64]), ALU.mult),
                      bc_read if c.start else None)
                S(dve.tensor_tensor(S1, S1, T1, ALU.add), dve_step)
                diag(SR)
                wait_bc(5)
                for c, bc, r in halves():
                    S(dve.tensor_tensor(T1[:, c], S1[:, c], bc, ALU.mult), bc_read if c.start else None)
                S(dve.tensor_reduce(row, btk(T1), AX.X, ALU.add))
                S(dve.tensor_copy(yr[:, :, SEQ:T], row.rearrange("p (b t) -> p t b", b=NS)), norm_a)
                for t in range(4):
                    dve.wait_ge(mean_mm.sem, mean_mm.at(t + 1))
                    S(dve.scalar_tensor_tensor(out=yr[:, t, 0:T], in0=pt(0), scalar=-1.0 / 64, in1=yr[:, t, 0:T],
                                               op0=ALU.mult, op1=ALU.add), cent)
                for t in range(4):
                    y, r = yr[:, t, 0:T], xr(8 + t)[:, 0:T]
                    dve.wait_ge(root_ready.sem, root_ready.at(t + 1))
                    S(dve.reciprocal(r, r))
                    S(dve.tensor_tensor(y, y, r, ALU.mult))
                    S(dve.tensor_scalar(y, y, v("ln_w", t), v("ln_b", t), ALU.mult, ALU.add))
                    S(dve.tensor_tensor(y, y, xr(4 + t)[:, 0:T], ALU.add))
                    dve.wait_ge(g_mm.sem, g_mm.at(t + 1))
                    S(dve.tensor_tensor(y, y, pt(2 + t % 2), ALU.mult), g_read)
        end_of_block()

        silu_done, hid_done = signal("silu_done"), signal("hid_done")
        emb_in = signal("emb_in")
        tmp2 = lambda n: C[:, (n % 2) * T:(n % 2) * T + T]
        hid = lambda k: B[:, k * T:(k + 1) * T]

        def slab_rows(name, n):
            return i[name][bass.ds(n * P, P), :]

        def prefetch(sp, q0, name, count=RING):
            for q in range(count):
                load_slab(sp, q0 + q, slab_rows(name, q))

        def out_block(q0, name, rhs, nxt):
            with nc.Block() as block:
                @block.sync
                def _(sp):
                    for m in range(RING, KD):
                        load_slab(sp, q0 + m, slab_rows(name, m))
                    if nxt:
                        prefetch(sp, q0 + KD, nxt)

                @block.tensor
                def _(pe):
                    for m in range(KD):
                        wait_slab(pe, q0 + m)
                        if m >= 4:
                            pe.wait_ge(evac.sem, evac.at(m - 3))
                        slab_used.on(product(pe, pt(m), slot(q0 + m), KD, rhs))

                @block.vector
                def _(dve):
                    for m in range(KD):
                        dve.wait_ge(slab_used.sem, q0 + m + 1)
                        evac.on(dve.tensor_tensor(h3[:, m, :], pt(m), h3[:, m, :], ALU.add))
                        if m >= 2:
                            add_square(dve, m - 1)
                    add_square(dve, KD - 1)

                @block.scalar
                def _(act):
                    for m in range(KD):
                        act.wait_ge(evac.sem, evac.at(m + 1))
                        square(act, m)
            squares_counted()
            end_of_block()

        def ffn_block(gain):
            PEEL, PER, TRIPS = 4, 6, 3
            DPEEL, DPER, DTRIPS = 2, 3, 2

            def hidden_tiles(e, body):
                for m in range(PEEL):
                    body(m, None)
                with e.Fori(0, TRIPS) as turn:
                    for j in range(PER):
                        body(PEEL + j, turn)

            def down_tiles(e, body):
                for m in range(DPEEL):
                    body(m, None)
                with e.Fori(0, DTRIPS) as turn:
                    for j in range(DPER):
                        body(DPEEL + j, turn)

            def nth(n, turn, per):
                return n if turn is None else n + per * turn

            with nc.Block() as block:
                @block.sync
                def _(sp):
                    for n in range(RING, 2 * PEEL):
                        load_slab(sp, Q_GU + n, slab_rows("w_gu", n))
                    with sp.Fori(0, TRIPS) as turn:
                        for j in range(2 * PER):
                            n = 2 * PEEL + j
                            load_slab(sp, Q_GU + n, slab_rows("w_gu", n + 2 * PER * turn), (turn, 2 * PER))
                    for n in range(2 * DPEEL):
                        load_slab(sp, Q_DN + n, slab_rows("w_dn", n))
                    with sp.Fori(0, DTRIPS) as turn:
                        for j in range(2 * DPER):
                            n = 2 * DPEEL + j
                            load_slab(sp, Q_DN + n, slab_rows("w_dn", n + 2 * DPER * turn), (turn, 2 * DPER))
                    prefetch(sp, Q_PLE0, "w_ple0")

                @block.tensor
                def _(pe):
                    def hidden(m, turn):
                        k = None if turn is None else (turn, 2 * PER)
                        if m >= 2:
                            pe.wait_ge(hid_done.sem, hid_done.at(nth(m - 1, turn, PER)))
                        for s in range(2):
                            wait_slab(pe, Q_GU + 2 * m + s, k)
                            product(pe, pt(2 * (m % 2) + s), slot(Q_GU + 2 * m + s), KD,
                                    normed(pe) if m == 0 and s == 0 else lambda n: u3[:, n, :]).then_inc(slab_used.sem, 1)

                    norm_pe(pe)
                    hidden_tiles(pe, hidden)

                    def down(m, turn):
                        k = None if turn is None else (turn, 2 * DPER)
                        if m < DPEEL:
                            pe.wait_ge(hid_done.sem, hid_done.at(KF))
                        if m >= 2:
                            pe.wait_ge(evac.sem, evac.at(nth(m - 2, turn, DPER)))
                        for s in range(2):
                            wait_slab(pe, Q_DN + 2 * m + s, k)
                            product(pe, pt(m), slot(Q_DN + 2 * m + s), KF // 2, lambda n: hid(s * (KF // 2) + n),
                                    first=s == 0, last=s == 1).then_inc(slab_used.sem, 1)

                    down_tiles(pe, down)

                @block.scalar
                def _(act):
                    def silu(m, turn):
                        act.wait_ge(slab_used.sem, nth(Q_GU + 2 * m + 1, turn, 2 * PER))
                        if m >= 2:
                            act.wait_ge(hid_done.sem, hid_done.at(nth(m - 1, turn, PER)))
                        act.activation(tmp2(m), pt(2 * (m % 2)), ACT.Silu).then_inc(silu_done.sem, 1)

                    norm_act(act)
                    hidden_tiles(act, silu)
                    silu_done.add(KF)

                    def squares(m, turn):
                        act.wait_ge(evac.sem, evac.at(nth(m + 1, turn, DPER)))
                        if turn is None:
                            square(act, m)
                        else:
                            square(act, m, h_sb[:, bass.ds(m * T + (DPER * T) * turn, T)], DPER * turn, True)

                    down_tiles(act, squares)

                @block.vector
                def _(dve):
                    def gate(m, turn):
                        dve.wait_ge(silu_done.sem, silu_done.at(nth(m + 1, turn, PER)))
                        dve.wait_ge(slab_used.sem, nth(Q_GU + 2 * m + 2, turn, 2 * PER))
                        dst = hid(m) if turn is None else B[:, bass.ds(m * T + (PER * T) * turn, T)]
                        dve.tensor_tensor(dst, tmp2(m), pt(2 * (m % 2) + 1), ALU.mult).then_inc(hid_done.sem, 1)

                    norm_dve(dve, gain)
                    hidden_tiles(dve, gate)
                    hid_done.add(KF)

                    def add(m, turn):
                        dve.wait_ge(slab_used.sem, nth(Q_DN + 2 * m + 2, turn, 2 * DPER))
                        dst = h3[:, m, :] if turn is None else h_sb[:, bass.ds(m * T + (DPER * T) * turn, T)]
                        dve.tensor_tensor(dst, pt(m), dst, ALU.add).then_inc(evac.sem, 1)
                        if m >= 2:
                            add_square(dve, m - 1, DPER * turn, True)

                    down_tiles(dve, add)
                    add_square(dve, KD - 1)
                    evac.add(KD)
            squares_counted()
            slab_used.add(2 * KF + 2 * KD)
            for q in range(Q_GU + 2 * PEEL + 2 * PER, Q_DN):
                slab_in[q % RING].add(16)
            for q in range(Q_DN + 2 * DPEEL + 2 * DPER, Q_PLE0):
                slab_in[q % RING].add(16)
            end_of_block()

        def ple_block(q0, layer, nxt, gain):
            emb = A[:, 0:2 * T].rearrange("p (k t) -> p k t", t=T)
            with nc.Block() as block:
                @block.sync
                def _(sp):
                    for m in range(RING, KD):
                        load_slab(sp, q0 + m, slab_rows(f"w_ple{layer}", m))
                    if nxt:
                        prefetch(sp, q0 + KD, nxt)

                @block.gpsimd
                def _(pool):
                    emb_in.on(pool.dma_start(emb, i["p"][layer]), 16)

                @block.tensor
                def _(pe):
                    norm_pe(pe)
                    for m in range(KD):
                        wait_slab(pe, q0 + m)
                        if m >= 2:
                            pe.wait_ge(evac.sem, evac.at(m - 1))
                        product(pe, pt(2 * (m % 2)), slot(q0 + m), KD, lambda k: u3[:, k, :] if m else normed(pe)(k))
                        if m == 0:
                            pe.wait_ge(emb_in.sem, emb_in.at(16))
                        slab_used.on(product(pe, pt(2 * (m % 2) + 1), slot(q0 + m)[:, KD * P:], 2,
                                             lambda k: emb[:, k, :]))

                @block.scalar
                def _(act):
                    norm_act(act)
                    for m in range(KD + 1):
                        if m < KD:
                            act.wait_ge(slab_used.sem, q0 + m + 1)
                            if m >= 2:
                                act.wait_ge(evac.sem, evac.at(m - 1))
                            silu_done.on(act.activation(tmp2(m), pt(2 * (m % 2)), ACT.Sigmoid))
                        if m:
                            act.wait_ge(evac.sem, evac.at(m))
                            square(act, m - 1)

                @block.vector
                def _(dve):
                    norm_dve(dve, gain)
                    S = Serial(dve, dve_step)
                    for m in range(KD):
                        dve.wait_ge(silu_done.sem, silu_done.at(m + 1))
                        S(dve.tensor_tensor(tmp2(m), tmp2(m), pt(2 * (m % 2) + 1), ALU.mult))
                        evac.on(dve.tensor_tensor(h3[:, m, :], tmp2(m), h3[:, m, :], ALU.add))
                        if m >= 2:
                            add_square(dve, m - 1)
                    add_square(dve, KD - 1)
            squares_counted()
            end_of_block()

        out_block(Q_OUT0, "w_out_ab", lambda k: ga(k) if k < 4 else yr[:, k - 4, 0:T], "w_gu")
        ffn_block("norm_ffn0")
        ple_block(Q_PLE0, 0, "w_in_cd", "norm_ple0")

        G0 = 8 * PAD
        qt = lambda t: A[:, G0 + t * T:G0 + (t + 1) * T]
        kt = lambda t: A[:, G0 + (2 + t) * T:G0 + (3 + t) * T]
        vt = lambda t: A[:, G0 + (4 + t) * T:G0 + (5 + t) * T]
        zt = lambda t: A[:, G0 + (8 + t) * T:G0 + (9 + t) * T]
        gt = lambda t: A[:, G0 + (12 + t) * T:G0 + (13 + t) * T]
        sm = A[:, G0 + 16 * T:G0 + 17 * T]
        KN = lambda t: C[:, t * SEQ:(t + 1) * SEQ]
        tq = lambda n: C[:, 1024 + n * 548:1024 + n * 548 + 548]
        cum, dtr = C[0:8, 3216:3728], C[0:8, 3728:4248]
        col8 = 0
        parts = {}
        for name, width in (("sel8", 1024), ("selp", 512), ("last", P), ("ssdmask", P), ("glamask", P),
                            ("reset128", SEQ), ("reset32", SEQ), ("alpha", 256), ("router", 64), ("reset8", 40), ("iota", P), ("index", 1), ("before", NEXP)):
            parts[name] = Dm[:, col8:col8 + width]
            col8 += width
        sel8 = lambda n: parts["sel8"][0:8, n * P:(n + 1) * P]
        selp = lambda t: parts["selp"][0:8, t * P:(t + 1) * P]
        s_hist = stage[:, 0:192].rearrange("p (t b k) -> p t b k", t=8, b=NS)
        o2_convp = stage[:, 192:216].rearrange("p (t k) -> p t k", t=8)
        o2_convs = stage[:, 216:408].rearrange("p (t b k) -> p t b k", t=8, b=NS)
        cumT, dtT, cend, ecend, wend = [small[:, 4 + 32 * n:36 + 32 * n] for n in range(5)]
        dts, las = [small[:, 164 + 32 * n:196 + 32 * n].rearrange("p (t b) -> p t b", t=4) for n in range(2)]
        gdec = small[:, 228:260].rearrange("p (t c) -> p t c", t=2)
        gds = small[:, 260:276].rearrange("p (t b) -> p t b", t=2)
        aneg, las8 = small[0:8, 276:277], small[0:8, 277:285]
        sm_mm, conv_done, dt_abs, dt_exp, dt_ready = map(signal, ("sm_mm", "conv_done", "dt_abs", "dt_exp", "dt_ready"))
        al_mm, al_log, al_min, al_read, cs2_ready, ex2_ready, gla_read = map(signal, (
            "al_mm", "al_log", "al_min", "al_read", "cs2_ready", "ex2_ready", "gla_read"))
        X_M = lambda n: 1 + n
        with nc.Block() as block:
            @block.sync
            def _(sp):
                loaded.on(sp.dma_start(Dm[:, 0:col8], i["ph_cd"]), 16)
                loaded.on(sp.dma_start(stage[:, 0:192], i["st_cd"]), 16)
                for m in range(RING, NCD):
                    load_slab(sp, Q_CD + m, slab_rows("w_in_cd", m))
                prefetch(sp, Q_OUT1, "w_out_cd")

            @block.gpsimd
            def _(pool):
                S = Serial(pool, pool_step)
                xa8 = A[:, 0:8 * PAD].rearrange("p (t c) -> p t c", t=8)
                S(pool.memset(xa8[:, :, 0:3], 0.0))
                pool.wait_ge(loaded.sem, loaded.count)
                for t in range(8):
                    S(pool.tensor_copy(xa8[:, t, SAMP:PAD].rearrange("p (b k) -> p b k", k=4)[:, :, 0:3], s_hist[:, t]))
                    S(pool.tensor_copy(o2_convs[:, t, :, 0:2], s_hist[:, t, :, 1:3]))
                setup_done.on(pool.memset(small[:, 3:4], 0.0))

            @block.tensor
            def _(pe):
                norm_pe(pe)
                for m in range(NCD):
                    wait_slab(pe, Q_CD + m)
                    if m >= 2:
                        pe.wait_ge(evac.sem, evac.at(m - 1))
                    slab_used.on(product(pe, pt(m % 2), slot(Q_CD + m), KD, lambda k: u3[:, k, :] if m else normed(pe)(k),
                                         width=48 if m == 0 else P))
                    if m in (10, 13):
                        t = (m - 10) // 3
                        pe.wait_ge(evac.sem, evac.at(1))
                        if t:
                            pe.wait_ge(al_read.sem, al_read.at(t))
                        for a in (0, HALF):
                            mm = pe.matmul(pt(2)[:, a:a + HALF], parts["alpha"][32:48, t * P:(t + 1) * P],
                                           sm[32:48, a:a + HALF], start=True, stop=True)
                        al_mm.on(mm)

            @block.scalar
            def _(act):
                S = Serial(act, act_step)
                norm_act(act)
                act.wait_ge(setup_done.sem, setup_done.at(1))
                S(act.activation(aneg, v("a_log")[0:8], ACT.Exp))
                for m in range(NCD):
                    act.wait_ge(slab_used.sem, Q_CD + m + 1)
                    src = pt(m % 2)
                    if m == 0:
                        S(act.activation(sm[0:48], src[0:48], ACT.Copy), evac)
                        S(act.activation(dtr, sm[0:8], ACT.Identity, bias=v("dt_bias")[0:8]))
                        S(act.activation(tq(0)[0:8, 0:T], dtr, ACT.Abs))
                        S(act.activation(tq(0)[0:8, 0:T], tq(0)[0:8, 0:T], ACT.Exp, scale=-1.0), dt_exp)
                    elif m < 9:
                        n = m - 1
                        act_step.on(act.activation(xa(n)[:, 3:3 + SEQ], src[:, 0:SEQ], ACT.Copy))
                        act_step.on(act.activation(xa(n)[:, SAMP + 3:PAD:4], src[:, SEQ:T], ACT.Copy))
                        act_step.on(act.activation(o2_convp[:, n, :], src[:, SEQ - 3:SEQ], ACT.Copy))
                        evac.on(act.activation(o2_convs[:, n, :, 2], src[:, SEQ:T], ACT.Copy))
                    elif m < 17:
                        evac.on(act.activation(A[:, G0 + (m - 9) * T:G0 + (m - 8) * T], src, ACT.Copy))
                    else:
                        evac.on(act.activation(A[:, G0 + (m - 9) * T:G0 + (m - 8) * T], src, ACT.Silu))
                    if m in (11, 14):
                        t = (m - 11) // 3
                        if t:
                            act.wait_ge(gla_read.sem, gla_read.at(t))
                        else:
                            act.wait_ge(dt_ready.sem, dt_ready.at(1))
                        act.wait_ge(al_mm.sem, al_mm.at(t + 1))
                        S(act.activation(tq(2)[:, 0:T], pt(2), ACT.Abs, bias=v("alpha_b", t)))
                        S(act.activation(tq(2)[:, 0:T], tq(2)[:, 0:T], ACT.Exp, scale=-1.0))
                        S(act.activation(tq(2)[:, 0:T], tq(2)[:, 0:T], ACT.Ln, bias=small[:, 2:3]), al_log)
                        act.wait_ge(cs2_ready.sem, cs2_ready.at(t + 1))
                        S(act.activation(tq(3)[:, 0:SEQ], tq(1)[:, 0:SEQ], ACT.Exp, scale=1.0 / 16))
                        S(act.activation(tq(1)[:, 0:SEQ], tq(1)[:, 0:SEQ], ACT.Exp, scale=-1.0 / 16))
                        S(act.activation(gds[:, t, :], tq(2)[:, SEQ:T], ACT.Exp, scale=1.0 / 16))
                        S(act.activation(tq(2)[:, 0:SEQ], tq(2)[:, 0:SEQ], ACT.Exp, scale=1.0 / 16), ex2_ready)
                    if 3 <= m < 9 or m == 9 or m == 10:
                        n = m - 3
                        act.wait_ge(conv_done.sem, conv_done.at(n + 1))
                        S(act.activation(xa(n)[:, 0:T], xa(n)[:, 0:T], ACT.Silu))

            @block.vector
            def _(dve):
                S = Serial(dve, dve_step)
                norm_dve(dve, "norm_mix1")
                dve.wait_ge(dt_exp.sem, dt_exp.at(1))
                softplus_small(dve, None, S, dtr, tq(0)[0:8, 0:T], tq(1)[0:8, 0:T], tq(2)[0:8, 0:T], 1.0)
                S(dve.tensor_scalar(aneg, aneg, -1.0, None, ALU.mult))
                S(dve.tensor_scalar(tq(0)[0:8, 0:T], dtr, aneg, None, ALU.mult))
                S(dve.tensor_copy(las8, tq(0)[0:8, SEQ:T]))
                S(dve.tensor_tensor_scan(cum, parts["reset128"][0:8, :], tq(0)[0:8, 0:SEQ], 0.0, ALU.mult, ALU.add), dt_ready)

                def conv(n):
                    w = lambda k: v("ssd_w", 8 * k + n)
                    x, y = xa(n), tq(0)
                    dve.wait_ge(evac.sem, evac.at(n + 2))
                    S(dve.tensor_scalar(y[:, 0:544], x[:, 3:547], w(3), v("ssd_b", n), ALU.mult, ALU.add))
                    for k in (2, 1):
                        S(dve.scalar_tensor_tensor(out=y[:, 0:544], in0=x[:, k:k + 544], scalar=w(k),
                                                   in1=y[:, 0:544], op0=ALU.mult, op1=ALU.add))
                    S(dve.scalar_tensor_tensor(out=x[:, SEQ:T], in0=x[:, SAMP:PAD:4], scalar=w(0),
                                               in1=y[:, SAMP:544:4], op0=ALU.mult, op1=ALU.add))
                    S(dve.scalar_tensor_tensor(out=x[:, 0:SEQ], in0=x[:, 0:SEQ], scalar=w(0),
                                               in1=y[:, 0:SEQ], op0=ALU.mult, op1=ALU.add), conv_done)

                def decay(t):
                    la, cs, to_end = tq(2)[:, 0:T], tq(1)[:, 0:SEQ], tq(2)[:, 0:SEQ]
                    dve.wait_ge(al_log.sem, al_log.at(t + 1))
                    S(dve.tensor_scalar(tq(3)[:, 0:T], pt(2), v("alpha_b", t), 0.0, ALU.add, ALU.min), al_read)
                    S(dve.tensor_tensor(la, tq(3)[:, 0:T], la, ALU.subtract))
                    S(dve.tensor_tensor_scan(cs, parts["reset32"], la[:, 0:SEQ], 0.0, ALU.mult, ALU.add))
                    c32 = cs.rearrange("p (c q) -> p c q", q=32)
                    S(dve.tensor_tensor(to_end.rearrange("p (c q) -> p c q", q=32),
                                        c32[:, :, 31:32].broadcast_to([P, 16, 32]), c32, ALU.subtract), cs2_ready)

                def gla_ready(t):
                    dve.wait_ge(ex2_ready.sem, ex2_ready.at(t + 1))
                    dve.wait_ge(evac.sem, evac.at(12 + t))
                    S(dve.tensor_copy(gdec[:, t, :], tq(3)[:, 31:SEQ:32]))
                    S(dve.tensor_tensor(KN(t), kt(t)[:, 0:SEQ], tq(2)[:, 0:SEQ], ALU.mult))
                    S(dve.tensor_tensor(kt(t)[:, 0:SEQ], kt(t)[:, 0:SEQ], tq(1)[:, 0:SEQ], ALU.mult))
                    S(dve.scalar_tensor_tensor(out=qt(t)[:, 0:SEQ], in0=qt(t)[:, 0:SEQ], scalar=0.125,
                                               in1=tq(3)[:, 0:SEQ], op0=ALU.mult, op1=ALU.mult))
                    S(dve.tensor_scalar(qt(t)[:, SEQ:T], qt(t)[:, SEQ:T], 0.125, None, ALU.mult), gla_read)

                for n in range(4):
                    conv(n)
                for n in range(4, 8):
                    conv(n)
                decay(0)
                gla_ready(0)
                decay(1)
                gla_ready(1)
        end_of_block()

        NC = SEQ // P
        BT0, CT0 = 4, 6
        XD = B[:, 0:2048].rearrange("p (c h q) -> p c h q", c=NC, h=8)
        WX = B[:, 2048:4096].rearrange("p (c h q) -> p c h q", c=NC, h=8)
        BTt = B[:, 4096:5120].rearrange("p (g c n) -> p g c n", g=2, c=NC)
        CB = B[:, 5120:6144].rearrange("p (g c n) -> p g c n", g=2, c=NC)
        ST = B[:, 6144:8192].rearrange("p (c h q) -> p c h q", c=NC, h=8)
        EB = lambda n: B[:, 8192 + 512 * (n % 2):8704 + 512 * (n % 2)]
        SG2 = lambda n: B[:, 9216 + 512 * (n % 2):9728 + 512 * (n % 2)]
        CE = lambda n: B[:, 10240 + 512 * (n % 2):10752 + 512 * (n % 2)]
        c4 = lambda ap: ap.rearrange("p (c n) -> p c n", c=NC)
        names = ("x_tr", "xd", "b_tr", "b_cp", "cb_mm", "cb_cp", "t_tr", "t_cp", "end_mm", "end_ex", "wx", "s_mm",
                 "s_up", "bc", "eb", "dif", "seg", "m", "y_mm", "y_cp", "smp_mm", "smp_cp")
        q = {n: signal("ssd_" + n) for n in names}

        def wq(e, name, n):
            e.wait_ge(q[name].sem, q[name].at(n))

        def head_y(pe, n):
            t, hh = n // 2, n % 2
            wq(pe, "m", n + 1)
            wq(pe, "s_up", NC)
            if n >= 4:
                wq(pe, "y_cp", n // 2 - 1)
            bank = 512 * (t % 2)
            for c in range(NC):
                dst = ps[2][64 * hh:64 * hh + 64, bank + c * P:bank + (c + 1) * P]
                mm = pe.matmul(dst, XD[:, c, n, :], SG2(n)[:, c * P:(c + 1) * P], start=True, stop=c == 0)
                if c:
                    mm = pe.matmul(dst, ST[:, c - 1, n, :], CE(n)[:, c * P:(c + 1) * P], start=False, stop=True)
            q["y_mm"].on(mm)

        with nc.Block() as block:
            @block.sync
            def _(sp):
                st_in.on(sp.dma_start(u_sb[:, 0:4096], i["s_ssd"]), 16)

            @block.tensor
            def _(pe):
                for n, src in enumerate((cum, dtr)):
                    for c in range(NC):
                        mm = pe.transpose(ps[3][:, 32 * n + 8 * c:32 * n + 8 * c + 8], src[:, c * P:(c + 1) * P],
                                          ident[0:8, 0:8])
                q["t_tr"].on(mm)
                for c in range(NC):
                    if c >= 2:
                        wq(pe, "xd", c - 1)
                    for t in range(4):
                        mm = pe.transpose(ps[0][:, 512 * (c % 2) + t * P:512 * (c % 2) + (t + 1) * P],
                                          xa(t)[:, c * P:(c + 1) * P], ident)
                    q["x_tr"].on(mm)
                for gq in range(2):
                    for c in range(NC):
                        mm = pe.transpose(ps[1][:, 512 * gq + c * P:512 * gq + (c + 1) * P],
                                          xa(BT0 + gq)[:, c * P:(c + 1) * P], ident)
                q["b_tr"].on(mm)
                for gq in range(2):
                    for c in range(NC):
                        mm = pe.matmul(ps[2][:, 512 * gq + c * P:512 * gq + (c + 1) * P],
                                       xa(BT0 + gq)[:, c * P:(c + 1) * P], xa(CT0 + gq)[:, c * P:(c + 1) * P],
                                       start=True, stop=True)
                q["cb_mm"].on(mm)
                wq(pe, "t_cp", 2)
                q["end_mm"].on(pe.matmul(ps[3][:, 64:96], parts["last"], cumT, start=True, stop=True))
                wq(pe, "end_ex", 2)
                for n, src in enumerate((las8, dtr[:, SEQ:T])):
                    for t in range(4):
                        mm = pe.matmul(ps[3][:, 512 + 32 * n + 8 * t:512 + 32 * n + 8 * t + 8], selp(t), src,
                                       start=True, stop=True)
                q["smp_mm"].on(mm)
                wq(pe, "b_cp", 1)
                for c in range(NC):
                    wq(pe, "wx", c + 2)
                    if c >= 2:
                        wq(pe, "s_up", c - 1)
                    elif c == 0:
                        wq(pe, "xd", NC)
                    for gq in range(2):
                        mm = pe.matmul(ps[0][:, 512 * (c % 2) + 256 * gq:512 * (c % 2) + 256 * gq + 256],
                                       BTt[:, gq, c, :], B[:, 2048 + 512 * c + 256 * gq:2048 + 512 * c + 256 * gq + 256],
                                       start=True, stop=True)
                    q["s_mm"].on(mm)
                wq(pe, "cb_cp", 1)
                wq(pe, "smp_cp", 1)
                for n in range(8):
                    t, hh, gq = n // 2, n % 2, n // 4
                    if n >= 2:
                        wq(pe, "seg", n - 1)
                        wq(pe, "eb", n - 1)
                        wq(pe, "dif", n - 1)
                    q["bc"].on(pe.matmul(ps[1][:, 512 * (n % 2):512 * (n % 2) + 512], sel8(n), cum, start=True, stop=True))
                    if n == 0:
                        continue
                    head_y(pe, n - 1)
                head_y(pe, 7)

            @block.scalar
            def _(act):
                S = Serial(act, act_step)
                wq(act, "t_tr", 1)
                S(act.activation(cumT, ps[3][:, 0:32], ACT.Copy), q["t_cp"])
                S(act.activation(dtT, ps[3][:, 32:64], ACT.Copy), q["t_cp"])
                wq(act, "b_tr", 1)
                S(act.activation(B[:, 4096:5120], ps[1][:, :], ACT.Copy), q["b_cp"])
                wq(act, "cb_mm", 1)
                S(act.activation(B[:, 5120:6144], ps[2][:, :], ACT.Copy), q["cb_cp"])
                wq(act, "end_mm", 1)
                S(act.activation(cend, ps[3][:, 64:96], ACT.Copy), q["end_ex"])
                S(act.activation(ecend, ps[3][:, 64:96], ACT.Exp), q["end_ex"])
                wq(act, "wx", 1)
                S(act.activation(wend, wend, ACT.Exp), q["end_ex"])
                wq(act, "smp_mm", 1)
                S(act.activation(small[:, 196:228], ps[3][:, 512:544], ACT.Exp))
                S(act.activation(small[:, 164:196], ps[3][:, 544:576], ACT.Copy), q["smp_cp"])
                for n in range(8):
                    wq(act, "bc", n + 1)
                    if n >= 2:
                        wq(act, "m", n - 1)
                    q["eb"].on(act.activation(EB(n), ps[1][:, 512 * (n % 2):512 * (n % 2) + 512], ACT.Exp))
                    wq(act, "dif", n + 1)
                    q["seg"].on(act.activation(SG2(n), SG2(n), ACT.Exp))

            @block.vector
            def _(dve):
                S = Serial(dve, dve_step)
                wq(dve, "t_cp", 2)
                for c in range(NC):
                    wq(dve, "x_tr", c + 1)
                    S(dve.tensor_tensor(XD[:, c], ps[0][:, 512 * (c % 2):512 * (c % 2) + 512].rearrange("p (h q) -> p h q", h=8),
                                        dtT[:, 8 * c:8 * c + 8].unsqueeze(2).broadcast_to([P, 8, 64]), ALU.mult), q["xd"])
                wq(dve, "end_ex", 2)
                S(dve.tensor_tensor(wend, cend, cumT, ALU.subtract), q["wx"])
                wq(dve, "end_ex", 3)
                for c in range(NC):
                    S(dve.tensor_tensor(WX[:, c], XD[:, c], wend[:, 8 * c:8 * c + 8].unsqueeze(2).broadcast_to([P, 8, 64]),
                                        ALU.mult), q["wx"] if c < 3 else q["wx"])
                for c in range(NC):
                    wq(dve, "s_mm", c + 1)
                    inc = ps[0][:, 512 * (c % 2):512 * (c % 2) + 512].rearrange("p (h q) -> p h q", h=8)
                    if c:
                        S(dve.tensor_tensor(ST[:, c], ST[:, c - 1], ecend[:, 8 * c:8 * c + 8].unsqueeze(2).broadcast_to([P, 8, 64]), ALU.mult))
                        S(dve.tensor_tensor(ST[:, c], ST[:, c], inc, ALU.add), q["s_up"])
                    else:
                        S(dve.tensor_copy(ST[:, c], inc), q["s_up"])
                for n in range(9):
                    if n < 8:
                        t, gq = n // 2, n // 4
                        bank = ps[1][:, 512 * (n % 2):512 * (n % 2) + 512]
                        wq(dve, "eb", n + 1)
                        if n >= 2:
                            wq(dve, "y_mm", n - 1)
                        for c in range(NC):
                            ins = dve.scalar_tensor_tensor(
                                out=SG2(n)[:, c * P:(c + 1) * P], in0=bank[:, c * P:(c + 1) * P],
                                scalar=cumT[:, 8 * c + n:8 * c + n + 1], in1=parts["ssdmask"], op0=ALU.subtract, op1=ALU.min)
                            S(ins, q["dif"] if c == NC - 1 else None)
                        S(dve.tensor_tensor(CE(n), EB(n), xa(CT0 + gq)[:, 0:SEQ], ALU.mult))
                        wq(dve, "seg", n + 1)
                        S(dve.tensor_tensor(SG2(n), SG2(n), B[:, 5120 + 512 * gq:5632 + 512 * gq], ALU.mult), q["m"])
                    if n >= 2 and n % 2 == 0:
                        t = n // 2 - 1
                        wq(dve, "y_mm", n)
                        S(dve.scalar_tensor_tensor(out=xa(t)[:, 0:SEQ], in0=xa(t)[:, 0:SEQ], scalar=v("ssd_d", t),
                                                   in1=ps[2][:, 512 * (t % 2):512 * (t % 2) + 512],
                                                   op0=ALU.mult, op1=ALU.add), q["y_cp"])
        end_of_block()

        SS = u_sb[:, 0:4096]
        ss_b = SS.rearrange("p (b t n) -> p b t n", b=NS, t=4)
        SDG, ST2 = B[:, 0:2048], B[:, 2048:4096]
        srow = small[:, 300:332].rearrange("p (b t) -> p b t", b=NS)
        dtx = small[:, 332:364].rearrange("p (t b) -> p t b", t=4)
        with nc.Block() as block:
            @block.sync
            def _(sp):
                stored.on(sp.dma_start(o["ssd_p"], B[:, 6144 + 3 * 512:8192]), 16)
                stored.on(sp.dma_start(o["cd_small"], stage[:, 192:408]), 16)
                sp.wait_ge(dve_step.sem, dve_step.at(1))
                stored.on(sp.dma_start(o["ssd_s"], SS), 16)
                sp.wait_ge(stored.sem, stored.count)

            @block.tensor
            def _(pe):
                for n in range(2):
                    pe.wait_ge(dg_ready.sem, dg_ready.at(n + 1))
                    if n:
                        pe.wait_ge(bc_read.sem, bc_read.at(n))
                    for r in range(4):
                        mm = pe.matmul(ps[r // 2][:, 512 * (r % 2):512 * (r % 2) + 512], ones,
                                       SDG[:, 512 * r:512 * r + 512], start=True, stop=True)
                    bc_mm.on(mm)

            @block.vector
            def _(dve):
                S = Serial(dve, norm_b)
                dve.wait_ge(st_in.sem, st_in.count)
                for n, tile0 in enumerate((BT0, CT0)):
                    for gq in range(2):
                        S(dve.tensor_tensor(SDG[:, 1024 * gq:1024 * gq + 1024].rearrange("p (b n) -> p b n", b=NS),
                                            ident.unsqueeze(1).broadcast_to([P, NS, P]),
                                            xa(tile0 + gq)[:, SEQ:T].unsqueeze(2).broadcast_to([P, NS, P]), ALU.mult),
                          dg_ready if gq else None)
                    if n == 0:
                        S(dve.tensor_tensor(dtx, dts, A[:, 0:4 * PAD].rearrange("p (t c) -> p t c", t=4)[:, :, SEQ:T], ALU.mult))
                        for b in range(2):
                            c = slice(4 * b, 4 * b + 4)
                            S(dve.tensor_tensor(SS[:, 2048 * b:2048 * b + 2048].rearrange("p (b t n) -> p b t n", b=4, t=4),
                                                SS[:, 2048 * b:2048 * b + 2048].rearrange("p (b t n) -> p b t n", b=4, t=4),
                                                las[:, :, c].rearrange("p t b -> p b t").unsqueeze(3).broadcast_to([P, 4, 4, P]), ALU.mult))
                    dve.wait_ge(bc_mm.sem, bc_mm.at(n + 1))
                    for t in range(4):
                        bc = ps[t // 2][:, :].rearrange("p (b n) -> p b n", b=NS)
                        tmp = ST2[:, 0:1024].rearrange("p (b n) -> p b n", b=NS)
                        if n == 0:
                            S(dve.tensor_tensor(tmp, bc, dtx[:, t, :].unsqueeze(2).broadcast_to([P, NS, P]), ALU.mult),
                              bc_read if t == 3 else None)
                            S(dve.tensor_tensor(ss_b[:, :, t, :], ss_b[:, :, t, :], tmp, ALU.add), dve_step if t == 3 else None)
                        else:
                            S(dve.tensor_tensor(tmp, bc, ss_b[:, :, t, :], ALU.mult), bc_read if t == 3 else None)
                            S(dve.tensor_reduce(srow[:, :, t], tmp, AX.X, ALU.add))
                for t in range(4):
                    S(dve.scalar_tensor_tensor(out=xa(t)[:, SEQ:T], in0=xa(t)[:, SEQ:T], scalar=v("ssd_d", t),
                                               in1=srow[:, :, t], op0=ALU.mult, op1=ALU.add))
        end_of_block()

        VT = B[:, 0:2048].rearrange("p (c h n) -> p c h n", c=NC, h=4)
        KT = B[:, 2048:3072].rearrange("p (c t n) -> p c t n", c=NC, t=2)
        ATT = lambda h: B[:, 3072 + 512 * h:3584 + 512 * h]
        GS = B[:, 5120:9216].rearrange("p (t s n) -> p t s n", t=2, s=16)
        bank = lambda n: ps[n // 2][:, 512 * (n % 2):512 * (n % 2) + 512]
        ATT_BANK, O_BANK = (6, 7, 4, 5), (0, 1, 2, 3)
        v_tr, v_cp, k_tr, k_cp, att_mm, att_cp, inc_mm, state_up, o_mm = (
            q["x_tr"], q["xd"], q["b_tr"], q["b_cp"], q["cb_mm"], q["cb_cp"], q["s_mm"], q["s_up"], q["y_mm"])
        with nc.Block() as block:
            @block.sync
            def _(sp):
                st_in.on(sp.dma_start(u_sb[:, 0:2048], i["s_gla"]), 16)

            @block.tensor
            def _(pe):
                for c in range(NC):
                    for h in range(4):
                        mm = pe.transpose(bank(c)[:, h * P:(h + 1) * P], vt(h)[:, c * P:(c + 1) * P], ident)
                    v_tr.on(mm)
                for t in range(2):
                    for c in range(NC):
                        mm = pe.transpose(ps[2][:, (2 * c + t) * P:(2 * c + t + 1) * P], KN(t)[:, c * P:(c + 1) * P], ident)
                k_tr.on(mm)
                for h in range(4):
                    t, r = h // 2, slice(64 * (h % 2), 64 * (h % 2) + 64)
                    if h >= 2:
                        pe.wait_ge(k_cp.sem, k_cp.at(1))
                    for c in range(NC):
                        cc = slice(c * P, (c + 1) * P)
                        mm = pe.matmul(bank(ATT_BANK[h])[:, cc], kt(t)[r, cc], qt(t)[r, cc], start=True, stop=True)
                    att_mm.on(mm)
                pe.wait_ge(v_cp.sem, v_cp.at(4))
                for t in range(2):
                    if t:
                        pe.wait_ge(att_cp.sem, att_cp.at(4))
                    for s in range(16):
                        c, r = s // 4, slice(32 * (s % 4), 32 * (s % 4) + 32)
                        for hh in range(2):
                            mm = pe.matmul(bank(4 * t + s % 4)[64 * hh:64 * hh + 64, c * P:(c + 1) * P],
                                           KT[r, c, t, 64 * hh:64 * hh + 64], VT[r, c, 2 * t + hh, :], start=True, stop=True)
                    inc_mm.on(mm)
                for h in range(4):
                    t, r = h // 2, slice(64 * (h % 2), 64 * (h % 2) + 64)
                    pe.wait_ge(state_up.sem, state_up.at(t + 1))
                    for c in range(NC):
                        dst = bank(O_BANK[h])
                        pe.matmul(dst[:, c * P:(c + 1) * P], VT[:, c, h, :], ATT(h)[:, c * P:(c + 1) * P],
                                  start=True, stop=False)
                        for s in range(4 * c, 4 * c + 4):
                            if s:
                                mm = pe.matmul(dst[:, 32 * s:32 * s + 32], GS[r, t, s - 1, :], qt(t)[r, 32 * s:32 * s + 32],
                                               start=False, stop=s % 4 == 3)
                    o_mm.on(mm)

            @block.scalar
            def _(act):
                for c in range(NC):
                    act.wait_ge(v_tr.sem, v_tr.at(c + 1))
                    v_cp.on(act.activation(B[:, 512 * c:512 * c + 512], bank(c), ACT.Copy))
                for h in range(4):
                    act.wait_ge(o_mm.sem, o_mm.at(h + 1))
                    act_step.on(act.activation(vt(h)[:, 0:SEQ], bank(O_BANK[h]), ACT.Copy))

            @block.vector
            def _(dve):
                S = Serial(dve, dve_step)
                dve.wait_ge(k_tr.sem, k_tr.at(1))
                k_cp.on(dve.tensor_copy(B[:, 2048:3072], ps[2][:, :]))
                for h in range(4):
                    dve.wait_ge(att_mm.sem, att_mm.at(h + 1))
                    att_cp.on(dve.tensor_tensor(c4(ATT(h)), c4(bank(ATT_BANK[h])),
                                                parts["glamask"].unsqueeze(1).broadcast_to([P, NC, P]), ALU.mult))
                for t in range(2):
                    for s in range(16):
                        inc = bank(4 * t + s % 4)[:, (s // 4) * P:(s // 4 + 1) * P]
                        if s == 0:
                            dve.wait_ge(inc_mm.sem, inc_mm.at(t + 1))
                        if s == 0:
                            S(dve.tensor_copy(GS[:, t, 0, :], inc))
                        else:
                            S(dve.scalar_tensor_tensor(out=GS[:, t, s, :], in0=GS[:, t, s - 1, :], scalar=gdec[:, t, s:s + 1],
                                                       in1=inc, op0=ALU.mult, op1=ALU.add), state_up if s == 15 else None)
        end_of_block()

        SG = u_sb[:, 0:2048]
        sg4 = SG.rearrange("p (b t n) -> p b t n", b=NS, t=2)
        VD = lambda hh: B[:, 2048 * hh:2048 * hh + 2048]
        KV = u_sb[:, 2048:4096].rearrange("p (b t n) -> p b t n", b=NS, t=2)
        vk = lambda t0, n: A[:, G0 + t0 * T:G0 + (t0 + n) * T].rearrange("p (t c) -> p t c", c=T)
        per_b = lambda ap: ap.rearrange("p t b -> p b t").unsqueeze(3).broadcast_to([P, NS, 2, P])
        with nc.Block() as block:
            @block.sync
            def _(sp):
                for t in range(2):
                    stored.on(sp.dma_start(o["gla_p"][:, t * P:(t + 1) * P], GS[:, t, 15, :]), 16)
                sp.wait_ge(dve_step.sem, dve_step.at(1))
                stored.on(sp.dma_start(o["gla_s"], SG), 16)
                sp.wait_ge(stored.sem, stored.count)

            @block.tensor
            def _(pe):
                for hh in range(2):
                    pe.wait_ge(dg_ready.sem, dg_ready.at(hh + 1))
                    for r in range(4):
                        mm = pe.matmul(bank(r)[64 * hh:64 * hh + 64, :], ones[:, 0:64], VD(hh)[:, 512 * r:512 * r + 512],
                                       start=True, stop=True)
                    bc_mm.on(mm)
                pe.wait_ge(dve_step.sem, dve_step.at(1))
                for hh in range(2):
                    r = slice(64 * hh, 64 * hh + 64)
                    for t in range(2):
                        for b in range(NS):
                            mm = pe.matmul(bank(4 + hh)[:, NS * t + b:NS * t + b + 1], sg4[r, b, t, :],
                                           qt(t)[r, SEQ + b:SEQ + b + 1], start=True, stop=True)
                o_mm.on(mm)

            @block.vector
            def _(dve):
                S = Serial(dve, norm_b)
                for hh in range(2):
                    for t in range(2):
                        S(dve.tensor_tensor(VD(hh).rearrange("p (b t n) -> p b t n", b=NS, t=2)[:, :, t, :],
                                            ident.unsqueeze(1).broadcast_to([P, NS, P]),
                                            vt(2 * t + hh)[:, SEQ:T].unsqueeze(2).broadcast_to([P, NS, P]), ALU.mult),
                          dg_ready if t else None)
                dve.wait_ge(st_in.sem, st_in.count)
                S(dve.tensor_tensor(sg4, sg4, per_b(gds), ALU.mult))
                dve.wait_ge(bc_mm.sem, bc_mm.at(2))
                for n in range(2):
                    bs = slice(4 * n, 4 * n + 4)
                    S(dve.tensor_tensor(KV[:, bs], ps[n][:, :].rearrange("p (b t n) -> p b t n", b=4, t=2),
                                        per_b(vk(2, 2)[:, :, SEQ:T])[:, bs], ALU.mult))
                S(dve.tensor_tensor(sg4, sg4, KV, ALU.add), dve_step)
                dve.wait_ge(o_mm.sem, o_mm.at(1))
                for h in range(4):
                    t, hh = h // 2, h % 2
                    S(dve.tensor_copy(vt(h)[:, SEQ:T], bank(4 + hh)[:, NS * t:NS * t + NS]))
        end_of_block()

        SQ = lambda n: B[:, n * T:n * T + T]
        RT = lambda n: B[:, (8 + n) * T:(9 + n) * T]
        yz, ysq, ysum, yroot = q["bc"], q["eb"], q["dif"], q["seg"]
        with nc.Block() as block:
            @block.tensor
            def _(pe):
                for n in range(8):
                    pe.wait_ge(ysq.sem, ysq.at(n + 1))
                    if n == 7:
                        pe.wait_ge(yroot.sem, yroot.at(1))
                    mm = product(pe, pt(0) if n < 4 else pt(n - 3), ones, 1, lambda k: SQ(n), first=n == 0 or n > 3,
                                 last=n >= 3)
                    if n >= 3:
                        ysum.on(mm)

            @block.scalar
            def _(act):
                for n in range(8):
                    if n < 4:
                        act.wait_ge(yz.sem, yz.at(n + 1))
                    ysq.on(act.activation(SQ(n), xa(n)[:, 0:T] if n < 4 else vt(n - 4), ACT.Square))
                for n in range(5):
                    act.wait_ge(ysum.sem, ysum.at(n + 1))
                    yroot.on(act.activation(RT(n), pt(n), ACT.Sqrt, bias=small[:, 0:1], scale=1.0 / (512 if n == 0 else P)))

            @block.vector
            def _(dve):
                S = Serial(dve, dve_step)
                for t in range(4):
                    yz.on(dve.tensor_tensor(xa(t)[:, 0:T], xa(t)[:, 0:T], zt(t), ALU.mult))
                dve.wait_ge(ysq.sem, ysq.at(4))
                for n in range(5):
                    dve.wait_ge(yroot.sem, yroot.at(n + 1))
                    S(dve.reciprocal(RT(n), RT(n)))
                    if n == 0:
                        for t in range(4):
                            dve_step.on(dve.scalar_tensor_tensor(out=xa(t)[:, 0:T], in0=xa(t)[:, 0:T],
                                                                 scalar=v("ssd_norm", t), in1=RT(0), op0=ALU.mult, op1=ALU.mult))
                    else:
                        if n == 1:
                            dve.wait_ge(ysq.sem, ysq.at(8))
                        o_h = vt(n - 1)
                        S(dve.scalar_tensor_tensor(out=o_h, in0=o_h, scalar=v("gla_norm"), in1=RT(n), op0=ALU.mult, op1=ALU.mult))
                        S(dve.tensor_tensor(o_h, o_h, gt(n - 1), ALU.mult))
        end_of_block()

        out_block(Q_OUT1, "w_out_cd", lambda k: xa(k)[:, 0:T] if k < 4 else vt(k - 4), None)

        NT = 5
        tile_w = lambda tt: P if tt < 4 else NS
        e3 = lambda n: small[:, 300 + 40 * n:340 + 40 * n]
        r5 = lambda n: small[:, 580 + 5 * n:585 + 5 * n]
        by_e = lambda ap: ap.rearrange("p (t e) -> p t e", e=NEXP)
        logit, prob, first1, first2, rest, scan = [e3(n) for n in range(6)]
        top, tot, top2 = r5(0), r5(1), r5(2)
        row8 = lambda ap: ap.unsqueeze(2).broadcast_to([P, NT, NEXP])
        token_pos = [small[:, 540 + 5 * n:545 + 5 * n] for n in range(2)]
        slot_id = small[:, 550:551]
        n_e, blocks, start128, end_e = [small[0:8, 551 + n:552 + n] for n in range(4)]
        block_cmp, block5 = small[0:8, 560:576], small[0:8, 600:605]
        U_TOK = lambda tt: A[:, 1024 * tt:1024 * (tt + 1)]
        place = [A[:, 5120 + n * T:5120 + (n + 1) * T] for n in range(2)]
        gate = [A[:, 5120 + (2 + n) * T:5120 + (3 + n) * T] for n in range(2)]
        GK = A[:, 7200:7200 + T]
        GT1 = A[:, 7720:7720 + T]
        XG = A[:, 8240:8240 + 1024]
        YS = A[:, 9264:9264 + 1024]
        PK = A[:, 10288:10288 + NT * P]
        HK = lambda f: B[:, f * P:(f + 1) * P]
        TMPH = lambda m: C[:, 128 * (m % 2):128 * (m % 2) + 128]
        row_t = lambda n: B[0:8, 2048 + n * T:2048 + (n + 1) * T]
        F1T, F2T, GTT, FT, CUM, POS, R0, R1, R2, R3 = [row_t(n) for n in range(10)]
        (rt_mm, rt_exp, rt_sub, rt_gate, rt_tr, rt_cp, rt_bc, u_tr, u_cp, nb_ready, bs_mm, rows_ready, ek_mm, pk_ready,
         xg_mm, xg_cp, y_cp, g_ready, sc_mm) = (q[n] for n in (
             "bc", "eb", "dif", "seg", "m", "y_mm", "y_cp", "x_tr", "xd", "b_tr", "b_cp", "cb_mm", "cb_cp", "t_tr",
             "t_cp", "end_mm", "end_ex", "wx", "s_mm"))

        def build_places(dve, S, last=None):
            for tt in range(NT):
                w = tile_w(tt)
                dst = PK[0:w, tt * P:(tt + 1) * P]
                S(dve.tensor_scalar(dst, parts["iota"][0:w, :], token_pos[0][0:w, tt:tt + 1], None, ALU.is_equal))
                S(dve.scalar_tensor_tensor(out=dst, in0=parts["iota"][0:w, :], scalar=token_pos[1][0:w, tt:tt + 1],
                                           in1=dst, op0=ALU.is_equal, op1=ALU.add), last if tt == NT - 1 else None)

        with nc.Block() as block:
            @block.tensor
            def _(pe):
                norm_pe(pe)
                pe.wait_ge(u_ready.sem, u_ready.at(KD))
                for tt in range(NT):
                    w = tile_w(tt)
                    for k in range(KD):
                        mm = pe.matmul(ps[0][0:w, 8 * tt:8 * tt + 8], u3[:, k, tt * P:tt * P + w],
                                       parts["router"][:, 8 * k:8 * k + 8], start=k == 0, stop=k == KD - 1)
                rt_mm.on(mm)
                for tt in range(NT):
                    w = tile_w(tt)
                    if tt >= 2:
                        pe.wait_ge(u_cp.sem, u_cp.at(tt - 1))
                    for k in range(KD):
                        mm = pe.transpose(ps[2 + tt % 2][0:w, k * P:(k + 1) * P], u3[:, k, tt * P:tt * P + w], ident)
                    u_tr.on(mm)
                pe.wait_ge(rt_gate.sem, rt_gate.at(1))
                pe.wait_ge(u_cp.sem, u_cp.at(NT))
                for n, src in enumerate((first1, first2, prob)):
                    for tt in range(NT):
                        w = tile_w(tt)
                        mm = pe.transpose(ps[1 + n][0:8, tt * P:tt * P + w], src[0:w, 8 * tt:8 * tt + 8], ident[0:w, 0:w])
                rt_tr.on(mm)
                pe.wait_ge(nb_ready.sem, nb_ready.at(1))
                bs_mm.on(pe.matmul(ps[0][0:8, 40:41], parts["before"][0:8, :], blocks, start=True, stop=True))
                pe.wait_ge(nb_ready.sem, nb_ready.at(2))
                pe.matmul(ps[0][0:1, 64:80], ones[0:8, 0:1], block_cmp, start=True, stop=True)
                pe.matmul(ps[0][0:1, 80:81], ones[0:8, 0:1], blocks, start=True, stop=True)
                pe.wait_ge(rows_ready.sem, rows_ready.at(1))
                for n, row in enumerate((R0, R1)):
                    for tt in range(NT):
                        w = tile_w(tt)
                        mm = pe.matmul(ps[0][0:w, 96 + 5 * n + tt:97 + 5 * n + tt], row[:, tt * P:tt * P + w],
                                       ones[0:8, 0:1], start=True, stop=True)
                ek_mm.on(mm)
                for n, row in enumerate((R0, R1, R2, R3)):
                    if n == 3:
                        pe.wait_ge(rt_bc.sem, rt_bc.at(1))
                    rt_cp.on(product(pe, pt(1 + n % 3), ones[0:8, :], 1, lambda k: row))

            @block.scalar
            def _(act):
                norm_act(act)
                for tt in range(NT):
                    w = tile_w(tt)
                    if tt == 1:
                        act.wait_ge(rt_sub.sem, rt_sub.at(1))
                        rt_exp.on(act.activation(prob, logit, ACT.Exp))
                    act.wait_ge(u_tr.sem, u_tr.at(tt + 1))
                    u_cp.on(act.activation(U_TOK(tt)[0:w, :], ps[2 + tt % 2][0:w, :], ACT.Copy))
                for n, dst in enumerate(place + gate):
                    act.wait_ge(rt_cp.sem, rt_cp.at(n + 1))
                    rt_bc.on(act.activation(dst, pt(1 + n % 3), ACT.Copy))

            @block.vector
            def _(dve):
                S = Serial(dve, dve_step)

                def first_of(dst, src, peak):
                    S(dve.tensor_tensor(by_e(dst), by_e(src), row8(peak), ALU.is_equal))
                    S(dve.tensor_tensor_scan(scan, parts["reset8"], dst, 0.0, ALU.mult, ALU.add))
                    S(dve.scalar_tensor_tensor(out=dst, in0=scan, scalar=1.0, in1=dst, op0=ALU.is_equal, op1=ALU.mult))

                norm_dve(dve, "norm_ffn1")
                S(dve.memset(logit, 0.0))
                S(dve.memset(small[:, 540:550], 0.0))
                dve.wait_ge(rt_mm.sem, rt_mm.at(1))
                S(dve.tensor_copy(logit[:, 0:32], ps[0][:, 0:32]))
                S(dve.tensor_copy(logit[0:NS, 32:40], ps[0][0:NS, 32:40]))
                S(dve.tensor_reduce(top, by_e(logit), AX.X, ALU.max))
                S(dve.tensor_tensor(by_e(logit), by_e(logit), row8(top), ALU.subtract), rt_sub)
                dve.wait_ge(rt_exp.sem, rt_exp.at(1))
                S(dve.tensor_reduce(tot, by_e(prob), AX.X, ALU.add))
                S(dve.reciprocal(tot, tot))
                S(dve.tensor_tensor(by_e(prob), by_e(prob), row8(tot), ALU.mult))
                S(dve.tensor_reduce(top, by_e(prob), AX.X, ALU.max))
                first_of(first1, prob, top)
                S(dve.scalar_tensor_tensor(out=rest, in0=first1, scalar=-2.0, in1=prob, op0=ALU.mult, op1=ALU.add))
                S(dve.tensor_reduce(top2, by_e(rest), AX.X, ALU.max))
                first_of(first2, rest, top2)
                S(dve.tensor_tensor(tot, top, top2, ALU.add))
                S(dve.reciprocal(tot, tot))
                S(dve.tensor_tensor(by_e(prob), by_e(prob), row8(tot), ALU.mult), rt_gate)
                dve.wait_ge(rt_tr.sem, rt_tr.at(1))
                for n, dst in enumerate((F1T, F2T, GTT)):
                    S(dve.tensor_copy(dst, ps[1 + n][0:8, 0:T]))
                S(dve.tensor_tensor(FT, F1T, F2T, ALU.add))
                S(dve.tensor_tensor_scan(CUM, FT, FT, 0.0, ALU.add, ALU.max))
                S(dve.tensor_copy(n_e, CUM[:, T - 1:T]))
                S(dve.tensor_scalar(block5, parts["iota"][0:8, 0:5], float(P), n_e, ALU.mult, ALU.is_lt))
                S(dve.tensor_reduce(blocks, block5, AX.X, ALU.add), nb_ready)
                dve.wait_ge(bs_mm.sem, bs_mm.at(1))
                S(dve.tensor_tensor(end_e, ps[0][0:8, 40:41], blocks, ALU.add))
                S(dve.tensor_scalar(start128, ps[0][0:8, 40:41], float(P), None, ALU.mult))
                S(dve.tensor_scalar(block_cmp, parts["iota"][0:8, 0:MAXB], end_e, None, ALU.is_ge), nb_ready)
                S(dve.tensor_scalar(POS, CUM, start128, -1.0, ALU.add, ALU.add))
                S(dve.tensor_tensor(R0, F1T, POS, ALU.mult))
                S(dve.tensor_tensor(R1, F2T, POS, ALU.mult))
                S(dve.tensor_tensor(R2, F1T, GTT, ALU.mult))
                S(dve.tensor_tensor(R3, F2T, GTT, ALU.mult), rows_ready)
                S(dve.tensor_copy(slot_id, parts["index"]))
                dve.wait_ge(ek_mm.sem, ek_mm.at(1))
                S(dve.tensor_scalar(expert_of[0:1, 0:MAXB], ps[0][0:1, 64:80], float(NEXP - 1), None, ALU.min))
                S(dve.tensor_copy(expert_of[0:1, MAXB:MAXB + 1], ps[0][0:1, 80:81]))
                for n in range(2):
                    S(dve.tensor_copy(token_pos[n][:, 0:4], ps[0][:, 96 + 5 * n:100 + 5 * n]))
                    S(dve.tensor_copy(token_pos[n][0:NS, 4:5], ps[0][0:NS, 100 + 5 * n:101 + 5 * n]))
                build_places(dve, S, pk_ready)
        end_of_block()

        def moe_src(n, e):
            if n < 2 * KE:
                return i["w_moe_gu"][bass.ds(e * (2 * KE * P) + n * P, P), :]
            return i["w_moe_dn"][bass.ds(e * (KD * P) + (n - 2 * KE) * P, P), :]

        scatter_pt = lambda m: pt((0, 1, 3)[m % 3])
        hid_psum = lambda m, s: ps[m % 2][:, 512 * s:512 * s + P]
        N_PK = 2 * NT + 4
        def skip(e, counts):
            for s, n in counts:
                e.sem_inc(s.sem, n)

        with nc.Block() as block:
            @block.sync
            def _(sp):
                used = sp.value_load(expert_of[0:1, MAXB:MAXB + 1], min_val=1, max_val=MAXB)
                with sp.Fori(0, MAXB) as k:
                    with sp.If(k < used):
                        e = sp.value_load(expert_of[0:1, bass.ds(k, 1)], min_val=0, max_val=NEXP - 1)
                        for n in range(PER_E):
                            load_slab(sp, Q_MOE + n, moe_src(n, e), (k, PER_E))
                    with sp.Else():
                        sp.wait_ge(slab_used.sem, Q_MOE + PER_E * k)
                        skip(sp, [(s, 16 * (PER_E // RING)) for s in slab_in])
                prefetch(sp, Q_PLE1, "w_ple1")

            @block.tensor
            def _(pe):
                used = pe.value_load(expert_of[0:1, MAXB:MAXB + 1], min_val=1, max_val=MAXB)
                with pe.Fori(0, MAXB) as k:
                    with pe.If(k < used):
                        turn = (k, PER_E)
                        pe.wait_ge(pk_ready.sem, pk_ready.at(0) + k)
                        pe.wait_ge(evac.sem, evac.at(0) + KD * k)
                        for m in range(KD):
                            for tt in range(NT):
                                w = tile_w(tt)
                                mm = pe.matmul(ps[3][:, m * P:(m + 1) * P], U_TOK(tt)[0:w, m * P:(m + 1) * P],
                                               PK[0:w, tt * P:(tt + 1) * P], start=tt == 0, stop=tt == NT - 1)
                            if m % 4 == 3:
                                mm.then_inc(xg_mm.sem, 1)
                        for m in range(KE):
                            if m >= 2:
                                pe.wait_ge(hid_done.sem, hid_done.at(m - 1) + KE * k)
                            for s in range(2):
                                wait_slab(pe, Q_MOE + 2 * m + s, turn)
                                for f in range(KD):
                                    if m == 0 and s == 0 and f % 4 == 0:
                                        pe.wait_ge(xg_cp.sem, xg_cp.at(f // 4 + 1) + 2 * k)
                                    mm = pe.matmul(hid_psum(m, s), slot(Q_MOE + 2 * m + s)[:, f * P:(f + 1) * P],
                                                   XG[:, f * P:(f + 1) * P], start=f == 0, stop=f == KD - 1)
                                mm.then_inc(slab_used.sem, 1)
                        for m in range(KD):
                            wait_slab(pe, Q_MOE + 2 * KE + m, turn)
                            for f in range(KE):
                                if m == 0 and f in (0, KE - 1):
                                    pe.wait_ge(hid_done.sem, hid_done.at(KE - 1 if f == 0 else KE) + KE * k)
                                mm = pe.matmul(ps[2][:, m * P:(m + 1) * P], HK(f), slot(Q_MOE + 2 * KE + m)[:, f * P:(f + 1) * P],
                                               start=f == 0, stop=f == KE - 1)
                            mm.then_inc(slab_used.sem, 1)
                        pe.wait_ge(g_ready.sem, g_ready.at(1) + k)
                        for m in range(KD):
                            if m % 4 == 0:
                                pe.wait_ge(y_cp.sem, y_cp.at(m // 4 + 1) + 2 * k)
                            if m >= 3:
                                pe.wait_ge(evac.sem, evac.at(m - 2) + KD * k)
                            product(pe, scatter_pt(m), YS[:, m * P:(m + 1) * P], 1, lambda _: GK).then_inc(sc_mm.sem, 1)
                    with pe.Else():
                        pe.drain()
                        skip(pe, [(xg_mm, 2), (slab_used, PER_E), (sc_mm, KD)])

            @block.scalar
            def _(act):
                used = act.value_load(expert_of[0:1, MAXB:MAXB + 1], min_val=1, max_val=MAXB)
                with act.Fori(0, MAXB) as k:
                    with act.If(k < used):
                        for n in range(2):
                            act.wait_ge(xg_mm.sem, xg_mm.at(n + 1) + 2 * k)
                            act.activation(XG[:, 512 * n:512 * n + 512], ps[3][:, 512 * n:512 * n + 512],
                                           ACT.Copy).then_inc(xg_cp.sem, 1)
                        for m in range(KE):
                            act.wait_ge(slab_used.sem, Q_MOE + 2 * m + 1 + PER_E * k)
                            if m != 1:
                                act.wait_ge(hid_done.sem, hid_done.at(max(m - 1, 0)) + KE * k)
                            act.activation(TMPH(m), hid_psum(m, 0), ACT.Silu).then_inc(silu_done.sem, 1)
                        for n in range(2):
                            act.wait_ge(slab_used.sem, Q_MOE + 2 * KE + 4 * n + 4 + PER_E * k)
                            act.activation(YS[:, 512 * n:512 * n + 512], ps[2][:, 512 * n:512 * n + 512],
                                           ACT.Copy).then_inc(y_cp.sem, 1)
                    with act.Else():
                        act.drain()
                        skip(act, [(xg_cp, 2), (silu_done, KE), (y_cp, 2)])

            @block.vector
            def _(dve):
                used = dve.value_load(expert_of[0:1, MAXB:MAXB + 1], min_val=1, max_val=MAXB)
                with dve.Fori(0, MAXB) as k:
                    with dve.If(k < used):
                        step = [0]

                        def S(ins, signal=None):
                            if signal:
                                ins.then_inc(signal.sem, 1)
                                dve.wait_ge(signal.sem, signal.at(1) + k)
                            else:
                                step[0] += 1
                                ins.then_inc(dve_step.sem, 1)
                                dve.wait_ge(dve_step.sem, dve_step.at(step[0]) + N_PK * k)

                        S(dve.scalar_tensor_tensor(out=GK, in0=place[0], scalar=slot_id, in1=gate[0], op0=ALU.is_equal, op1=ALU.mult))
                        S(dve.scalar_tensor_tensor(out=GT1, in0=place[1], scalar=slot_id, in1=gate[1], op0=ALU.is_equal, op1=ALU.mult))
                        S(dve.tensor_tensor(GK, GK, GT1, ALU.add), g_ready)
                        S(dve.tensor_scalar(slot_id, slot_id, float(P), None, ALU.add))
                        for n in range(2):
                            S(dve.tensor_scalar(token_pos[n], token_pos[n], -float(P), None, ALU.add))
                        dve.wait_ge(xg_mm.sem, xg_mm.at(2) + 2 * k)
                        build_places(dve, S, pk_ready)
                        assert step[0] == N_PK
                        for m in range(KE):
                            dve.wait_ge(silu_done.sem, silu_done.at(m + 1) + KE * k)
                            dve.wait_ge(slab_used.sem, Q_MOE + 2 * m + 2 + PER_E * k)
                            dve.tensor_tensor(HK(m), TMPH(m), hid_psum(m, 1), ALU.mult).then_inc(hid_done.sem, 1)
                        for m in range(KD):
                            dve.wait_ge(sc_mm.sem, sc_mm.at(m + 1) + KD * k)
                            if m == 0:
                                dve.wait_ge(evac.sem, evac.at(0) + KD * k)
                            dve.tensor_tensor(h3[:, m, :], scatter_pt(m), h3[:, m, :], ALU.add).then_inc(evac.sem, 1)
                    with dve.Else():
                        dve.drain()
                        skip(dve, [(g_ready, 1), (dve_step, N_PK), (pk_ready, 1), (hid_done, KE), (evac, KD)])
        slab_used.add(MAXB * PER_E)
        for n in range(RING):
            slab_in[n].add(16 * (PER_E // RING) * MAXB)
        for s, n in ((silu_done, KE), (hid_done, KE), (dve_step, N_PK), (evac, KD), (sc_mm, KD), (g_ready, 1),
                     (pk_ready, 1), (y_cp, 2), (xg_cp, 2), (xg_mm, 2)):
            s.add(n * MAXB)
        end_of_block()

        square_block()
        ple_block(Q_PLE1, 1, None, "norm_ple1")
        with nc.Block() as block:
            @block.sync
            def _(sp):
                for n in range(4):
                    sp.wait_ge(u_ready.sem, u_ready.at(2 * n + 2))
                    stored.on(sp.dma_start(o["y"][:, 2 * T * n:2 * T * (n + 1)], u_sb[:, 2 * T * n:2 * T * (n + 1)]), 16)
                sp.wait_ge(stored.sem, stored.count)

            @block.tensor
            def _(pe):
                norm_pe(pe)

            @block.scalar
            def _(act):
                norm_act(act)

            @block.vector
            def _(dve):
                norm_dve(dve, "norm_final")


def slabs(w, tiles=None):
    k, m = w.shape
    return np.ascontiguousarray(w.reshape(k // P, P, m // P, P).transpose(2, 1, 0, 3).reshape(m // P, P, k))


def fm(a):
    return a.reshape(a.shape[0], -1, P).transpose(2, 1, 0)


def col(a):
    return a.reshape(-1, P).T


def shape_constants():
    eye = np.eye(P, dtype=np.float32)
    one = np.ones((P, P), np.float32)
    blk = np.kron(np.eye(2, dtype=np.float32), np.ones((64, 64), np.float32))
    out = {"consts": np.concatenate([eye, one, blk], 1)}
    r64 = np.ones((P, SEQ), np.float32)
    r64[:, ::64] = 0
    out["reset64"] = r64
    s, t = np.meshgrid(np.arange(64), np.arange(64), indexing="ij")
    incl, strict = (s <= t).astype(np.float32), (s < t).astype(np.float32)
    rwmask = np.block([[-incl, 0 * strict], [incl, strict]])
    levels = []
    r = np.arange(P)
    for l in range(6):
        m = 1 << l
        ti, si = r[:, None], r[None, :]
        levels.append(((ti // (2 * m) == si // (2 * m)) & ((ti // m) % 2 == 1) & ((si // m) % 2 == 0)).astype(np.float32))
    sign = np.where(np.arange(P) < 64, -1.0, 1.0).astype(np.float32)[:, None]
    i64 = np.tile(np.eye(64, dtype=np.float32), (2, 1))
    out["ph_rw"] = np.concatenate([rwmask] + levels + [sign, i64], 1)
    sel8 = np.zeros((P, 8, P), np.float32)
    selp = np.zeros((P, 4, P), np.float32)
    for n in range(8):
        sel8[n, n] = 1
        selp[n, n // 2, 64 * (n % 2):64 * (n % 2) + 64] = 1
    last = np.zeros((P, P), np.float32)
    last[P - 1] = 1
    j, t = np.meshgrid(np.arange(P), np.arange(P), indexing="ij")
    ssdmask = np.where(j <= t, 0.0, -1e30)
    glamask = ((j <= t) & (j // 32 == t // 32)).astype(np.float32)
    rs = lambda n, w: np.where(np.arange(w) % n == 0, 0.0, 1.0)[None].repeat(P, 0)
    out["cd"] = (np.concatenate([sel8.reshape(P, -1), selp.reshape(P, -1), last, ssdmask, glamask,
                                 rs(128, SEQ), rs(32, SEQ)], 1), 
                 np.concatenate([rs(8, 40), np.tile(np.arange(P), (P, 1)), np.arange(P)[:, None],
                                 np.triu(np.ones((P, P)), 1)[:, 0:NEXP]], 1))
    return {k: np.ascontiguousarray(a, np.float32) if k != "cd" else [y.astype(np.float32) for y in a] for k, a in out.items()}


def pack(x):
    c = shape_constants()
    a = {}
    a["x"] = fm(np.concatenate([x["x_prompt"][0], x["x_sample"][:, 0]], 0))
    z = lambda n: np.zeros(n, np.float32)
    pad1 = lambda y: np.concatenate([y.reshape(-1), z(P - y.size)])[:, None]
    vecs = {
        "norm_mix0": col(x["norm_mix"][0]), "norm_mix1": col(x["norm_mix"][1]),
        "norm_ffn0": col(x["norm_ffn"][0]), "norm_ffn1": col(x["norm_ffn"][1]),
        "norm_ple0": col(x["norm_ple"][0]), "norm_ple1": col(x["norm_ple"][1]), "norm_final": col(x["norm_final"]),
        "lru_w": col(x["lru_conv_w"][0]), "lru_b": col(x["lru_conv_b"][0]), "b_r": col(x["lru_b_r"][0]),
        "b_i": col(x["lru_b_i"][0]), "lam": col(x["lru_lambda"][0]), "mu": col(x["rwkv_mu"][0]),
        "w0": col(x["rwkv_w0"][0]), "a0": col(x["rwkv_a0"][0]), "k_k": col(x["rwkv_k_k"][0]),
        "k_a": col(x["rwkv_k_a"][0]), "r_k": col(x["rwkv_r_k"][0]), "ln_w": col(x["rwkv_ln_w"][0]),
        "ln_b": col(x["rwkv_ln_b"][0]), "ssd_w": col(x["ssd_conv_w"][0]), "ssd_b": col(x["ssd_conv_b"][0]),
        "ssd_norm": col(x["ssd_norm_w"][0]), "ssd_d": col(np.repeat(x["ssd_d"][0], 64)),
        "alpha_b": col(x["gla_alpha_b"][0]), "gla_norm": col(x["gla_norm_w"][0]),
        "dt_bias": pad1(x["ssd_dt_bias"][0]), "a_log": pad1(x["ssd_a_log"][0]),
    }
    a["vecs"] = np.concatenate([vecs[n] for n, _ in VECS], 1)
    a["consts"] = c["consts"]

    bd = np.zeros((2, P, 4, P), np.float32)
    for n, w in enumerate((x["lru_w_r"][0], x["lru_w_i"][0])):
        for t in range(4):
            bd[n, 0:64, t, 0:64] = w[2 * t]
            bd[n, 64:, t, 64:] = w[2 * t + 1]
    a["ph_ab"] = np.concatenate([bd[0].reshape(P, 512), bd[1].reshape(P, 512),
                                 np.concatenate([x["rwkv_w2"][0], x["rwkv_a2"][0]], 0), x["rwkv_g2"][0],
                                 c["reset64"]], 1)
    hist = x["state_lru_conv"][0].reshape(NS, 3, 4, P).transpose(3, 2, 0, 1)
    shift = x["state_rwkv_shift"][0].reshape(NS, 14, P).transpose(2, 1, 0)
    h0 = x["state_lru_h"][0].reshape(NS, 4, P).transpose(2, 1, 0)
    a["st_ab"] = np.concatenate([hist.reshape(P, 96), shift.reshape(P, 112), h0.reshape(P, 32)], 1)
    w = x["w_in_ab"][0]
    order = [n if k == "xa" else 4 + n if k == "ga" else 8 + n for k, n in AB_TILES]
    a["w_in_ab"] = slabs(w)[order]
    a["w_out_ab"] = slabs(x["w_out_ab"][0])
    a["ph_rw"] = c["ph_rw"]
    a["s_rw"] = x["state_rwkv_wkv"][0].reshape(NS, 4, 2 * 64, 64).transpose(2, 0, 1, 3).reshape(P, 2048)
    flat = lambda y: y.reshape(-1, y.shape[-1])
    for n in ("w_in_ab", "w_out_ab"):
        a[n] = flat(a[n])
    g, u = slabs(x["ffn_w_gate"][0]), slabs(x["ffn_w_up"][0])
    a["w_gu"] = flat(np.stack([g, u], 1))
    a["w_dn"] = slabs(x["ffn_w_down"][0]).reshape(KD * P, 2, SLAB).reshape(KD, P, 2, SLAB).transpose(0, 2, 1, 3).reshape(-1, SLAB)
    for l in range(2):
        a[f"w_ple{l}"] = flat(np.concatenate([slabs(x["w_ple_gate"][l]), slabs(x["w_ple_proj"][l])], 2))
    a["p"] = np.stack([fm(np.concatenate([x["p_prompt"][l, 0], x["p_sample"][l, :, 0]], 0)) for l in range(2)])
    w = x["w_in_cd"][0]
    z_, xbc, dt, q, k, v_, g, al = np.split(w, np.cumsum([512, 1024, 8, 256, 256, 512, 512]), 1)
    tail = np.concatenate([dt, np.zeros((D, 24), np.float32), al], 1)
    body = slabs(np.concatenate([xbc, q, k, v_, z_, g], 1))
    tail = tail.reshape(KD, P, 48).transpose(1, 0, 2).reshape(1, P, KD * 48)
    a["w_in_cd"] = flat(np.concatenate([np.concatenate([tail, np.zeros((1, P, D - KD * 48), np.float32)], 2), body], 0))
    alpha = np.zeros((P, 256), np.float32)
    alpha[32:48] = x["gla_alpha_up"][0]
    router = x["moe_router"][0].reshape(KD, P, NEXP).transpose(1, 0, 2).reshape(P, -1)
    a["ph_cd"] = np.concatenate([c["cd"][0], alpha, router, c["cd"][1]], 1)
    a["st_cd"] = x["state_ssd_conv"][0].reshape(NS, 3, 8, P).transpose(3, 2, 0, 1).reshape(P, -1)
    a["s_ssd"] = x["state_ssd"][0].reshape(NS, 4, P, P).transpose(2, 0, 1, 3).reshape(P, -1)
    a["s_gla"] = x["state_gla"][0].reshape(NS, 2, P, P).transpose(2, 0, 1, 3).reshape(P, -1)
    a["w_out_cd"] = flat(slabs(x["w_out_cd"][0]))
    g, u = [x[n][0].reshape(NEXP, KD, P, KE, P).transpose(0, 3, 2, 1, 4).reshape(NEXP, KE, P, D)
            for n in ("moe_w_gate", "moe_w_up")]
    a["w_moe_gu"] = np.stack([g, u], 2).reshape(-1, D)
    a["w_moe_dn"] = x["moe_w_down"][0].reshape(NEXP, KE, P, KD, P).transpose(0, 3, 2, 1, 4).reshape(-1, FFE)
    return {k: np.ascontiguousarray(y) for k, y in a.items()}


def unpack(r):
    tok = lambda a, f: a.reshape(P, f, -1).transpose(2, 1, 0).reshape(a.size // (P * f), f * P)
    y = tok(r["y"], KD)
    small = r["ab_small"]
    conv_p, conv_s = small[:, 0:12].reshape(P, 4, 3), small[:, 12:108].reshape(P, 4, NS, 3)
    shift, lru_h = tok(small[:, 108:234], 14), tok(small[:, 234:270], 4)
    wkv_p = r["wkv_p"].reshape(2, 64, 4, 64).transpose(2, 0, 3, 1).reshape(8, 64, 64)
    wkv_s = r["wkv_s"].reshape(2, 64, NS, 4, 64).transpose(2, 3, 0, 1, 4).reshape(NS, 8, 64, 64)
    c2 = r["cd_small"]
    conv2_p, conv2_s = c2[:, 0:24].reshape(P, 8, 3), c2[:, 24:216].reshape(P, 8, NS, 3)
    ssd_p = r["ssd_p"].reshape(P, 8, 64).transpose(1, 2, 0)
    ssd_s = r["ssd_s"].reshape(P, NS, 4, P).transpose(1, 2, 0, 3).reshape(NS, 8, 64, P)
    gla_p = r["gla_p"].reshape(2, 64, 2, P).transpose(2, 0, 1, 3).reshape(4, 64, P)
    gla_s = r["gla_s"].reshape(2, 64, NS, 2, P).transpose(2, 3, 0, 1, 4).reshape(NS, 4, 64, P)
    hist_p = lambda c: c.transpose(2, 1, 0).reshape(3, -1)
    hist_s = lambda c: c.transpose(2, 3, 1, 0).reshape(NS, 3, -1)
    outs = (y[:SEQ][None], y[SEQ:][:, None],
            hist_p(conv_p)[None, None], lru_h[0:1][None], shift[0:1][None], wkv_p[None, None],
            hist_p(conv2_p)[None, None], ssd_p[None, None], gla_p[None, None],
            hist_s(conv_s)[None], lru_h[1:][None], shift[1:][None], wkv_s[None],
            hist_s(conv2_s)[None], ssd_s[None], gla_s[None])
    return tuple(np.ascontiguousarray(a) for a in outs)


OUTPUTS = {"wkv_p": 256, "wkv_s": 2048, "ab_small": 270, "ssd_p": 512, "cd_small": 216, "ssd_s": 4096,
           "gla_p": 256, "gla_s": 2048, "y": KD * T}


def kernel(**inputs):
    import concourse.bacc as _bacc
    from concourse.bass_utils import run_bass_kernel_spmd as _run

    arrays = pack({k: np.asarray(a) for k, a in inputs.items()})
    nc = _bacc.Bacc("TRN2", target_bir_lowering=False, num_devices=1)
    i = {k: nc.dram_tensor("in_" + k, a.shape, F32, kind="ExternalInput").ap() for k, a in arrays.items()}
    o = {k: nc.dram_tensor("out_" + k, [P, c], F32, kind="ExternalOutput").ap() for k, c in OUTPUTS.items()}
    build_program(nc, i, o)
    r = _run(nc, [{"in_" + k: a for k, a in arrays.items()}], core_ids=[0])
    return unpack({k: r.results[0]["out_" + k] for k in OUTPUTS})
```

```python
from contextlib import ExitStack

import numpy as np
import concourse.bass as bass
from concourse import mybir

F32 = mybir.dt.float32
ALU = mybir.AluOpType
ACT = mybir.ActivationFunctionType
AX = mybir.AxisListType

P = 128
SEQ = 512
NS = 8
T = SEQ + NS
HALF = T // 2
D = 1024
KD = D // P
EPS = 1e-6
GN_EPS = 64e-5
FF, FFE, NEXP = 2816, 1408, 8
KF, KE = FF // P, FFE // P
PAD = 547
SAMP = 3 + SEQ
SHW = 532
C0 = float(np.exp(-0.5))

RING = 6
SLAB = 1408

VECS = [("norm_mix0", 8), ("norm_ffn0", 8), ("norm_ple0", 8), ("norm_mix1", 8), ("norm_ffn1", 8),
        ("norm_ple1", 8), ("norm_final", 8), ("lru_w", 16), ("lru_b", 4), ("b_r", 4), ("b_i", 4), ("lam", 4),
        ("mu", 14), ("w0", 4), ("a0", 4), ("k_k", 4), ("k_a", 4), ("r_k", 4), ("ln_w", 4), ("ln_b", 4),
        ("ssd_w", 32), ("ssd_b", 8), ("ssd_norm", 4), ("ssd_d", 4), ("alpha_b", 2), ("gla_norm", 1),
        ("dt_bias", 1), ("a_log", 1)]
VCOL, NVEC = {}, 0
for _n, _w in VECS:
    VCOL[_n] = NVEC
    NVEC += _w

AB_TILES = [("xa", i) for i in range(4)] + [("x", 12), ("x", 13)] + [("x", i) for i in (4, 5, 6, 7)] \
    + [("x", i) for i in (0, 1, 2, 3)] + [("x", i) for i in (8, 9, 10, 11)] + [("ga", i) for i in range(4)]
NAB = len(AB_TILES)
NCD = 25
Q_AB = 0
Q_OUT0 = Q_AB + NAB
Q_GU = Q_OUT0 + KD
Q_DN = Q_GU + 2 * KF
Q_PLE0 = Q_DN + 2 * KD
Q_CD = Q_PLE0 + KD
Q_OUT1 = Q_CD + NCD
Q_MOE = Q_OUT1 + KD
PER_E = 2 * KE + KD
MAXB = (2 * T - NEXP) // P + NEXP
Q_PLE1 = Q_MOE + MAXB * PER_E


class Signal:

    def __init__(self, sem):
        self.sem, self.count, self.base = sem, 0, 0

    def on(self, ins, by=1):
        ins.then_inc(self.sem, by)
        self.count += by
        return ins

    def add(self, n):
        self.count += n

    def at(self, n):
        return self.base + n


class Serial:

    def __init__(self, engine, signal):
        self.e, self.own = engine, signal

    def __call__(self, ins, signal=None):
        s = signal or self.own
        s.on(ins)
        self.e.wait_ge(s.sem, s.count)
        return ins


def build_program(nc, i, o):
    with ExitStack() as ctx:
        def sb(name, cols):
            return ctx.enter_context(nc.sbuf_tensor(name, [P, cols], F32))

        signals = []

        def signal(name):
            s = Signal(ctx.enter_context(nc.semaphore(name)))
            signals.append(s)
            return s

        def end_of_block():
            for s in signals:
                s.base = s.count

        h_sb, u_sb = sb("resid", KD * T), sb("normed", KD * T)
        h3 = h_sb[:, :].rearrange("p (k t) -> p k t", t=T)
        u3 = u_sb[:, :].rearrange("p (k t) -> p k t", t=T)
        A, B, C = sb("proj", 13796), sb("wide", KF * T), sb("temps", 4 * T + 4 * 548)
        ring = sb("ring", RING * SLAB)
        vec = sb("vecs", NVEC)
        const = sb("consts", 3 * P)
        ident, ones, blk = const[:, 0:P], const[:, P:2 * P], const[:, 2 * P:3 * P]
        Dm = sb("phase", 3500)
        stage = sb("staging", 560)
        small = sb("small", 700)
        expert_of = ctx.enter_context(nc.sbuf_tensor("expert_of", [P, MAXB + 1], mybir.dt.int32))
        ps = [ctx.enter_context(nc.psum_tensor(f"ps{n}", [P, 1024], F32)) for n in range(4)]

        def pt(n, parts=P, p0=0):
            return ps[n % 4][p0:p0 + parts, 512 - HALF:512 + HALF]

        def v(name, k=0, n=1):
            return vec[:, VCOL[name] + k:VCOL[name] + k + n]

        slab_in = [signal(f"slab_in{s}") for s in range(RING)]
        slab_used = signal("slab_used")
        loaded = signal("loaded")
        resid_in = signal("resid_in")
        stored = signal("stored")
        dve_step, act_step, pool_step = map(signal, ("dve_step", "act_step", "pool_step"))
        evac = signal("evac")

        def slot(q):
            return ring[:, (q % RING) * SLAB:(q % RING + 1) * SLAB]

        def load_slab(sp, q, src, k=None):
            cols = src.shape[-1]
            if k is None:
                if q >= RING:
                    sp.wait_ge(slab_used.sem, q - RING + 1)
            else:
                turn, per = k
                sp.wait_ge(slab_used.sem, q - RING + 1 + per * turn)
            ins = sp.dma_start(slot(q)[:, 0:cols], src)
            if k is None:
                slab_in[q % RING].on(ins, 16)
            else:
                ins.then_inc(slab_in[q % RING].sem, 16)

        def wait_slab(e, q, k=None):
            n = 16 * (q // RING + 1)
            if k is not None:
                turn, per = k
                n = n + (16 * (per // RING)) * turn
            e.wait_ge(slab_in[q % RING].sem, n)

        def product(pe, dst, slab, kt, rhs, first=True, last=True, width=P, k0=0):
            for k in range(kt):
                x = rhs(k)
                for a in (0, HALF):
                    mm = pe.matmul(dst[0:width, a:a + HALF], slab[:, k * width:(k + 1) * width],
                                   x[:, a:a + HALF], start=first and k == 0, stop=last and k == kt - 1)
            return mm

        sq_done, sq_added, norm_sum, norm_root, u_ready = map(signal, (
            "squares", "sq_added", "norm_sum", "norm_root", "u_ready"))
        sq_tmp = lambda m: C[:, (2 + m % 3) * T:(3 + m % 3) * T]
        SQ_SUM, ROOT, RINV = [C[:, (5 + n) * T:(6 + n) * T] for n in range(3)]

        def square(act, m, src=None, more=0, in_loop=False):
            if m >= 4 or in_loop:
                act.wait_ge(sq_added.sem, sq_added.at(m - 3) + more)
            act.activation(SQ_SUM if m == 0 else sq_tmp(m), h3[:, m, :] if src is None else src,
                           ACT.Square).then_inc(sq_done.sem, 1)

        def add_square(dve, m, more=0, in_loop=False):
            if m >= 2 or in_loop:
                dve.wait_ge(sq_added.sem, sq_added.at(m - 1) + more)
            dve.wait_ge(sq_done.sem, sq_done.at(m + 1) + more)
            dve.tensor_tensor(SQ_SUM, SQ_SUM, sq_tmp(m), ALU.add).then_inc(sq_added.sem, 1)

        def squares_counted():
            sq_done.add(KD)
            sq_added.add(KD - 1)

        def norm_pe(pe):
            norm_sum.on(product(pe, pt(0), ones, 1, lambda k: SQ_SUM))

        def norm_act(act):
            act.wait_ge(norm_sum.sem, norm_sum.at(1))
            norm_root.on(act.activation(ROOT, pt(0), ACT.Sqrt, bias=small[:, 0:1], scale=1.0 / D))

        def norm_dve(dve, gain):
            dve.wait_ge(norm_root.sem, norm_root.at(1))
            dve_step.on(dve.reciprocal(RINV, ROOT))
            dve.wait_ge(dve_step.sem, dve_step.count)
            for k in range(KD):
                u_ready.on(dve.scalar_tensor_tensor(out=u3[:, k, :], in0=h3[:, k, :], scalar=v(gain, k), in1=RINV,
                                                    op0=ALU.mult, op1=ALU.mult))

        def normed(pe):
            def tile(k):
                pe.wait_ge(u_ready.sem, u_ready.at(k + 1))
                return u3[:, k, :]
            return tile

        def square_block():
            with nc.Block() as block:
                @block.scalar
                def _(act):
                    for m in range(KD):
                        square(act, m)

                @block.vector
                def _(dve):
                    for m in range(1, KD):
                        add_square(dve, m)
            squares_counted()
            end_of_block()

        ab_src = lambda m: i["w_in_ab"][m * P:(m + 1) * P, :]
        with nc.Block() as block:
            @block.sync
            def _(sp):
                for n in range(2):
                    resid_in.on(sp.dma_start(h3[:, 4 * n:4 * n + 4, :], i["x"][:, 4 * n:4 * n + 4, :]), 16)
                sp.wait_ge(resid_in.sem, resid_in.count)
                for q in range(RING):
                    load_slab(sp, q, ab_src(q))

            @block.scalar
            def _(act):
                loaded.on(act.dma_start(const[:, :], i["consts"]), 16)
                loaded.on(act.dma_start(vec[:, :], i["vecs"]), 16)
                loaded.on(act.dma_start(Dm[:, 0:2560], i["ph_ab"]), 16)
                loaded.on(act.dma_start(stage[:, 0:240], i["st_ab"]), 16)
                act.wait_ge(resid_in.sem, resid_in.count)
                for m in range(KD):
                    square(act, m)
                act.wait_ge(loaded.sem, loaded.count)

            @block.vector
            def _(dve):
                S = Serial(dve, dve_step)
                S(dve.memset(small[:, 0:1], EPS))
                S(dve.memset(small[:, 1:2], GN_EPS))
                S(dve.memset(small[:, 2:3], 1.0))
                for m in range(1, KD):
                    add_square(dve, m)
        squares_counted()
        end_of_block()


        def softplus_small(dve, S, x, e, t0, t1, sign):
            S(dve.tensor_scalar(t0, e, 2.0, None, ALU.add))
            S(dve.reciprocal(t0, t0))
            S(dve.tensor_tensor(e, e, t0, ALU.mult))
            S(dve.tensor_tensor(t0, e, e, ALU.mult))
            S(dve.tensor_scalar(t1, t0, 1.0 / 17, None, ALU.mult))
            for n in (15, 13, 11, 9, 7, 5, 3):
                S(dve.scalar_tensor_tensor(out=t1, in0=t1, scalar=1.0 / n, in1=t0, op0=ALU.add, op1=ALU.mult))
            S(dve.scalar_tensor_tensor(out=t1, in0=t1, scalar=1.0, in1=e, op0=ALU.add, op1=ALU.mult))
            S(dve.tensor_scalar(x, x, sign, 0.0, ALU.mult, ALU.max))
            S(dve.scalar_tensor_tensor(out=x, in0=t1, scalar=2.0, in1=x, op0=ALU.mult, op1=ALU.add))


        xa = lambda t: A[:, t * PAD:(t + 1) * PAD]
        ga = lambda t: A[:, 4 * PAD + t * T:4 * PAD + (t + 1) * T]
        X0 = 4 * PAD + 4 * T
        xr = lambda n: A[:, X0 + n * SHW:X0 + (n + 1) * SHW]
        SG0 = X0 + 14 * SHW
        sg = lambda t: A[:, SG0 + t * T:SG0 + (t + 1) * T]
        av = lambda t: A[:, t * PAD:t * PAD + T]
        ha = lambda t: C[:, t * T:(t + 1) * T]
        tm = lambda n: C[:, 4 * T + n * 548:4 * T + (n + 1) * 548]
        tb = lambda n: B[:, 10240 + n * 600:10240 + n * 600 + 544]
        rw4 = B[:, 0:10240].rearrange("p (t c k q) -> p t c k q", t=4, c=8, k=5)
        RB, RK, RR, RKAP, RV = range(5)

        def rw(t, k):
            return rw4[:, t, :, k, :]

        def chunks(ap):
            return ap.rearrange("p (c q) -> p c q", q=64)

        bd_r = lambda t: Dm[:, t * P:(t + 1) * P]
        bd_i = lambda t: Dm[:, 512 + t * P:512 + (t + 1) * P]
        wa2 = Dm[:, 1024:1536]
        g2 = Dm[:, 1536:2048]
        reset64 = Dm[:, 2048:2560]
        td = Dm[:, 2560:3104]
        st_conv = stage[:, 0:96].rearrange("p (t b k) -> p t b k", t=4, b=NS)
        st_shift = stage[:, 96:208].rearrange("p (t b) -> p t b", t=14)
        st_h0 = stage[:, 208:240].rearrange("p (t b) -> p t b", t=4)
        o_convp = stage[:, 240:252].rearrange("p (t k) -> p t k", t=4)
        o_convs = stage[:, 252:348].rearrange("p (t b k) -> p t b k", t=4, b=NS)
        o_shift = stage[:, 348:474].rearrange("p (t k) -> p t k", t=14)
        o_h = stage[:, 474:510].rearrange("p (t k) -> p t k", t=4)
        ncl, cl, oka = small[:, 4:8], small[:, 8:12], small[:, 12:16]
        sp_t = small[:, 16:32]
        smp = small[:, 32:224].rearrange("p (n t b) -> p n t b", n=6, t=4)
        SD, SKK, SBB, SK, SR, SV = range(6)
        dec = small[:, 224:256].rearrange("p (t c) -> p t c", t=4)

        xc_ready, gates_ready, gates_read = signal("xc_ready"), signal("gates_ready"), signal("gates_read")
        a_ready, m_ready, s_ready, rg_done = map(signal, ("a_ready", "m_ready", "s_ready", "rg_done"))
        x12_ready, wl_ready, wa_ready, wa_read = map(signal, ("x12_ready", "wl_ready", "wa_ready", "wa_read"))
        cs_ready, ex_ready, kk_raw, kk_sq = map(signal, ("cs_ready", "ex_ready", "kk_raw", "kk_sq"))
        kk_sum, kk_max, kk_root, rk_ready = map(signal, ("kk_sum", "kk_max", "kk_root", "rk_ready"))
        k_ready, r_ready, rr_done = map(signal, ("k_ready", "r_ready", "rr_done"))
        bon_sum, bon_read, setup_done = map(signal, ("bon_sum", "bon_read", "setup_done"))
        lam_exp = signal("lam_exp")

        with nc.Block() as block:
            @block.sync
            def _(sp):
                for q in range(RING, NAB):
                    load_slab(sp, q, ab_src(q))
                for q in range(RING):
                    load_slab(sp, Q_OUT0 + q, i["w_out_ab"][q * P:(q + 1) * P, :])

            @block.gpsimd
            def _(pool):
                S = Serial(pool, pool_step)
                xa4 = A[:, 0:4 * PAD].rearrange("p (t c) -> p t c", t=4)
                S(pool.memset(xa4[:, :, 0:3], 0.0))
                for t in range(4):
                    S(pool.tensor_copy(xa4[:, t, SAMP:PAD].rearrange("p (b k) -> p b k", k=4)[:, :, 0:3], st_conv[:, t]))
                x14 = A[:, X0:X0 + 14 * SHW].rearrange("p (n c) -> p n c", n=14)
                S(pool.memset(x14[:, :, 0:1], 0.0))
                S(pool.tensor_copy(x14[:, :, 513:513 + 2 * NS:2], st_shift))
                for t in range(4):
                    S(pool.tensor_copy(o_convs[:, t, :, 0:2], st_conv[:, t, :, 1:3]))
                setup_done.on(pool.memset(small[:, 3:4], 0.0))
                for t in range(4):
                    pool.wait_ge(k_ready.sem, k_ready.at(t + 1))
                    pool.wait_ge(r_ready.sem, r_ready.at(t + 1))
                    pool.wait_ge(ex_ready.sem, ex_ready.at(t + 1))
                    pool_step.on(pool.tensor_copy(smp[:, SK, t, :], xr(4 + t)[:, SEQ:T]))
                    pool_step.on(pool.tensor_copy(smp[:, SR, t, :], xr(t)[:, SEQ:T]))
                    pool_step.on(pool.tensor_copy(dec[:, t, :], tm(2)[:, 63:SEQ:64]))
                    rr_done.on(pool.tensor_tensor(rw(t, RR), chunks(xr(t)[:, 0:SEQ]), chunks(tm(2)[:, 0:SEQ]), ALU.mult))

            @block.tensor
            def _(pe):
                norm_pe(pe)
                for m in range(NAB):
                    wait_slab(pe, Q_AB + m)
                    if m >= 2:
                        pe.wait_ge(evac.sem, evac.at(m - 1))
                    slab_used.on(product(pe, pt(m % 2), slot(Q_AB + m), KD, lambda k: u3[:, k, :] if m else normed(pe)(k)))
                    if m in (4, 6, 8, 10):
                        t = (m - 4) // 2
                        pe.wait_ge(xc_ready.sem, xc_ready.at(t + 1))
                        if t:
                            pe.wait_ge(gates_read.sem, gates_read.at(t))
                        product(pe, pt(2), bd_r(t), 1, lambda k: xa(t))
                        gates_ready.on(product(pe, pt(3), bd_i(t), 1, lambda k: xa(t)))
                    if m in (12, 14, 16, 18):
                        t = (m - 12) // 2
                        pe.wait_ge(kk_sq.sem, kk_sq.at(t + 1))
                        pe.wait_ge(wa_read.sem, wa_read.at(t + 1))
                        kk_sum.on(product(pe, pt(2), blk, 1, lambda k: tb(0)))
                    if m in (11, 13, 15, 17):
                        t = (m - 11) // 2
                        if t:
                            pe.wait_ge(kk_max.sem, kk_max.at(t))
                        else:
                            pe.wait_ge(wl_ready.sem, wl_ready.at(1))
                            pe.wait_ge(gates_read.sem, gates_read.at(4))
                        for n, (p0, dst) in enumerate(((0, pt(2)), (64, pt(3)))):
                            for a in (0, HALF):
                                mm = pe.matmul(dst[:, a:a + HALF], wa2[p0:p0 + 64, t * P:(t + 1) * P],
                                               xr(12)[p0:p0 + 64, a:a + HALF], start=True, stop=True)
                        wa_ready.on(mm)
                    if m >= 18:
                        t = m - 18
                        pe.wait_ge(rk_ready.sem, rk_ready.at(t + 1))
                        pe.wait_ge(wa_read.sem, wa_read.at(4))
                        if t:
                            pe.wait_ge(kk_max.sem, kk_max.at(4))
                        if t >= 2:
                            pe.wait_ge(bon_read.sem, bon_read.at(t - 1))
                        bon_sum.on(product(pe, pt(3 - t % 2), blk, 1, lambda k: sg(t)))

            @block.scalar
            def _(act):
                S = Serial(act, act_step)
                S(act.activation(sp_t[:, 0:4], v("lam", 0, 4), ACT.Abs))
                S(act.activation(sp_t[:, 4:8], sp_t[:, 0:4], ACT.Exp, scale=-1.0), lam_exp)
                norm_act(act)
                act.wait_ge(setup_done.sem, setup_done.at(1))
                for m in range(NAB):
                    kind, n = AB_TILES[m]
                    act.wait_ge(slab_used.sem, Q_AB + m + 1)
                    src = pt(m % 2)
                    if kind == "xa":
                        act_step.on(act.activation(xa(n)[:, 3:3 + SEQ], src[:, 0:SEQ], ACT.Copy))
                        act_step.on(act.activation(xa(n)[:, SAMP + 3:PAD:4], src[:, SEQ:T], ACT.Copy))
                        act_step.on(act.activation(o_convp[:, n, :], src[:, SEQ - 3:SEQ], ACT.Copy))
                        evac.on(act.activation(o_convs[:, n, :, 2], src[:, SEQ:T], ACT.Copy))
                    elif kind == "x":
                        act_step.on(act.activation(xr(n)[:, 1:1 + SEQ], src[:, 0:SEQ], ACT.Copy))
                        act_step.on(act.activation(xr(n)[:, 514:514 + 2 * NS:2], src[:, SEQ:T], ACT.Copy))
                        evac.on(act.activation(o_shift[:, n, :], src[:, SEQ - 1:T], ACT.Copy))
                    else:
                        evac.on(act.activation(ga(n), src, ACT.Gelu_apprx_tanh))
                    if m in (5, 7, 9, 11):
                        t = (m - 5) // 2
                        act.wait_ge(gates_ready.sem, gates_ready.at(t + 1))
                        if t:
                            act.wait_ge(rg_done.sem, rg_done.at(t))
                        else:
                            act.wait_ge(xc_ready.sem, xc_ready.at(4))
                        S(act.activation(tm(1)[:, 0:T], pt(2), ACT.Sigmoid, bias=v("b_r", t)))
                        S(act.activation(tm(2)[:, 0:T], pt(3), ACT.Sigmoid, bias=v("b_i", t)), gates_read)
                        S(act.activation(tm(3)[:, 0:T], tm(1)[:, 0:T], ACT.Tanh, scale=ncl[:, t:t + 1]))
                        S(act.activation(tm(1)[:, 0:T], tm(1)[:, 0:T], ACT.Exp, scale=cl[:, t:t + 1]), a_ready)
                        act.wait_ge(m_ready.sem, m_ready.at(t + 1))
                        S(act.activation(tm(3)[:, 0:T], tm(0)[:, 0:T], ACT.Sqrt), s_ready)
                    if m == 10:
                        act.wait_ge(x12_ready.sem, x12_ready.at(2))
                        S(act.activation(xr(13)[:, 0:T], xr(13)[:, 0:T], ACT.Sigmoid))
                        S(act.activation(xr(12)[0:64, 0:T], xr(12)[0:64, 0:T], ACT.Tanh), wl_ready)
                    if m in (12, 14, 16, 18):
                        t = (m - 12) // 2
                        act.wait_ge(kk_raw.sem, kk_raw.at(t + 1))
                        S(act.activation(tb(0)[:, 0:T], tb(1)[:, 0:T], ACT.Square), kk_sq)
                        act.wait_ge(cs_ready.sem, cs_ready.at(t + 1))
                        if t:
                            act.wait_ge(rr_done.sem, rr_done.at(t))
                        S(act.activation(tm(2)[:, 0:SEQ], tm(0)[:, 0:SEQ], ACT.Exp, scale=-C0))
                        S(act.activation(tm(3)[:, 0:SEQ], tm(0)[:, 0:SEQ], ACT.Exp, scale=C0))
                        S(act.activation(tm(1)[:, 0:SEQ], tm(1)[:, 0:SEQ], ACT.Exp, scale=-C0))
                        S(act.activation(smp[:, SD, t, :], sg(t)[:, SEQ:T], ACT.Exp, scale=-C0), ex_ready)
                    if m in (11, 13, 15, 17):
                        t = (m - 11) // 2
                        act.wait_ge(wa_ready.sem, wa_ready.at(t + 1))
                        S(act.activation(sg(t), pt(2), ACT.Sigmoid, bias=v("w0", t)))
                        S(act.activation(av(t), pt(3), ACT.Sigmoid, bias=v("a0", t)), wa_read)
                    if m in (12, 14, 16, 18):
                        t = (m - 12) // 2
                        act.wait_ge(kk_max.sem, kk_max.at(t + 1))
                        S(act.activation(tb(0)[:, 0:T], tb(0)[:, 0:T], ACT.Sqrt), kk_root)

            @block.vector
            def _(dve):
                S = Serial(dve, dve_step)
                norm_dve(dve, "norm_mix0")
                dve.wait_ge(lam_exp.sem, lam_exp.at(1))
                S(dve.tensor_copy(ncl, v("lam", 0, 4)))
                softplus_small(dve, S, ncl, sp_t[:, 4:8], sp_t[:, 8:12], sp_t[:, 12:16], -1.0)
                S(dve.tensor_scalar(cl, ncl, -8.0, None, ALU.mult))
                S(dve.tensor_scalar(ncl, ncl, 8.0, None, ALU.mult))
                S(dve.tensor_scalar(oka, v("k_a", 0, 4), -1.0, 1.0, ALU.mult, ALU.add))
                for t in range(4):
                    w = lambda k: v("lru_w", 4 * k + t)
                    x, y = xa(t), tm(0)
                    dve.wait_ge(evac.sem, evac.at(t + 1))
                    S(dve.tensor_scalar(y[:, 0:544], x[:, 3:547], w(3), v("lru_b", t), ALU.mult, ALU.add))
                    for k in (2, 1):
                        S(dve.scalar_tensor_tensor(out=y[:, 0:544], in0=x[:, k:k + 544], scalar=w(k),
                                                   in1=y[:, 0:544], op0=ALU.mult, op1=ALU.add))
                    S(dve.scalar_tensor_tensor(out=x[:, SEQ:T], in0=x[:, SAMP:PAD:4], scalar=w(0),
                                               in1=y[:, SAMP:544:4], op0=ALU.mult, op1=ALU.add))
                    S(dve.scalar_tensor_tensor(out=x[:, 0:SEQ], in0=x[:, 0:SEQ], scalar=w(0),
                                               in1=y[:, 0:SEQ], op0=ALU.mult, op1=ALU.add), xc_ready)
                def rg_lru(t):
                    a, gi, th = tm(1)[:, 0:T], tm(2)[:, 0:T], tm(3)[:, 0:T]
                    mm = tm(0)[:, 0:T]
                    dve.wait_ge(a_ready.sem, a_ready.at(t + 1))
                    S(dve.tensor_tensor(mm, a, a, ALU.mult))
                    S(dve.scalar_tensor_tensor(out=mm, in0=mm, scalar=1.0, in1=th, op0=ALU.add, op1=ALU.mult), m_ready)
                    S(dve.tensor_tensor(gi, gi, xa(t)[:, 0:T], ALU.mult))
                    dve.wait_ge(s_ready.sem, s_ready.at(t + 1))
                    S(dve.tensor_tensor(gi, gi, th, ALU.mult))
                    S(dve.tensor_tensor_scan(ha(t)[:, 0:SEQ], a[:, 0:SEQ], gi[:, 0:SEQ], 0.0, ALU.mult, ALU.add))
                    S(dve.tensor_tensor(mm[:, 0:NS], a[:, SEQ:T], st_h0[:, t, :], ALU.mult))
                    S(dve.tensor_tensor(ha(t)[:, SEQ:T], mm[:, 0:NS], gi[:, SEQ:T], ALU.add))
                    S(dve.tensor_copy(o_h[:, t, :], ha(t)[:, SEQ - 1:T]), rg_done)

                def shift(n, s=None):
                    x, d = xr(n), td
                    dve.wait_ge(evac.sem, evac.at(1 + AB_TILES.index(("x", n))))
                    S(dve.tensor_tensor(d[:, 0:528], x[:, 0:528], x[:, 1:529], ALU.subtract))
                    S(dve.scalar_tensor_tensor(out=x[:, 0:SEQ], in0=d[:, 0:SEQ], scalar=v("mu", n),
                                               in1=x[:, 1:1 + SEQ], op0=ALU.mult, op1=ALU.add))
                    S(dve.scalar_tensor_tensor(out=x[:, SEQ:T], in0=d[:, 513:513 + 2 * NS:2], scalar=v("mu", n),
                                               in1=x[:, 514:514 + 2 * NS:2], op0=ALU.mult, op1=ALU.add), s)

                rg_lru(0)
                rg_lru(1)
                shift(12, x12_ready)
                shift(13, x12_ready)
                rg_lru(2)
                rg_lru(3)
                for t in range(4):
                    xk, xv_, kk, e = xr(4 + t), xr(8 + t), tb(1)[:, 0:T], tm
                    shift(4 + t)
                    S(dve.tensor_scalar(kk, xk[:, 0:T], v("k_k", t), None, ALU.mult), kk_raw)
                    dve.wait_ge(wa_read.sem, wa_read.at(t + 1))
                    S(dve.tensor_tensor_scan(tm(0)[:, 0:SEQ], reset64, sg(t)[:, 0:SEQ], 0.0, ALU.mult, ALU.add))
                    S(dve.tensor_tensor(tm(1)[:, 0:SEQ], tm(0)[:, 0:SEQ], sg(t)[:, 0:SEQ], ALU.subtract), cs_ready)
                    shift(t, r_ready)
                    S(dve.tensor_scalar(td[:, 0:T], av(t), v("k_a", t), oka[:, t:t + 1], ALU.mult, ALU.add))
                    S(dve.tensor_tensor(xk[:, 0:T], xk[:, 0:T], td[:, 0:T], ALU.mult), k_ready)
                    dve.wait_ge(ex_ready.sem, ex_ready.at(t + 1))
                    S(dve.scalar_tensor_tensor(out=sg(t), in0=xr(t)[:, 0:T], scalar=v("r_k", t),
                                               in1=xk[:, 0:T], op0=ALU.mult, op1=ALU.mult), rk_ready)
                    dve.wait_ge(kk_sum.sem, kk_sum.at(t + 1))
                    S(dve.tensor_scalar(tb(0)[:, 0:T], pt(2), 1e-12, None, ALU.max), kk_max)
                    S(dve.tensor_tensor(rw(t, RK), chunks(xk[:, 0:SEQ]), chunks(tm(3)[:, 0:SEQ]), ALU.mult))
                    dve.wait_ge(kk_root.sem, kk_root.at(t + 1))
                    S(dve.reciprocal(tb(0)[:, 0:T], tb(0)[:, 0:T]))
                    S(dve.tensor_tensor(kk, kk, tb(0)[:, 0:T], ALU.mult))
                    S(dve.tensor_tensor(av(t), kk, av(t), ALU.mult))
                    S(dve.tensor_tensor(rw(t, RKAP), chunks(kk[:, 0:SEQ]), chunks(tm(1)[:, 0:SEQ]), ALU.mult))
                    S(dve.tensor_tensor(rw(t, RB), chunks(av(t)[:, 0:SEQ]), chunks(tm(3)[:, 0:SEQ]), ALU.mult))
                    S(dve.tensor_copy(smp[:, SKK, t, :], kk[:, SEQ:T]))
                    S(dve.tensor_copy(smp[:, SBB, t, :], av(t)[:, SEQ:T]))
                for t in range(4):
                    xk, xv_ = xr(4 + t), xr(8 + t)
                    shift(8 + t)
                    S(dve.tensor_copy(rw(t, RV), chunks(xv_[:, 0:SEQ])))
                    S(dve.tensor_copy(smp[:, SV, t, :], xv_[:, SEQ:T]))
                    dve.wait_ge(bon_sum.sem, bon_sum.at(t + 1))
                    dve.wait_ge(rr_done.sem, rr_done.at(t + 1))
                    S(dve.tensor_tensor(xk[:, 0:T], pt(3 - t % 2), xv_[:, 0:T], ALU.mult), bon_read)
                for t in range(4):
                    dve.wait_ge(evac.sem, evac.at(19 + t))
                    S(dve.tensor_tensor(ga(t), ga(t), ha(t), ALU.mult))
        end_of_block()

        def spread(ap, n, axis):
            shape = list(ap.shape)
            shape.insert(axis, n)
            return ap.unsqueeze(axis).broadcast_to(shape)

        rwmask, level = Dm[:, 0:P], lambda l: Dm[:, P * (1 + l):P * (2 + l)]
        sign, i64 = Dm[:, 7 * P:7 * P + 1], Dm[:, 7 * P + 1:7 * P + 65]
        pairs = lambda ap: ap.rearrange("p (n c) -> p n c", c=P)
        AL, DD, EE, GG = [pairs(u_sb[:, n * 1024:(n + 1) * 1024]) for n in range(4)]
        OO = pairs(C[:, 0:1024])
        AM = C[:, 1024:3072].rearrange("p (c h t q) -> p c h t q", c=2, h=2, t=4)
        BK = C[:, 3072:4096].rearrange("p (h c t q) -> p h c t q", c=2, h=2, t=4)
        PV = B[:, 10240:11264].rearrange("p (h c t q) -> p h c t q", c=2, h=2, t=4)
        Qs = Dm[:, 2560:2816].rearrange("p (t q) -> p t q", t=4)
        Zs = [Dm[:, 2816 + 256 * n:3072 + 256 * n].rearrange("p (t q) -> p t q", t=4) for n in range(2)]
        yr = A[:, X0:X0 + 4 * SHW].rearrange("p (t c) -> p t c", t=4)

        def rk(t, c, k, hh, n=1):
            j = ((t * 8 + c) * 5 + k) * 64
            return B[64 * hh:64 * hh + 64, j:j + 64 * n]

        names = ("ab_mm", "ab_read", "am_mm", "am_read", "bk_mm", "bk_read", "v_mm", "v_read", "d_ready", "e_mm",
                 "e_read", "o_ready", "next_o", "g_mm", "g_read", "eg_mm", "de_read", "q_mm", "q_read", "p_mm",
                 "p_read", "z_mm", "y_mm", "y_read", "z_read")
        g = {n: signal("rw_" + n) for n in names}

        def w(e, name, n):
            e.wait_ge(g[name].sem, g[name].at(n))

        def qz_psum(half, hh, t):
            n = 512 * half + 64 * (t % 2)
            return ps[0][64 * hh:64 * hh + 64, n:n + 64]

        def qz(half):
            return ps[0][:, 512 * half:512 * half + P].rearrange("p (t q) -> p t q", t=2)

        def nth(s, l, cc):
            return 10 * s + 2 * l + cc + 1

        with nc.Block() as block:
            @block.sync
            def _(sp):
                loaded.on(sp.dma_start(Dm[:, 0:961], i["ph_rw"]), 16)

            @block.gpsimd
            def _(pool):
                S = Serial(pool, pool_step)
                pool_step.on(pool.memset(B[0:64, 10240:11264], 0.0))
                S(pool.memset(u_sb[:, 0:1024], 0.0))
                for s in range(4):
                    for l in range(4):
                        for cc in range(2):
                            n = slice(4 * cc, 4 * cc + 4)
                            w(pool, "g_mm", nth(s, l, cc))
                            g["next_o"].on(pool.tensor_tensor(OO[:, n], AL[:, n], spread(level(l + 2), 4, 1), ALU.mult))

            @block.tensor
            def _(pe):
                for s in range(4):
                    if s:
                        w(pe, "de_read", 10 * s)
                        w(pe, "z_read", 4 * s)
                        w(pe, "y_read", 2 * s)
                    for cc in range(2):
                        for t in range(4):
                            n = (4 * cc + t) * P
                            for hh in range(2):
                                mm = pe.matmul(ps[0][64 * hh:64 * hh + 64, n + 64 * hh:n + 64 * hh + 64],
                                               rk(t, 2 * s + cc, RKAP, hh), rk(t, 2 * s + cc, RB, hh),
                                               start=True, stop=True)
                    g["ab_mm"].on(mm)
                    for cc in range(2):
                        for t in range(4):
                            for hh in range(2):
                                mm = pe.matmul(ps[1 + cc][:, 512 * hh + t * P:512 * hh + (t + 1) * P],
                                               rk(t, 2 * s + cc, RB, hh, 2), rk(t, 2 * s + cc, RR, hh, 2),
                                               start=True, stop=True)
                        g["am_mm"].on(mm)
                    for cc in range(2):
                        for t in range(4):
                            for hh in range(2):
                                j, n = 64 * hh, 512 * hh + (4 * cc + t) * 64
                                mm = pe.transpose(ps[3][:, n:n + 64], rk(t, 2 * s + cc, RB, hh, 2),
                                                  ident[j:j + 64, j:j + 64])
                    g["bk_mm"].on(mm)
                    w(pe, "ab_read", s + 1)
                    for cc in range(2):
                        for t in range(4):
                            for hh in range(2):
                                j, n = 64 * hh, 512 * hh + (4 * cc + t) * 64
                                mm = pe.transpose(ps[0][:, n:n + 64], rk(t, 2 * s + cc, RKAP, hh, 2),
                                                  ident[j:j + 64, j:j + 64])
                    g["v_mm"].on(mm)
                    w(pe, "d_ready", s + 1)
                    w(pe, "am_read", 2 * s + 2)
                    for n in range(8):
                        mm = pe.transpose(ps[1][:, n * P:(n + 1) * P], DD[:, n, :], ident)
                    g["e_mm"].on(mm)
                    w(pe, "v_read", s + 1)
                    for l in range(5):
                        for cc in range(2):
                            if l == 0:
                                w(pe, "o_ready", 2 * s + cc + 1)
                                w(pe, "e_read", s + 1)
                            else:
                                w(pe, "next_o", 8 * s + 2 * (l - 1) + cc + 1)
                                w(pe, "de_read", nth(s, l - 1, cc))
                            for n in range(4 * cc, 4 * cc + 4):
                                mm = pe.matmul(ps[0][:, n * P:(n + 1) * P], OO[:, n, :], EE[:, n, :], start=True, stop=True)
                            g["g_mm"].on(mm)
                        for cc in range(2):
                            w(pe, "g_read", nth(s, l, cc))
                            for n in range(4 * cc, 4 * cc + 4):
                                if l < 4:
                                    pe.matmul(ps[1][:, n * P:(n + 1) * P], GG[:, n, :], DD[:, n, :], start=True, stop=True)
                                mm = pe.matmul(ps[2][:, n * P:(n + 1) * P], DD[:, n, :], GG[:, n, :], start=True, stop=True)
                            g["eg_mm"].on(mm)
                    w(pe, "de_read", 10 * s + 10)
                    w(pe, "bk_read", s + 1)
                    for cc in range(2):
                        c = 2 * s + cc
                        z = Zs[(c + 1) % 2]
                        for half in range(2):
                            if c:
                                w(pe, "z_read", 2 * c - 1 + half)
                            for t in (2 * half, 2 * half + 1):
                                for hh in range(2):
                                    dst = qz_psum(half, hh, t)
                                    if c:
                                        pe.matmul(dst, rk(t, c, RKAP, hh), z[64 * hh:64 * hh + 64, t, :], start=True, stop=False)
                                    mm = pe.matmul(dst, AM[:, cc, hh, t, 64:P], PV[:, hh, cc, t, :],
                                                   start=c == 0, stop=True)
                            g["q_mm"].on(mm)
                        for half in range(2):
                            w(pe, "q_read", 2 * c + half + 1)
                            for t in (2 * half, 2 * half + 1):
                                for hh in range(2):
                                    j = 64 * hh
                                    mm = pe.matmul(ps[1 + half][0:64, 512 * hh + 64 * t:512 * hh + 64 * t + 64],
                                                   EE[j:j + 64, 4 * cc + t, j:j + 64], Qs[j:j + 64, t, :],
                                                   start=True, stop=True)
                            g["p_mm"].on(mm)
                        for half in range(2):
                            w(pe, "p_read", 2 * c + half + 1)
                            for t in (2 * half, 2 * half + 1):
                                for hh in range(2):
                                    mm = pe.matmul(qz_psum(half, hh, t), BK[:, hh, cc, t, :], PV[:, hh, cc, t, :],
                                                   start=True, stop=True)
                            g["z_mm"].on(mm)
                        if c:
                            w(pe, "y_read", c)
                        for t in range(4):
                            for hh in range(2):
                                dst = ps[3][64 * hh:64 * hh + 64, 64 * t:64 * t + 64]
                                if c:
                                    pe.matmul(dst, z[64 * hh:64 * hh + 64, t, :], rk(t, c, RR, hh), start=True, stop=False)
                                mm = pe.matmul(dst, PV[:, hh, cc, t, :], AM[:, cc, hh, t, 0:64],
                                               start=c == 0, stop=True)
                        g["y_mm"].on(mm)

            @block.scalar
            def _(act):
                for s in range(4):
                    w(act, "bk_mm", s + 1)
                    if s == 0:
                        act.wait_ge(loaded.sem, loaded.count)
                    else:
                        w(act, "z_mm", 4 * s)
                    g["bk_read"].on(act.activation(C[:, 3072:4096], ps[3][:, :], ACT.Copy, scale=sign))
                    w(act, "v_mm", s + 1)
                    if s:
                        w(act, "y_mm", 2 * s)
                    g["v_read"].on(act.activation(B[64:P, 10240:11264], ps[0][64:P, :], ACT.Copy))
                    w(act, "e_mm", s + 1)
                    g["e_read"].on(act.activation(u_sb[:, 2048:3072], ps[1][:, :], ACT.Copy))
                    for l in range(5):
                        for cc in range(2):
                            w(act, "g_mm", nth(s, l, cc))
                            if l:
                                w(act, "eg_mm", nth(s, l - 1, cc))
                            g["g_read"].on(act.activation(u_sb[:, 3072 + 512 * cc:3584 + 512 * cc],
                                                          ps[0][:, 512 * cc:512 * cc + 512], ACT.Copy))
                    for cc in range(2):
                        c = 2 * s + cc
                        for half in range(2):
                            w(act, "p_mm", 2 * c + half + 1)
                            tt = slice(2 * half, 2 * half + 2)
                            for hh in range(2):
                                ins = act.activation(PV[0:64, hh, cc, tt], ps[1 + half][0:64, 512 * hh:512 * hh + 256]
                                                     .rearrange("p (t q) -> p t q", t=4)[:, tt], ACT.Copy)
                                (g["p_read"] if hh else act_step).on(ins)
                        w(act, "y_mm", c + 1)
                        g["y_read"].on(act.activation(yr[:, :, 64 * c:64 * c + 64],
                                                      ps[3][:, 0:256].rearrange("p (t q) -> p t q", t=4), ACT.Copy))

            @block.vector
            def _(dve):
                S = Serial(dve, dve_step)
                dve.wait_ge(loaded.sem, loaded.count)
                dve.wait_ge(pool_step.sem, pool_step.at(2))
                for s in range(4):
                    w(dve, "ab_mm", s + 1)
                    for hh in range(2):
                        j = 64 * hh
                        S(dve.tensor_copy(AL[j:j + 64, :, j:j + 64], pairs(ps[0][j:j + 64, :])[:, :, j:j + 64]),
                          g["ab_read"] if hh else None)
                    S(dve.tensor_tensor(OO, AL, spread(level(0), 8, 1), ALU.mult))
                    S(dve.tensor_tensor(DD, spread(ident, 8, 1), OO, ALU.subtract), g["d_ready"])
                    for cc in range(2):
                        n = slice(4 * cc, 4 * cc + 4)
                        S(dve.tensor_tensor(OO[:, n], AL[:, n], spread(level(1), 4, 1), ALU.mult), g["o_ready"])
                    for cc in range(2):
                        w(dve, "am_mm", 2 * s + cc + 1)
                        if s and cc == 0:
                            w(dve, "y_mm", 2 * s)
                        S(dve.tensor_tensor(pairs(C[:, 1024 * (1 + cc):1024 * (2 + cc)]), pairs(ps[1 + cc][:, :]),
                                            spread(rwmask, 8, 1), ALU.mult), g["am_read"])
                    for l in range(5):
                        for cc in range(2):
                            n, half = slice(4 * cc, 4 * cc + 4), slice(512 * cc, 512 * cc + 512)
                            w(dve, "eg_mm", nth(s, l, cc))
                            if l < 4:
                                S(dve.tensor_tensor(DD[:, n], DD[:, n], pairs(ps[1][:, half]), ALU.subtract))
                            S(dve.tensor_tensor(EE[:, n], EE[:, n], pairs(ps[2][:, half]), ALU.subtract), g["de_read"])
                    for cc in range(2):
                        c = 2 * s + cc
                        z, z1 = Zs[(c + 1) % 2], Zs[c % 2]
                        dc = dec[:, :, c].unsqueeze(2).broadcast_to([P, 4, 64])
                        for half in range(2):
                            tt = slice(2 * half, 2 * half + 2)
                            w(dve, "q_mm", 2 * c + half + 1)
                            S(dve.tensor_copy(Qs[:, tt], qz(half)), g["q_read"])
                        for half in range(2):
                            tt = slice(2 * half, 2 * half + 2)
                            w(dve, "z_mm", 2 * c + half + 1)
                            if c and not half:
                                w(dve, "y_mm", c)
                            if c:
                                S(dve.tensor_tensor(z1[:, tt], qz(half), z[:, tt], ALU.add))
                                S(dve.tensor_tensor(z1[:, tt], z1[:, tt], dc[:, tt], ALU.mult), g["z_read"])
                            else:
                                S(dve.tensor_tensor(z1[:, tt], qz(half), dc[:, tt], ALU.mult), g["z_read"])
        end_of_block()

        S0 = u_sb[:, 0:2048]
        DG = u_sb[:, 2048:4096]
        S1, T1 = B[:, 0:2048], B[:, 2048:4096]
        btk = lambda ap: ap.rearrange("p (n k) -> p n k", k=64)
        row = small[:, 256:288]

        def per_bt(n):
            return smp[:, n].rearrange("p t b -> p b t").unsqueeze(3).broadcast_to([P, NS, 4, 64])

        b4 = lambda ap: ap.rearrange("p (b t k) -> p b t k", b=NS, t=4)
        dg_ready, bc_mm, bc_read, st_in, norm_a, norm_b = map(signal, (
            "dg_ready", "bc_mm", "bc_read", "st_in", "norm_a", "norm_b"))
        mean_mm, var_mm, g_mm, sq_ready, root_ready, cent, g_read = map(signal, (
            "mean_mm", "var_mm", "g_mm", "sq_ready", "root_ready", "cent", "g_read"))
        scaled = signal("scaled")
        gn_bank = lambda t: ps[2 + t // 2][:, 512 * (t % 2):512 * (t % 2) + SEQ]
        sqr = lambda t: xr(8 + t)[:, 0:SEQ]
        gb = lambda t: B[:, 4096 + t * SEQ:4096 + (t + 1) * SEQ]
        ysm, ysq = Dm[:, 2560:2592], Dm[:, 2592:2624]
        tb_ = lambda ap: ap.rearrange("p (t b) -> p t b", t=4)
        xk4 = A[:, X0 + 4 * SHW:X0 + 8 * SHW].rearrange("p (t c) -> p t c", c=SHW)
        with nc.Block() as block:
            @block.sync
            def _(sp):
                st_in.on(sp.dma_start(S0, i["s_rw"]), 16)
                stored.on(sp.dma_start(o["wkv_p"], Dm[:, 3072:3328]), 16)
                stored.on(sp.dma_start(o["ab_small"], stage[:, 240:510]), 16)
                sp.wait_ge(dve_step.sem, dve_step.at(1))
                stored.on(sp.dma_start(o["wkv_s"], S1), 16)
                sp.wait_ge(stored.sem, stored.count)

            @block.tensor
            def _(pe):
                def broadcast(n):
                    pe.wait_ge(dg_ready.sem, dg_ready.at(n + 1))
                    if n:
                        pe.wait_ge(bc_read.sem, bc_read.at(n))
                    for r in range(4):
                        mm = pe.matmul(ps[r // 2][:, 512 * (r % 2):512 * (r % 2) + 512], blk,
                                       DG[:, 512 * r:512 * r + 512], start=True, stop=True)
                    bc_mm.on(mm)

                def mean(t):
                    mean_mm.on(pe.matmul(gn_bank(t), blk, yr[:, t, 0:SEQ], start=True, stop=True))

                def var(t):
                    pe.wait_ge(sq_ready.sem, sq_ready.at(t + 1))
                    var_mm.on(pe.matmul(gn_bank(t), blk, sqr(t), start=True, stop=True))

                mean(0)
                mean(1)
                broadcast(0)
                mean(2)
                mean(3)
                broadcast(1)
                var(0)
                var(1)
                broadcast(2)
                var(2)
                var(3)
                for t in range(4):
                    pe.wait_ge(root_ready.sem, root_ready.at(t + 1))
                    g_mm.on(pe.matmul(gn_bank(t), g2[:, t * P:(t + 1) * P], xr(13)[:, 0:SEQ], start=True, stop=True))
                broadcast(3)
                broadcast(4)
                pe.wait_ge(norm_a.sem, norm_a.at(1))
                mean_mm.on(pe.matmul(ps[0][:, 0:32], blk, ysm, start=True, stop=True))
                for t in range(4):
                    mm = pe.matmul(ps[1][:, 512 + 8 * t:520 + 8 * t], g2[:, t * P:(t + 1) * P], xr(13)[:, SEQ:T],
                                   start=True, stop=True)
                g_mm.on(mm)
                pe.wait_ge(sq_ready.sem, sq_ready.at(5))
                var_mm.on(pe.matmul(ps[0][:, 512:544], blk, ysq, start=True, stop=True))

            @block.scalar
            def _(act):
                for t in range(4):
                    act.wait_ge(cent.sem, cent.at(t + 1))
                    sq_ready.on(act.activation(sqr(t), yr[:, t, 0:SEQ], ACT.Square))
                for t in range(4):
                    act.wait_ge(var_mm.sem, var_mm.at(t + 1))
                    root_ready.on(act.activation(sqr(t), gn_bank(t), ACT.Sqrt, bias=small[:, 1:2], scale=1.0 / 64))
                for t in range(4):
                    act.wait_ge(g_mm.sem, g_mm.at(t + 1))
                    g_read.on(act.activation(gb(t), gn_bank(t), ACT.Copy))
                act.wait_ge(cent.sem, cent.at(5))
                sq_ready.on(act.activation(ysq, ysm, ACT.Square))
                act.wait_ge(var_mm.sem, var_mm.at(5))
                root_ready.on(act.activation(ysq, ps[0][:, 512:544], ACT.Sqrt, bias=small[:, 1:2], scale=1.0 / 64))

            @block.gpsimd
            def _(pool):
                S = Serial(pool, pool_step)
                for n, kind in enumerate((SKK, SD, SBB, SK, SR)):
                    if n:
                        pool.wait_ge(bc_mm.sem, bc_mm.at(n))
                    S(pool.tensor_tensor(b4(DG), i64.unsqueeze(1).unsqueeze(1).broadcast_to([P, NS, 4, 64]),
                                         per_bt(kind), ALU.mult), dg_ready)
                for t in range(4):
                    y = yr[:, t, 0:SEQ]
                    pool.wait_ge(scaled.sem, scaled.at(t + 1))
                    S(pool.tensor_scalar(y, y, v("ln_w", t), v("ln_b", t), ALU.mult, ALU.add))
                    S(pool.tensor_tensor(y, y, xr(4 + t)[:, 0:SEQ], ALU.add))
                    pool.wait_ge(g_read.sem, g_read.at(t + 1))
                    S(pool.tensor_tensor(y, y, gb(t), ALU.mult))

            @block.vector
            def _(dve):
                S = Serial(dve, norm_b)

                def halves():
                    for r in range(2):
                        yield slice(1024 * r, 1024 * r + 1024), ps[r][:, :], slice(16 * r, 16 * r + 16)

                def wait_bc(n):
                    dve.wait_ge(bc_mm.sem, bc_mm.at(n))

                def center(t):
                    dve.wait_ge(mean_mm.sem, mean_mm.at(t + 1))
                    S(dve.scalar_tensor_tensor(out=yr[:, t, 0:SEQ], in0=gn_bank(t), scalar=-1.0 / 64,
                                               in1=yr[:, t, 0:SEQ], op0=ALU.mult, op1=ALU.add), cent)

                def scale(t):
                    dve.wait_ge(root_ready.sem, root_ready.at(t + 1))
                    S(dve.reciprocal(sqr(t), sqr(t)))
                    S(dve.tensor_tensor(yr[:, t, 0:SEQ], yr[:, t, 0:SEQ], sqr(t), ALU.mult), scaled)

                center(0)
                center(1)
                dve.wait_ge(st_in.sem, st_in.count)
                wait_bc(1)
                for c, bc, r in halves():
                    S(dve.tensor_tensor(T1[:, c], S0[:, c], bc, ALU.mult), bc_read if c.start else None)
                S(dve.tensor_reduce(row, btk(T1), AX.X, ALU.add))
                center(2)
                center(3)
                wait_bc(2)
                for c, bc, r in halves():
                    S(dve.tensor_tensor(S1[:, c], S0[:, c], bc, ALU.mult), bc_read if c.start else None)
                scale(0)
                wait_bc(3)
                for c, bc, r in halves():
                    S(dve.tensor_tensor(btk(T1[:, c]), btk(bc), row[:, r].unsqueeze(2).broadcast_to([P, 16, 64]), ALU.mult),
                      bc_read if c.start else None)
                S(dve.tensor_tensor(S1, S1, T1, ALU.subtract))
                S(dve.tensor_copy(row.rearrange("p (b t) -> p b t", b=NS), smp[:, SV].rearrange("p t b -> p b t")))
                scale(1)
                wait_bc(4)
                for c, bc, r in halves():
                    S(dve.tensor_tensor(btk(T1[:, c]), btk(bc), row[:, r].unsqueeze(2).broadcast_to([P, 16, 64]), ALU.mult),
                      bc_read if c.start else None)
                S(dve.tensor_tensor(S1, S1, T1, ALU.add), dve_step)
                wait_bc(5)
                for c, bc, r in halves():
                    S(dve.tensor_tensor(T1[:, c], S1[:, c], bc, ALU.mult), bc_read if c.start else None)
                S(dve.tensor_reduce(row, btk(T1), AX.X, ALU.add))
                S(dve.tensor_copy(tb_(ysm), row.rearrange("p (b t) -> p t b", b=NS)), norm_a)
                scale(2)
                dve.wait_ge(mean_mm.sem, mean_mm.at(5))
                S(dve.scalar_tensor_tensor(out=ysm, in0=ps[0][:, 0:32], scalar=-1.0 / 64, in1=ysm,
                                           op0=ALU.mult, op1=ALU.add), cent)
                scale(3)
                dve.wait_ge(root_ready.sem, root_ready.at(5))
                S(dve.reciprocal(ysq, ysq))
                S(dve.tensor_tensor(ysm, ysm, ysq, ALU.mult))
                for t in range(4):
                    yt = ysm[:, 8 * t:8 * t + 8]
                    S(dve.tensor_scalar(yt, yt, v("ln_w", t), v("ln_b", t), ALU.mult, ALU.add))
                S(dve.tensor_tensor(tb_(ysm), tb_(ysm), xk4[:, :, SEQ:T], ALU.add))
                dve.wait_ge(g_mm.sem, g_mm.at(5))
                S(dve.tensor_tensor(yr[:, :, SEQ:T], tb_(ysm), tb_(ps[1][:, 512:544]), ALU.mult))
        end_of_block()

        silu_done, hid_done = signal("silu_done"), signal("hid_done")
        emb_in = signal("emb_in")
        tmp2 = lambda n: C[:, (n % 2) * T:(n % 2) * T + T]
        hid = lambda k: B[:, k * T:(k + 1) * T]

        def slab_rows(name, n):
            return i[name][bass.ds(n * P, P), :]

        def prefetch(sp, q0, name, count=RING):
            for q in range(count):
                load_slab(sp, q0 + q, slab_rows(name, q))

        def out_block(q0, name, rhs, nxt):
            with nc.Block() as block:
                @block.sync
                def _(sp):
                    for m in range(RING, KD):
                        load_slab(sp, q0 + m, slab_rows(name, m))
                    if nxt:
                        prefetch(sp, q0 + KD, nxt)

                @block.tensor
                def _(pe):
                    for m in range(KD):
                        wait_slab(pe, q0 + m)
                        if m >= 4:
                            pe.wait_ge(evac.sem, evac.at(m - 3))
                        slab_used.on(product(pe, pt(m), slot(q0 + m), KD, rhs))

                @block.vector
                def _(dve):
                    for m in range(KD):
                        dve.wait_ge(slab_used.sem, q0 + m + 1)
                        evac.on(dve.tensor_tensor(h3[:, m, :], pt(m), h3[:, m, :], ALU.add))
                        if m >= 2:
                            add_square(dve, m - 1)
                    add_square(dve, KD - 1)

                @block.scalar
                def _(act):
                    for m in range(KD):
                        act.wait_ge(evac.sem, evac.at(m + 1))
                        square(act, m)
            squares_counted()
            end_of_block()

        def ffn_block(gain):
            PEEL, PER, TRIPS = 4, 6, 3
            DPEEL, DPER, DTRIPS = 2, 3, 2

            def hidden_tiles(e, body):
                for m in range(PEEL):
                    body(m, None)
                with e.Fori(0, TRIPS) as turn:
                    for j in range(PER):
                        body(PEEL + j, turn)

            def down_tiles(e, body):
                for m in range(DPEEL):
                    body(m, None)
                with e.Fori(0, DTRIPS) as turn:
                    for j in range(DPER):
                        body(DPEEL + j, turn)

            def nth(n, turn, per):
                return n if turn is None else n + per * turn

            with nc.Block() as block:
                @block.sync
                def _(sp):
                    for n in range(RING, 2 * PEEL):
                        load_slab(sp, Q_GU + n, slab_rows("w_gu", n))
                    with sp.Fori(0, TRIPS) as turn:
                        for j in range(2 * PER):
                            n = 2 * PEEL + j
                            load_slab(sp, Q_GU + n, slab_rows("w_gu", n + 2 * PER * turn), (turn, 2 * PER))
                    for n in range(2 * DPEEL):
                        load_slab(sp, Q_DN + n, slab_rows("w_dn", n))
                    with sp.Fori(0, DTRIPS) as turn:
                        for j in range(2 * DPER):
                            n = 2 * DPEEL + j
                            load_slab(sp, Q_DN + n, slab_rows("w_dn", n + 2 * DPER * turn), (turn, 2 * DPER))
                    prefetch(sp, Q_PLE0, "w_ple0")

                @block.tensor
                def _(pe):
                    def hidden(m, turn):
                        k = None if turn is None else (turn, 2 * PER)
                        if m >= 2:
                            pe.wait_ge(hid_done.sem, hid_done.at(nth(m - 1, turn, PER)))
                        for s in range(2):
                            wait_slab(pe, Q_GU + 2 * m + s, k)
                            product(pe, pt(2 * (m % 2) + s), slot(Q_GU + 2 * m + s), KD,
                                    normed(pe) if m == 0 and s == 0 else lambda n: u3[:, n, :]).then_inc(slab_used.sem, 1)

                    norm_pe(pe)
                    hidden_tiles(pe, hidden)

                    def down(m, turn):
                        k = None if turn is None else (turn, 2 * DPER)
                        if m < DPEEL:
                            pe.wait_ge(hid_done.sem, hid_done.at(KF))
                        if m >= 2:
                            pe.wait_ge(evac.sem, evac.at(nth(m - 2, turn, DPER)))
                        for s in range(2):
                            wait_slab(pe, Q_DN + 2 * m + s, k)
                            product(pe, pt(m), slot(Q_DN + 2 * m + s), KF // 2, lambda n: hid(s * (KF // 2) + n),
                                    first=s == 0, last=s == 1).then_inc(slab_used.sem, 1)

                    down_tiles(pe, down)

                @block.scalar
                def _(act):
                    def silu(m, turn):
                        act.wait_ge(slab_used.sem, nth(Q_GU + 2 * m + 1, turn, 2 * PER))
                        if m >= 2:
                            act.wait_ge(hid_done.sem, hid_done.at(nth(m - 1, turn, PER)))
                        act.activation(tmp2(m), pt(2 * (m % 2)), ACT.Silu).then_inc(silu_done.sem, 1)

                    norm_act(act)
                    hidden_tiles(act, silu)
                    silu_done.add(KF)

                    def squares(m, turn):
                        act.wait_ge(evac.sem, evac.at(nth(m + 1, turn, DPER)))
                        if turn is None:
                            square(act, m)
                        else:
                            square(act, m, h_sb[:, bass.ds(m * T + (DPER * T) * turn, T)], DPER * turn, True)

                    down_tiles(act, squares)

                @block.vector
                def _(dve):
                    def gate(m, turn):
                        dve.wait_ge(silu_done.sem, silu_done.at(nth(m + 1, turn, PER)))
                        dve.wait_ge(slab_used.sem, nth(Q_GU + 2 * m + 2, turn, 2 * PER))
                        dst = hid(m) if turn is None else B[:, bass.ds(m * T + (PER * T) * turn, T)]
                        dve.tensor_tensor(dst, tmp2(m), pt(2 * (m % 2) + 1), ALU.mult).then_inc(hid_done.sem, 1)

                    norm_dve(dve, gain)
                    hidden_tiles(dve, gate)
                    hid_done.add(KF)

                    def add(m, turn):
                        dve.wait_ge(slab_used.sem, nth(Q_DN + 2 * m + 2, turn, 2 * DPER))
                        dst = h3[:, m, :] if turn is None else h_sb[:, bass.ds(m * T + (DPER * T) * turn, T)]
                        dve.tensor_tensor(dst, pt(m), dst, ALU.add).then_inc(evac.sem, 1)
                        if m >= 2:
                            add_square(dve, m - 1, DPER * turn, True)

                    down_tiles(dve, add)
                    add_square(dve, KD - 1)
                    evac.add(KD)
            squares_counted()
            slab_used.add(2 * KF + 2 * KD)
            for q in range(Q_GU + 2 * PEEL + 2 * PER, Q_DN):
                slab_in[q % RING].add(16)
            for q in range(Q_DN + 2 * DPEEL + 2 * DPER, Q_PLE0):
                slab_in[q % RING].add(16)
            end_of_block()

        def ple_block(q0, layer, nxt, gain):
            emb = A[:, 0:2 * T].rearrange("p (k t) -> p k t", t=T)
            with nc.Block() as block:
                @block.sync
                def _(sp):
                    for m in range(RING, KD):
                        load_slab(sp, q0 + m, slab_rows(f"w_ple{layer}", m))
                    if nxt:
                        prefetch(sp, q0 + KD, nxt)

                @block.gpsimd
                def _(pool):
                    emb_in.on(pool.dma_start(emb, i["p"][layer]), 16)

                @block.tensor
                def _(pe):
                    def project(m):
                        return product(pe, pt(2 * (m % 2) + 1), slot(q0 + m)[:, KD * P:], 2, lambda k: emb[:, k, :])

                    norm_pe(pe)
                    pe.wait_ge(emb_in.sem, emb_in.at(16))
                    for m in range(2):
                        wait_slab(pe, q0 + m)
                        project(m)
                    for m in range(KD):
                        wait_slab(pe, q0 + m)
                        if m >= 2:
                            pe.wait_ge(evac.sem, evac.at(m - 1))
                            project(m)
                        slab_used.on(product(pe, pt(2 * (m % 2)), slot(q0 + m), KD,
                                             lambda k: u3[:, k, :] if m else normed(pe)(k)))

                @block.scalar
                def _(act):
                    norm_act(act)
                    for m in range(KD + 1):
                        if m < KD:
                            act.wait_ge(slab_used.sem, q0 + m + 1)
                            if m >= 2:
                                act.wait_ge(evac.sem, evac.at(m - 1))
                            silu_done.on(act.activation(tmp2(m), pt(2 * (m % 2)), ACT.Sigmoid))
                        if m:
                            act.wait_ge(evac.sem, evac.at(m))
                            square(act, m - 1)

                @block.vector
                def _(dve):
                    norm_dve(dve, gain)
                    S = Serial(dve, dve_step)
                    for m in range(KD):
                        dve.wait_ge(silu_done.sem, silu_done.at(m + 1))
                        S(dve.tensor_tensor(tmp2(m), tmp2(m), pt(2 * (m % 2) + 1), ALU.mult))
                        evac.on(dve.tensor_tensor(h3[:, m, :], tmp2(m), h3[:, m, :], ALU.add))
                        if m >= 2:
                            add_square(dve, m - 1)
                    add_square(dve, KD - 1)
            squares_counted()
            end_of_block()

        out_block(Q_OUT0, "w_out_ab", lambda k: ga(k) if k < 4 else yr[:, k - 4, 0:T], "w_gu")
        ffn_block("norm_ffn0")
        ple_block(Q_PLE0, 0, "w_in_cd", "norm_ple0")

        G0 = 8 * PAD
        qt = lambda t: A[:, G0 + t * T:G0 + (t + 1) * T]
        kt = lambda t: A[:, G0 + (2 + t) * T:G0 + (3 + t) * T]
        vt = lambda t: A[:, G0 + (4 + t) * T:G0 + (5 + t) * T]
        zt = lambda t: A[:, G0 + (8 + t) * T:G0 + (9 + t) * T]
        gt = lambda t: A[:, G0 + (12 + t) * T:G0 + (13 + t) * T]
        sm = A[:, G0 + 16 * T:G0 + 17 * T]
        KN = lambda t: C[:, t * SEQ:(t + 1) * SEQ]
        tq = lambda n: C[:, 1024 + n * 548:1024 + n * 548 + 548]
        cum, dtr = C[0:8, 3216:3728], C[0:8, 3728:4248]
        col8 = 0
        parts = {}
        for name, width in (("sel8", 1024), ("selp", 512), ("last", P), ("ssdmask", P), ("glamask", P),
                            ("reset128", SEQ), ("reset32", SEQ), ("alpha", 256), ("router", 64), ("reset8", 40), ("iota", P), ("index", 1), ("before", NEXP)):
            parts[name] = Dm[:, col8:col8 + width]
            col8 += width
        sel8 = lambda n: parts["sel8"][0:8, n * P:(n + 1) * P]
        selp = lambda t: parts["selp"][0:8, t * P:(t + 1) * P]
        s_hist = stage[:, 0:192].rearrange("p (t b k) -> p t b k", t=8, b=NS)
        o2_convp = stage[:, 192:216].rearrange("p (t k) -> p t k", t=8)
        o2_convs = stage[:, 216:408].rearrange("p (t b k) -> p t b k", t=8, b=NS)
        cumT, dtT, cend, ecend, wend = [small[:, 4 + 32 * n:36 + 32 * n] for n in range(5)]
        dts, las = [small[:, 164 + 32 * n:196 + 32 * n].rearrange("p (t b) -> p t b", t=4) for n in range(2)]
        gdec = small[:, 228:260].rearrange("p (t c) -> p t c", t=2)
        gds = small[:, 260:276].rearrange("p (t b) -> p t b", t=2)
        aneg, las8 = small[0:8, 276:277], small[0:8, 277:285]
        conv_done, dt_exp, dt_ready = map(signal, ("conv_done", "dt_exp", "dt_ready"))
        al_mm, al_log, al_read, cs2_ready, ex2_ready, gla_read = map(signal, (
            "al_mm", "al_log", "al_read", "cs2_ready", "ex2_ready", "gla_read"))
        with nc.Block() as block:
            @block.sync
            def _(sp):
                loaded.on(sp.dma_start(Dm[:, 0:col8], i["ph_cd"]), 16)
                loaded.on(sp.dma_start(stage[:, 0:192], i["st_cd"]), 16)
                for m in range(RING, NCD):
                    load_slab(sp, Q_CD + m, slab_rows("w_in_cd", m))
                prefetch(sp, Q_OUT1, "w_out_cd")

            @block.gpsimd
            def _(pool):
                S = Serial(pool, pool_step)
                xa8 = A[:, 0:8 * PAD].rearrange("p (t c) -> p t c", t=8)
                S(pool.memset(xa8[:, :, 0:3], 0.0))
                pool.wait_ge(loaded.sem, loaded.count)
                for t in range(8):
                    S(pool.tensor_copy(xa8[:, t, SAMP:PAD].rearrange("p (b k) -> p b k", k=4)[:, :, 0:3], s_hist[:, t]))
                    S(pool.tensor_copy(o2_convs[:, t, :, 0:2], s_hist[:, t, :, 1:3]))
                setup_done.on(pool.memset(small[:, 3:4], 0.0))

            @block.tensor
            def _(pe):
                norm_pe(pe)
                for m in range(NCD):
                    wait_slab(pe, Q_CD + m)
                    if m >= 2:
                        pe.wait_ge(evac.sem, evac.at(m - 1))
                    slab_used.on(product(pe, pt(m % 2), slot(Q_CD + m), KD, lambda k: u3[:, k, :] if m else normed(pe)(k),
                                         width=48 if m == 0 else P))
                    if m in (10, 13):
                        t = (m - 10) // 3
                        pe.wait_ge(evac.sem, evac.at(1))
                        if t:
                            pe.wait_ge(al_read.sem, al_read.at(t))
                        for a in (0, HALF):
                            mm = pe.matmul(pt(2)[:, a:a + HALF], parts["alpha"][32:48, t * P:(t + 1) * P],
                                           sm[32:48, a:a + HALF], start=True, stop=True)
                        al_mm.on(mm)

            @block.scalar
            def _(act):
                S = Serial(act, act_step)
                norm_act(act)
                act.wait_ge(setup_done.sem, setup_done.at(1))
                S(act.activation(aneg, v("a_log")[0:8], ACT.Exp))
                for m in range(NCD):
                    act.wait_ge(slab_used.sem, Q_CD + m + 1)
                    src = pt(m % 2)
                    if m == 0:
                        S(act.activation(sm[0:48], src[0:48], ACT.Copy), evac)
                        S(act.activation(dtr, sm[0:8], ACT.Identity, bias=v("dt_bias")[0:8]))
                        S(act.activation(tq(0)[0:8, 0:T], dtr, ACT.Abs))
                        S(act.activation(tq(0)[0:8, 0:T], tq(0)[0:8, 0:T], ACT.Exp, scale=-1.0), dt_exp)
                    elif m < 9:
                        n = m - 1
                        act_step.on(act.activation(xa(n)[:, 3:3 + SEQ], src[:, 0:SEQ], ACT.Copy))
                        act_step.on(act.activation(xa(n)[:, SAMP + 3:PAD:4], src[:, SEQ:T], ACT.Copy))
                        act_step.on(act.activation(o2_convp[:, n, :], src[:, SEQ - 3:SEQ], ACT.Copy))
                        evac.on(act.activation(o2_convs[:, n, :, 2], src[:, SEQ:T], ACT.Copy))
                    elif m < 17:
                        evac.on(act.activation(A[:, G0 + (m - 9) * T:G0 + (m - 8) * T], src, ACT.Copy))
                    else:
                        evac.on(act.activation(A[:, G0 + (m - 9) * T:G0 + (m - 8) * T], src, ACT.Silu))
                    if m in (11, 14):
                        t = (m - 11) // 3
                        if t:
                            act.wait_ge(gla_read.sem, gla_read.at(t))
                        else:
                            act.wait_ge(dt_ready.sem, dt_ready.at(1))
                        act.wait_ge(al_mm.sem, al_mm.at(t + 1))
                        S(act.activation(tq(2)[:, 0:T], pt(2), ACT.Abs, bias=v("alpha_b", t)))
                        S(act.activation(tq(2)[:, 0:T], tq(2)[:, 0:T], ACT.Exp, scale=-1.0))
                        S(act.activation(tq(2)[:, 0:T], tq(2)[:, 0:T], ACT.Ln, bias=small[:, 2:3]), al_log)
                        act.wait_ge(cs2_ready.sem, cs2_ready.at(t + 1))
                        S(act.activation(tq(3)[:, 0:SEQ], tq(1)[:, 0:SEQ], ACT.Exp, scale=1.0 / 16))
                        S(act.activation(tq(1)[:, 0:SEQ], tq(1)[:, 0:SEQ], ACT.Exp, scale=-1.0 / 16))
                        S(act.activation(gds[:, t, :], tq(2)[:, SEQ:T], ACT.Exp, scale=1.0 / 16))
                        S(act.activation(tq(2)[:, 0:SEQ], tq(2)[:, 0:SEQ], ACT.Exp, scale=1.0 / 16), ex2_ready)
                    if 3 <= m < 11:
                        n = m - 3
                        act.wait_ge(conv_done.sem, conv_done.at(n + 1))
                        S(act.activation(xa(n)[:, 0:T], xa(n)[:, 0:T], ACT.Silu))

            @block.vector
            def _(dve):
                S = Serial(dve, dve_step)
                norm_dve(dve, "norm_mix1")
                dve.wait_ge(dt_exp.sem, dt_exp.at(1))
                softplus_small(dve, S, dtr, tq(0)[0:8, 0:T], tq(1)[0:8, 0:T], tq(2)[0:8, 0:T], 1.0)
                S(dve.tensor_scalar(aneg, aneg, -1.0, None, ALU.mult))
                S(dve.tensor_scalar(tq(0)[0:8, 0:T], dtr, aneg, None, ALU.mult))
                S(dve.tensor_copy(las8, tq(0)[0:8, SEQ:T]))
                S(dve.tensor_tensor_scan(cum, parts["reset128"][0:8, :], tq(0)[0:8, 0:SEQ], 0.0, ALU.mult, ALU.add), dt_ready)

                def conv(n):
                    w = lambda k: v("ssd_w", 8 * k + n)
                    x, y = xa(n), tq(0)
                    dve.wait_ge(evac.sem, evac.at(n + 2))
                    S(dve.tensor_scalar(y[:, 0:544], x[:, 3:547], w(3), v("ssd_b", n), ALU.mult, ALU.add))
                    for k in (2, 1):
                        S(dve.scalar_tensor_tensor(out=y[:, 0:544], in0=x[:, k:k + 544], scalar=w(k),
                                                   in1=y[:, 0:544], op0=ALU.mult, op1=ALU.add))
                    S(dve.scalar_tensor_tensor(out=x[:, SEQ:T], in0=x[:, SAMP:PAD:4], scalar=w(0),
                                               in1=y[:, SAMP:544:4], op0=ALU.mult, op1=ALU.add))
                    S(dve.scalar_tensor_tensor(out=x[:, 0:SEQ], in0=x[:, 0:SEQ], scalar=w(0),
                                               in1=y[:, 0:SEQ], op0=ALU.mult, op1=ALU.add), conv_done)

                def decay(t):
                    la, cs, to_end = tq(2)[:, 0:T], tq(1)[:, 0:SEQ], tq(2)[:, 0:SEQ]
                    dve.wait_ge(al_log.sem, al_log.at(t + 1))
                    S(dve.tensor_scalar(tq(3)[:, 0:T], pt(2), v("alpha_b", t), 0.0, ALU.add, ALU.min), al_read)
                    S(dve.tensor_tensor(la, tq(3)[:, 0:T], la, ALU.subtract))
                    S(dve.tensor_tensor_scan(cs, parts["reset32"], la[:, 0:SEQ], 0.0, ALU.mult, ALU.add))
                    c32 = cs.rearrange("p (c q) -> p c q", q=32)
                    S(dve.tensor_tensor(to_end.rearrange("p (c q) -> p c q", q=32),
                                        c32[:, :, 31:32].broadcast_to([P, 16, 32]), c32, ALU.subtract), cs2_ready)

                def gla_ready(t):
                    dve.wait_ge(ex2_ready.sem, ex2_ready.at(t + 1))
                    dve.wait_ge(evac.sem, evac.at(12 + t))
                    S(dve.tensor_copy(gdec[:, t, :], tq(3)[:, 31:SEQ:32]))
                    S(dve.tensor_tensor(KN(t), kt(t)[:, 0:SEQ], tq(2)[:, 0:SEQ], ALU.mult))
                    S(dve.tensor_tensor(kt(t)[:, 0:SEQ], kt(t)[:, 0:SEQ], tq(1)[:, 0:SEQ], ALU.mult))
                    S(dve.scalar_tensor_tensor(out=qt(t)[:, 0:SEQ], in0=qt(t)[:, 0:SEQ], scalar=0.125,
                                               in1=tq(3)[:, 0:SEQ], op0=ALU.mult, op1=ALU.mult))
                    S(dve.tensor_scalar(qt(t)[:, SEQ:T], qt(t)[:, SEQ:T], 0.125, None, ALU.mult), gla_read)

                for n in range(8):
                    conv(n)
                decay(0)
                gla_ready(0)
                decay(1)
                gla_ready(1)
        end_of_block()

        NC = SEQ // P
        BT0, CT0 = 4, 6
        XD = B[:, 0:2048].rearrange("p (c h q) -> p c h q", c=NC, h=8)
        WX = B[:, 2048:4096].rearrange("p (c h q) -> p c h q", c=NC, h=8)
        BTt = B[:, 4096:5120].rearrange("p (g c n) -> p g c n", g=2, c=NC)
        CB = B[:, 5120:6144].rearrange("p (g c n) -> p g c n", g=2, c=NC)
        ST = B[:, 6144:8192].rearrange("p (c h q) -> p c h q", c=NC, h=8)
        EB = lambda n: B[:, 8192 + 512 * (n % 2):8704 + 512 * (n % 2)]
        SG2 = lambda n: B[:, 9216 + 512 * (n % 2):9728 + 512 * (n % 2)]
        CE = lambda n: B[:, 10240 + 512 * (n % 2):10752 + 512 * (n % 2)]
        c4 = lambda ap: ap.rearrange("p (c n) -> p c n", c=NC)
        names = ("x_tr", "xd", "b_tr", "b_cp", "cb_mm", "cb_cp", "t_tr", "t_cp", "end_mm", "end_ex", "wx", "s_mm",
                 "s_up", "bc", "eb", "dif", "seg", "m", "y_mm", "y_cp", "smp_mm", "smp_cp")
        q = {n: signal("ssd_" + n) for n in names}

        def wq(e, name, n):
            e.wait_ge(q[name].sem, q[name].at(n))

        def head_y(pe, n):
            t, hh = n // 2, n % 2
            wq(pe, "m", n + 1)
            wq(pe, "s_up", NC)
            if n >= 4:
                wq(pe, "y_cp", n // 2 - 1)
            bank = 512 * (t % 2)
            for c in range(NC):
                dst = ps[2][64 * hh:64 * hh + 64, bank + c * P:bank + (c + 1) * P]
                mm = pe.matmul(dst, XD[:, c, n, :], SG2(n)[:, c * P:(c + 1) * P], start=True, stop=c == 0)
                if c:
                    mm = pe.matmul(dst, ST[:, c - 1, n, :], CE(n)[:, c * P:(c + 1) * P], start=False, stop=True)
            q["y_mm"].on(mm)

        SS = u_sb[:, 0:4096]
        ss_b = SS.rearrange("p (b t n) -> p b t n", b=NS, t=4)
        SDG, SMP = C[:, 1024:3072], B[:, 2048:3072]
        srow = small[:, 300:332].rearrange("p (b t) -> p b t", b=NS)
        dtx = small[:, 332:364].rearrange("p (t b) -> p t b", t=4)
        x_smp = A[:, 0:4 * PAD].rearrange("p (t c) -> p t c", t=4)[:, :, SEQ:T]
        b_psum = lambda r: ps[(0, 3)[r // 2]][:, 512 * (r % 2):512 * (r % 2) + 512]
        p_bn = lambda ap: ap.rearrange("p (b n) -> p b n", b=NS)

        def ssd_broadcast(pe, n):
            pe.wait_ge(dg_ready.sem, dg_ready.at(n + 1))
            if n:
                pe.wait_ge(bc_read.sem, bc_read.at(n))
            else:
                wq(pe, "smp_cp", 1)
                wq(pe, "s_up", NC)
            for r in range(4):
                mm = pe.matmul(b_psum(r), ones, SDG[:, 512 * r:512 * r + 512], start=True, stop=True)
            bc_mm.on(mm)

        def ssd_diagonals(dve, S, n):
            for gq in range(2):
                S(dve.tensor_tensor(p_bn(SDG[:, 1024 * gq:1024 * gq + 1024]), ident.unsqueeze(1).broadcast_to([P, NS, P]),
                                    xa((BT0, CT0)[n] + gq)[:, SEQ:T].unsqueeze(2).broadcast_to([P, NS, P]), ALU.mult),
                  dg_ready if gq else None)

        def ssd_sample(dve, S, n):
            if n in (1, 2):
                dve.wait_ge(decayed.sem, decayed.at(1))
                dve.wait_ge(bc_mm.sem, bc_mm.at(1))
                for t in range(2 * n - 2, 2 * n):
                    S(dve.tensor_tensor(p_bn(SMP), p_bn(ps[(0, 3)[t // 2]][:, :]),
                                        dtx[:, t, :].unsqueeze(2).broadcast_to([P, NS, P]), ALU.mult),
                      bc_read if t == 3 else None)
                    S(dve.tensor_tensor(ss_b[:, :, t, :], ss_b[:, :, t, :], p_bn(SMP), ALU.add), norm_a if t == 3 else None)
            elif n in (4, 5):
                dve.wait_ge(bc_mm.sem, bc_mm.at(2))
                for t in range(2 * n - 8, 2 * n - 6):
                    S(dve.tensor_tensor(p_bn(SMP), p_bn(ps[(0, 3)[t // 2]][:, :]), ss_b[:, :, t, :], ALU.mult))
                    S(dve.tensor_reduce(srow[:, :, t], p_bn(SMP), AX.X, ALU.add))
            elif n == 6:
                for t in range(4):
                    S(dve.scalar_tensor_tensor(out=xa(t)[:, SEQ:T], in0=xa(t)[:, SEQ:T], scalar=v("ssd_d", t),
                                               in1=srow[:, :, t], op0=ALU.mult, op1=ALU.add))

        decayed = setup_done

        with nc.Block() as block:
            @block.sync
            def _(sp):
                st_in.on(sp.dma_start(SS, i["s_ssd"]), 16)
                stored.on(sp.dma_start(o["cd_small"], stage[:, 192:408]), 16)
                wq(sp, "s_up", NC)
                stored.on(sp.dma_start(o["ssd_p"], B[:, 6144 + 3 * 512:8192]), 16)
                sp.wait_ge(norm_a.sem, norm_a.at(1))
                stored.on(sp.dma_start(o["ssd_s"], SS), 16)
                sp.wait_ge(stored.sem, stored.count)

            @block.tensor
            def _(pe):
                for n, src in enumerate((cum, dtr)):
                    for c in range(NC):
                        mm = pe.transpose(ps[3][:, 32 * n + 8 * c:32 * n + 8 * c + 8], src[:, c * P:(c + 1) * P],
                                          ident[0:8, 0:8])
                q["t_tr"].on(mm)
                for c in range(NC):
                    if c >= 2:
                        wq(pe, "xd", c - 1)
                    for t in range(4):
                        mm = pe.transpose(ps[0][:, 512 * (c % 2) + t * P:512 * (c % 2) + (t + 1) * P],
                                          xa(t)[:, c * P:(c + 1) * P], ident)
                    q["x_tr"].on(mm)
                for gq in range(2):
                    for c in range(NC):
                        mm = pe.transpose(ps[1][:, 512 * gq + c * P:512 * gq + (c + 1) * P],
                                          xa(BT0 + gq)[:, c * P:(c + 1) * P], ident)
                q["b_tr"].on(mm)
                for gq in range(2):
                    for c in range(NC):
                        mm = pe.matmul(ps[2][:, 512 * gq + c * P:512 * gq + (c + 1) * P],
                                       xa(BT0 + gq)[:, c * P:(c + 1) * P], xa(CT0 + gq)[:, c * P:(c + 1) * P],
                                       start=True, stop=True)
                q["cb_mm"].on(mm)
                wq(pe, "t_cp", 2)
                q["end_mm"].on(pe.matmul(ps[3][:, 64:96], parts["last"], cumT, start=True, stop=True))
                wq(pe, "end_ex", 2)
                for n, src in enumerate((las8, dtr[:, SEQ:T])):
                    for t in range(4):
                        mm = pe.matmul(ps[3][:, 512 + 32 * n + 8 * t:512 + 32 * n + 8 * t + 8], selp(t), src,
                                       start=True, stop=True)
                q["smp_mm"].on(mm)
                wq(pe, "b_cp", 1)
                for c in range(NC):
                    wq(pe, "wx", c + 2)
                    if c >= 2:
                        wq(pe, "s_up", c - 1)
                    elif c == 0:
                        wq(pe, "xd", NC)
                    for gq in range(2):
                        mm = pe.matmul(ps[0][:, 512 * (c % 2) + 256 * gq:512 * (c % 2) + 256 * gq + 256],
                                       BTt[:, gq, c, :], B[:, 2048 + 512 * c + 256 * gq:2048 + 512 * c + 256 * gq + 256],
                                       start=True, stop=True)
                    q["s_mm"].on(mm)
                wq(pe, "cb_cp", 1)
                wq(pe, "smp_cp", 1)
                for n in range(8):
                    t, hh, gq = n // 2, n % 2, n // 4
                    if n >= 2:
                        wq(pe, "seg", n - 1)
                        wq(pe, "eb", n - 1)
                        wq(pe, "dif", n - 1)
                    q["bc"].on(pe.matmul(ps[1][:, 512 * (n % 2):512 * (n % 2) + 512], sel8(n), cum, start=True, stop=True))
                    if n == 0:
                        ssd_broadcast(pe, 0)
                        continue
                    head_y(pe, n - 1)
                    if n == 3:
                        ssd_broadcast(pe, 1)
                head_y(pe, 7)

            @block.gpsimd
            def _(pool):
                S = Serial(pool, pool_step)
                ssd_diagonals(pool, S, 0)
                wq(pool, "smp_cp", 1)
                S(pool.tensor_tensor(dtx, dts, x_smp, ALU.mult))
                pool.wait_ge(st_in.sem, st_in.count)
                for b in range(2):
                    half = SS[:, 2048 * b:2048 * b + 2048].rearrange("p (b t n) -> p b t n", b=4, t=4)
                    S(pool.tensor_tensor(half, half, las[:, :, 4 * b:4 * b + 4].rearrange("p t b -> p b t").unsqueeze(3)
                                         .broadcast_to([P, 4, 4, P]), ALU.mult), decayed if b else None)
                pool.wait_ge(bc_mm.sem, bc_mm.at(1))
                ssd_diagonals(pool, S, 1)

            @block.scalar
            def _(act):
                S = Serial(act, act_step)
                wq(act, "t_tr", 1)
                S(act.activation(cumT, ps[3][:, 0:32], ACT.Copy), q["t_cp"])
                S(act.activation(dtT, ps[3][:, 32:64], ACT.Copy), q["t_cp"])
                wq(act, "b_tr", 1)
                S(act.activation(B[:, 4096:5120], ps[1][:, :], ACT.Copy), q["b_cp"])
                wq(act, "cb_mm", 1)
                S(act.activation(B[:, 5120:6144], ps[2][:, :], ACT.Copy), q["cb_cp"])
                wq(act, "end_mm", 1)
                S(act.activation(cend, ps[3][:, 64:96], ACT.Copy), q["end_ex"])
                S(act.activation(ecend, ps[3][:, 64:96], ACT.Exp), q["end_ex"])
                wq(act, "wx", 1)
                S(act.activation(wend, wend, ACT.Exp), q["end_ex"])
                wq(act, "smp_mm", 1)
                S(act.activation(small[:, 196:228], ps[3][:, 512:544], ACT.Exp))
                S(act.activation(small[:, 164:196], ps[3][:, 544:576], ACT.Copy), q["smp_cp"])
                for n in range(8):
                    wq(act, "bc", n + 1)
                    if n >= 2:
                        wq(act, "m", n - 1)
                    q["eb"].on(act.activation(EB(n), ps[1][:, 512 * (n % 2):512 * (n % 2) + 512], ACT.Exp))
                    wq(act, "dif", n + 1)
                    q["seg"].on(act.activation(SG2(n), SG2(n), ACT.Exp))

            @block.vector
            def _(dve):
                S = Serial(dve, dve_step)
                wq(dve, "t_cp", 2)
                for c in range(NC):
                    wq(dve, "x_tr", c + 1)
                    S(dve.tensor_tensor(XD[:, c], ps[0][:, 512 * (c % 2):512 * (c % 2) + 512].rearrange("p (h q) -> p h q", h=8),
                                        dtT[:, 8 * c:8 * c + 8].unsqueeze(2).broadcast_to([P, 8, 64]), ALU.mult), q["xd"])
                wq(dve, "end_ex", 2)
                S(dve.tensor_tensor(wend, cend, cumT, ALU.subtract), q["wx"])
                wq(dve, "end_ex", 3)
                for c in range(NC):
                    S(dve.tensor_tensor(WX[:, c], XD[:, c], wend[:, 8 * c:8 * c + 8].unsqueeze(2).broadcast_to([P, 8, 64]),
                                        ALU.mult), q["wx"] if c < 3 else q["wx"])
                for c in range(NC):
                    wq(dve, "s_mm", c + 1)
                    inc = ps[0][:, 512 * (c % 2):512 * (c % 2) + 512].rearrange("p (h q) -> p h q", h=8)
                    if c:
                        S(dve.tensor_tensor(ST[:, c], ST[:, c - 1], ecend[:, 8 * c:8 * c + 8].unsqueeze(2).broadcast_to([P, 8, 64]), ALU.mult))
                        S(dve.tensor_tensor(ST[:, c], ST[:, c], inc, ALU.add), q["s_up"])
                    else:
                        S(dve.tensor_copy(ST[:, c], inc), q["s_up"])
                for n in range(9):
                    if n < 8:
                        t, gq = n // 2, n // 4
                        bank = ps[1][:, 512 * (n % 2):512 * (n % 2) + 512]
                        wq(dve, "eb", n + 1)
                        if n >= 2:
                            wq(dve, "y_mm", n - 1)
                        for c in range(NC):
                            ins = dve.scalar_tensor_tensor(
                                out=SG2(n)[:, c * P:(c + 1) * P], in0=bank[:, c * P:(c + 1) * P],
                                scalar=cumT[:, 8 * c + n:8 * c + n + 1], in1=parts["ssdmask"], op0=ALU.subtract, op1=ALU.min)
                            S(ins, q["dif"] if c == NC - 1 else None)
                        S(dve.tensor_tensor(CE(n), EB(n), xa(CT0 + gq)[:, 0:SEQ], ALU.mult))
                        wq(dve, "seg", n + 1)
                        S(dve.tensor_tensor(SG2(n), SG2(n), B[:, 5120 + 512 * gq:5632 + 512 * gq], ALU.mult), q["m"])
                    if n >= 2 and n % 2 == 0:
                        t = n // 2 - 1
                        wq(dve, "y_mm", n)
                        S(dve.scalar_tensor_tensor(out=xa(t)[:, 0:SEQ], in0=xa(t)[:, 0:SEQ], scalar=v("ssd_d", t),
                                                   in1=ps[2][:, 512 * (t % 2):512 * (t % 2) + 512],
                                                   op0=ALU.mult, op1=ALU.add), q["y_cp"])
                    ssd_sample(dve, S, n)
        end_of_block()


        VT = B[:, 0:2048].rearrange("p (c h n) -> p c h n", c=NC, h=4)
        KT = B[:, 2048:3072].rearrange("p (c t n) -> p c t n", c=NC, t=2)
        ATT = lambda h: B[:, 3072 + 512 * h:3584 + 512 * h]
        GS = B[:, 5120:9216].rearrange("p (t s n) -> p t s n", t=2, s=16)
        bank = lambda n: ps[n // 2][:, 512 * (n % 2):512 * (n % 2) + 512]
        ATT_BANK, O_BANK = (6, 7, 4, 5), (0, 1, 2, 3)
        v_tr, v_cp, k_tr, k_cp, att_mm, att_cp, inc_mm, state_up, o_mm = (
            q["x_tr"], q["xd"], q["b_tr"], q["b_cp"], q["cb_mm"], q["cb_cp"], q["s_mm"], q["s_up"], q["y_mm"])
        SQ = lambda n: B[:, 9216 + n * T:9216 + (n + 1) * T]
        yz, ysq, ysum, yroot = q["bc"], q["eb"], q["dif"], q["seg"]
        with nc.Block() as block:
            @block.sync
            def _(sp):
                st_in.on(sp.dma_start(u_sb[:, 0:2048], i["s_gla"]), 16)

            @block.tensor
            def _(pe):
                for c in range(NC):
                    for h in range(4):
                        mm = pe.transpose(bank(c)[:, h * P:(h + 1) * P], vt(h)[:, c * P:(c + 1) * P], ident)
                    v_tr.on(mm)
                for t in range(2):
                    for c in range(NC):
                        mm = pe.transpose(ps[2][:, (2 * c + t) * P:(2 * c + t + 1) * P], KN(t)[:, c * P:(c + 1) * P], ident)
                k_tr.on(mm)
                for h in range(4):
                    t, r = h // 2, slice(64 * (h % 2), 64 * (h % 2) + 64)
                    if h >= 2:
                        pe.wait_ge(k_cp.sem, k_cp.at(1))
                    for c in range(NC):
                        cc = slice(c * P, (c + 1) * P)
                        mm = pe.matmul(bank(ATT_BANK[h])[:, cc], kt(t)[r, cc], qt(t)[r, cc], start=True, stop=True)
                    att_mm.on(mm)
                pe.wait_ge(v_cp.sem, v_cp.at(4))
                for t in range(2):
                    if t:
                        pe.wait_ge(att_cp.sem, att_cp.at(4))
                    for s in range(16):
                        c, r = s // 4, slice(32 * (s % 4), 32 * (s % 4) + 32)
                        for hh in range(2):
                            mm = pe.matmul(bank(4 * t + s % 4)[64 * hh:64 * hh + 64, c * P:(c + 1) * P],
                                           KT[r, c, t, 64 * hh:64 * hh + 64], VT[r, c, 2 * t + hh, :], start=True, stop=True)
                    inc_mm.on(mm)
                for h in range(4):
                    t, r = h // 2, slice(64 * (h % 2), 64 * (h % 2) + 64)
                    pe.wait_ge(state_up.sem, state_up.at(t + 1))
                    if h == 2:
                        pe.wait_ge(ysq.sem, ysq.at(4))
                        for n in range(4):
                            mm = product(pe, pt(3), ones, 1, lambda k: SQ(n), first=n == 0, last=n == 3)
                        ysum.on(mm)
                    for c in range(NC):
                        dst = bank(O_BANK[h])
                        pe.matmul(dst[:, c * P:(c + 1) * P], VT[:, c, h, :], ATT(h)[:, c * P:(c + 1) * P],
                                  start=True, stop=False)
                        for s in range(4 * c, 4 * c + 4):
                            for half in range(2 if s else 0):
                                e = slice(64 * half, 64 * half + 64)
                                mm = pe.matmul(dst[e, 32 * s:32 * s + 32], GS[r, t, s - 1, e], qt(t)[r, 32 * s:32 * s + 32],
                                               start=False, stop=s % 4 == 3)
                    o_mm.on(mm)

            @block.scalar
            def _(act):
                for c in range(NC):
                    act.wait_ge(v_tr.sem, v_tr.at(c + 1))
                    v_cp.on(act.activation(B[:, 512 * c:512 * c + 512], bank(c), ACT.Copy))
                for n in range(4):
                    act.wait_ge(yz.sem, yz.at(n + 1))
                    ysq.on(act.activation(SQ(n), xa(n)[:, 0:T], ACT.Square))
                for h in range(4):
                    if h == 2:
                        act.wait_ge(ysum.sem, ysum.at(1))
                        yroot.on(act.activation(ROOT, pt(3), ACT.Sqrt, bias=small[:, 0:1], scale=1.0 / 512))
                    act.wait_ge(o_mm.sem, o_mm.at(h + 1))
                    act_step.on(act.activation(vt(h)[:, 0:SEQ], bank(O_BANK[h]), ACT.Copy))

            @block.vector
            def _(dve):
                S = Serial(dve, dve_step)
                for t in range(4):
                    yz.on(dve.tensor_tensor(xa(t)[:, 0:T], xa(t)[:, 0:T], zt(t), ALU.mult))
                dve.wait_ge(k_tr.sem, k_tr.at(1))
                k_cp.on(dve.tensor_copy(B[:, 2048:3072], ps[2][:, :]))
                for h in range(4):
                    dve.wait_ge(att_mm.sem, att_mm.at(h + 1))
                    att_cp.on(dve.tensor_tensor(c4(ATT(h)), c4(bank(ATT_BANK[h])),
                                                parts["glamask"].unsqueeze(1).broadcast_to([P, NC, P]), ALU.mult))
                for t in range(2):
                    for s in range(16):
                        inc = bank(4 * t + s % 4)[:, (s // 4) * P:(s // 4 + 1) * P]
                        if s == 0:
                            dve.wait_ge(inc_mm.sem, inc_mm.at(t + 1))
                        if s == 0:
                            S(dve.tensor_copy(GS[:, t, 0, :], inc))
                        else:
                            S(dve.scalar_tensor_tensor(out=GS[:, t, s, :], in0=GS[:, t, s - 1, :], scalar=gdec[:, t, s:s + 1],
                                                       in1=inc, op0=ALU.mult, op1=ALU.add), state_up if s == 15 else None)
                dve.wait_ge(yroot.sem, yroot.at(1))
                S(dve.reciprocal(RINV, ROOT))
                dve.wait_ge(yz.sem, yz.at(4))
                for t in range(4):
                    dve_step.on(dve.scalar_tensor_tensor(out=xa(t)[:, 0:T], in0=xa(t)[:, 0:T], scalar=v("ssd_norm", t),
                                                         in1=RINV, op0=ALU.mult, op1=ALU.mult))
        end_of_block()

        SG = u_sb[:, 0:2048]
        sg4 = SG.rearrange("p (b t n) -> p b t n", b=NS, t=2)
        VD = lambda hh: B[:, 2048 * hh:2048 * hh + 2048]
        KV = u_sb[:, 2048:4096].rearrange("p (b t n) -> p b t n", b=NS, t=2)
        vk = lambda t0, n: A[:, G0 + t0 * T:G0 + (t0 + n) * T].rearrange("p (t c) -> p t c", c=T)
        per_b = lambda ap: ap.rearrange("p t b -> p b t").unsqueeze(3).broadcast_to([P, NS, 2, P])
        SQH = lambda h: B[:, 9216 + h * SEQ:9216 + (h + 1) * SEQ]
        osm, osq = small[:, 300:332], small[:, 332:364]
        h_b = lambda ap: ap.rearrange("p (h b) -> p h b", b=NS)
        o_scaled, os_ready = q["wx"], q["m"]
        with nc.Block() as block:
            @block.sync
            def _(sp):
                for t in range(2):
                    stored.on(sp.dma_start(o["gla_p"][:, t * P:(t + 1) * P], GS[:, t, 15, :]), 16)
                sp.wait_ge(dve_step.sem, dve_step.at(1))
                stored.on(sp.dma_start(o["gla_s"], SG), 16)
                sp.wait_ge(stored.sem, stored.count)

            @block.tensor
            def _(pe):
                for hh in range(2):
                    pe.wait_ge(dg_ready.sem, dg_ready.at(hh + 1))
                    for r in range(4):
                        mm = pe.matmul(bank(r)[64 * hh:64 * hh + 64, :], ones[:, 0:64], VD(hh)[:, 512 * r:512 * r + 512],
                                       start=True, stop=True)
                    bc_mm.on(mm)
                for h in range(4):
                    pe.wait_ge(ysq.sem, ysq.at(h + 1))
                    if h >= 2:
                        pe.wait_ge(yroot.sem, yroot.at(h - 1))
                    ysum.on(pe.matmul(bank(6 + h % 2), ones, SQH(h), start=True, stop=True))
                pe.wait_ge(dve_step.sem, dve_step.at(1))
                for hh in range(2):
                    r = slice(64 * hh, 64 * hh + 64)
                    for t in range(2):
                        for b in range(NS):
                            for half in range(2):
                                e = slice(64 * half, 64 * half + 64)
                                mm = pe.matmul(bank(4 + hh)[e, NS * t + b:NS * t + b + 1], sg4[r, b, t, e],
                                               qt(t)[r, SEQ + b:SEQ + b + 1], start=True, stop=True)
                o_mm.on(mm)
                pe.wait_ge(ysq.sem, ysq.at(5))
                ysum.on(pe.matmul(bank(0)[:, 0:32], ones, osq, start=True, stop=True))

            @block.scalar
            def _(act):
                for h in range(4):
                    ysq.on(act.activation(SQH(h), vt(h)[:, 0:SEQ], ACT.Square))
                for h in range(4):
                    act.wait_ge(ysum.sem, ysum.at(h + 1))
                    yroot.on(act.activation(SQH(h), bank(6 + h % 2), ACT.Sqrt, bias=small[:, 0:1], scale=1.0 / P))
                act.wait_ge(os_ready.sem, os_ready.at(1))
                ysq.on(act.activation(osq, osm, ACT.Square))
                act.wait_ge(ysum.sem, ysum.at(5))
                yroot.on(act.activation(osq, bank(0)[:, 0:32], ACT.Sqrt, bias=small[:, 0:1], scale=1.0 / P))

            @block.vector
            def _(dve):
                S = Serial(dve, norm_b)

                def scale(h):
                    o_h = vt(h)[:, 0:SEQ]
                    dve.wait_ge(yroot.sem, yroot.at(h + 1))
                    S(dve.reciprocal(SQH(h), SQH(h)))
                    S(dve.scalar_tensor_tensor(out=o_h, in0=o_h, scalar=v("gla_norm"), in1=SQH(h), op0=ALU.mult,
                                               op1=ALU.mult), o_scaled)

                for hh in range(2):
                    for t in range(2):
                        S(dve.tensor_tensor(VD(hh).rearrange("p (b t n) -> p b t n", b=NS, t=2)[:, :, t, :],
                                            ident.unsqueeze(1).broadcast_to([P, NS, P]),
                                            vt(2 * t + hh)[:, SEQ:T].unsqueeze(2).broadcast_to([P, NS, P]), ALU.mult),
                          dg_ready if t else None)
                dve.wait_ge(st_in.sem, st_in.count)
                S(dve.tensor_tensor(sg4, sg4, per_b(gds), ALU.mult))
                dve.wait_ge(bc_mm.sem, bc_mm.at(2))
                for n in range(2):
                    bs = slice(4 * n, 4 * n + 4)
                    S(dve.tensor_tensor(KV[:, bs], ps[n][:, :].rearrange("p (b t n) -> p b t n", b=4, t=2),
                                        per_b(vk(2, 2)[:, :, SEQ:T])[:, bs], ALU.mult))
                S(dve.tensor_tensor(sg4, sg4, KV, ALU.add), dve_step)
                for h in range(3):
                    scale(h)
                dve.wait_ge(o_mm.sem, o_mm.at(1))
                for hh in range(2):
                    S(dve.tensor_copy(osm.rearrange("p (t e b) -> p t e b", t=2, e=2)[:, :, hh, :],
                                      bank(4 + hh)[:, 0:2 * NS].rearrange("p (t b) -> p t b", t=2)),
                      os_ready if hh else None)
                scale(3)
                dve.wait_ge(yroot.sem, yroot.at(5))
                S(dve.reciprocal(osq, osq))
                S(dve.scalar_tensor_tensor(out=osm, in0=osm, scalar=v("gla_norm"), in1=osq, op0=ALU.mult, op1=ALU.mult))
                S(dve.tensor_tensor(vk(4, 4)[:, :, SEQ:T], h_b(osm), vk(12, 4)[:, :, SEQ:T], ALU.mult))

            @block.gpsimd
            def _(pool):
                for h in range(4):
                    pool.wait_ge(o_scaled.sem, o_scaled.at(h + 1))
                    pool_step.on(pool.tensor_tensor(vt(h)[:, 0:SEQ], vt(h)[:, 0:SEQ], gt(h)[:, 0:SEQ], ALU.mult))
        end_of_block()

        out_block(Q_OUT1, "w_out_cd", lambda k: xa(k)[:, 0:T] if k < 4 else vt(k - 4), None)

        NT = 5
        tile_w = lambda tt: P if tt < 4 else NS
        e3 = lambda n: small[:, 300 + 40 * n:340 + 40 * n]
        r5 = lambda n: small[:, 580 + 5 * n:585 + 5 * n]
        by_e = lambda ap: ap.rearrange("p (t e) -> p t e", e=NEXP)
        logit, prob, first1, first2, rest, scan = [e3(n) for n in range(6)]
        top, tot, top2 = r5(0), r5(1), r5(2)
        row8 = lambda ap: ap.unsqueeze(2).broadcast_to([P, NT, NEXP])
        token_pos = [small[:, 540 + 5 * n:545 + 5 * n] for n in range(2)]
        slot_id = small[:, 550:551]
        n_e, blocks, start128, end_e = [small[0:8, 551 + n:552 + n] for n in range(4)]
        block_cmp, block5 = small[0:8, 560:576], small[0:8, 600:605]
        U_TOK = lambda tt: A[:, 1024 * tt:1024 * (tt + 1)]
        place = [A[:, 5120 + n * T:5120 + (n + 1) * T] for n in range(2)]
        gate = [A[:, 5120 + (2 + n) * T:5120 + (3 + n) * T] for n in range(2)]
        GK = A[:, 7200:7200 + T]
        GT1 = A[:, 7720:7720 + T]
        XG = A[:, 8240:8240 + 1024]
        YS = A[:, 9264:9264 + 1024]
        PK = A[:, 10288:10288 + NT * P]
        HK = lambda f: B[:, f * P:(f + 1) * P]
        TMPH = lambda m: C[:, 128 * (m % 2):128 * (m % 2) + 128]
        row_t = lambda n: B[0:8, 2048 + n * T:2048 + (n + 1) * T]
        F1T, F2T, GTT, FT, CUM, POS, R0, R1, R2, R3 = [row_t(n) for n in range(10)]
        (rt_mm, rt_exp, rt_sub, rt_gate, rt_tr, rt_cp, rt_bc, u_tr, u_cp, nb_ready, bs_mm, rows_ready, ek_mm, pk_ready,
         xg_mm, xg_cp, y_cp, g_ready, sc_mm) = (q[n] for n in (
             "bc", "eb", "dif", "seg", "m", "y_mm", "y_cp", "x_tr", "xd", "b_tr", "b_cp", "cb_mm", "cb_cp", "t_tr",
             "t_cp", "end_mm", "end_ex", "wx", "s_mm"))

        gt_cp = q["s_up"]

        def build_places(dve, S, last=None):
            for tt in range(NT):
                w = tile_w(tt)
                dst = PK[0:w, tt * P:(tt + 1) * P]
                S(dve.tensor_scalar(dst, parts["iota"][0:w, :], token_pos[0][0:w, tt:tt + 1], None, ALU.is_equal))
                S(dve.scalar_tensor_tensor(out=dst, in0=parts["iota"][0:w, :], scalar=token_pos[1][0:w, tt:tt + 1],
                                           in1=dst, op0=ALU.is_equal, op1=ALU.add), last if tt == NT - 1 else None)

        with nc.Block() as block:
            @block.tensor
            def _(pe):
                norm_pe(pe)
                for tt in range(NT):
                    for k in range(KD):
                        if tt == 0:
                            pe.wait_ge(u_ready.sem, u_ready.at(k + 1))
                        for t0 in range(0, tile_w(tt), 64):
                            w = min(64, tile_w(tt))
                            mm = pe.matmul(ps[0][t0:t0 + w, 8 * tt:8 * tt + 8], u3[:, k, tt * P + t0:tt * P + t0 + w],
                                           parts["router"][:, 8 * k:8 * k + 8], start=k == 0, stop=k == KD - 1)
                rt_mm.on(mm)
                for tt in range(NT):
                    w = tile_w(tt)
                    if tt >= 2:
                        pe.wait_ge(u_cp.sem, u_cp.at(tt - 1))
                    for k in range(KD):
                        mm = pe.transpose(ps[2 + tt % 2][0:w, k * P:(k + 1) * P], u3[:, k, tt * P:tt * P + w], ident)
                    u_tr.on(mm)
                pe.wait_ge(rt_gate.sem, rt_gate.at(1))
                pe.wait_ge(u_cp.sem, u_cp.at(NT))
                for n, src in enumerate((first1, first2, prob)):
                    for tt in range(NT):
                        w = tile_w(tt)
                        mm = pe.transpose(ps[1 + n][0:8, tt * P:tt * P + w], src[0:w, 8 * tt:8 * tt + 8], ident[0:w, 0:w])
                rt_tr.on(mm)
                pe.wait_ge(nb_ready.sem, nb_ready.at(1))
                bs_mm.on(pe.matmul(ps[0][0:8, 40:41], parts["before"][0:8, :], blocks, start=True, stop=True))
                pe.wait_ge(nb_ready.sem, nb_ready.at(2))
                pe.matmul(ps[0][0:1, 64:80], ones[0:8, 0:1], block_cmp, start=True, stop=True)
                pe.matmul(ps[0][0:1, 80:81], ones[0:8, 0:1], blocks, start=True, stop=True)
                pe.wait_ge(rows_ready.sem, rows_ready.at(1))
                for n, row in enumerate((R0, R1)):
                    for tt in range(NT):
                        w = tile_w(tt)
                        mm = pe.matmul(ps[0][0:w, 96 + 5 * n + tt:97 + 5 * n + tt], row[:, tt * P:tt * P + w],
                                       ones[0:8, 0:1], start=True, stop=True)
                ek_mm.on(mm)
                for n, row in enumerate((R0, R1, R2, R3)):
                    if n == 3:
                        pe.wait_ge(rt_bc.sem, rt_bc.at(1))
                    rt_cp.on(product(pe, pt(1 + n % 3), ones[0:8, :], 1, lambda k: row))

            @block.scalar
            def _(act):
                norm_act(act)
                for tt in range(NT):
                    w = tile_w(tt)
                    if tt == 1:
                        act.wait_ge(rt_sub.sem, rt_sub.at(1))
                        rt_exp.on(act.activation(prob, logit, ACT.Exp))
                    act.wait_ge(u_tr.sem, u_tr.at(tt + 1))
                    u_cp.on(act.activation(U_TOK(tt)[0:w, :], ps[2 + tt % 2][0:w, :], ACT.Copy))
                act.wait_ge(rt_tr.sem, rt_tr.at(1))
                gt_cp.on(act.activation(GTT, ps[3][0:8, 0:T], ACT.Copy))
                for n, dst in enumerate(place + gate):
                    act.wait_ge(rt_cp.sem, rt_cp.at(n + 1))
                    rt_bc.on(act.activation(dst, pt(1 + n % 3), ACT.Copy))

            @block.vector
            def _(dve):
                S = Serial(dve, dve_step)

                def first_of(dst, src, peak):
                    S(dve.tensor_tensor(by_e(dst), by_e(src), row8(peak), ALU.is_equal))
                    S(dve.tensor_tensor_scan(scan, parts["reset8"], dst, 0.0, ALU.mult, ALU.add))
                    S(dve.scalar_tensor_tensor(out=dst, in0=scan, scalar=1.0, in1=dst, op0=ALU.is_equal, op1=ALU.mult))

                norm_dve(dve, "norm_ffn1")
                S(dve.memset(logit, 0.0))
                S(dve.memset(small[:, 540:550], 0.0))
                dve.wait_ge(rt_mm.sem, rt_mm.at(1))
                S(dve.tensor_copy(logit[:, 0:32], ps[0][:, 0:32]))
                S(dve.tensor_copy(logit[0:NS, 32:40], ps[0][0:NS, 32:40]))
                S(dve.tensor_reduce(top, by_e(logit), AX.X, ALU.max))
                S(dve.tensor_tensor(by_e(logit), by_e(logit), row8(top), ALU.subtract), rt_sub)
                dve.wait_ge(rt_exp.sem, rt_exp.at(1))
                S(dve.tensor_reduce(tot, by_e(prob), AX.X, ALU.add))
                S(dve.reciprocal(tot, tot))
                S(dve.tensor_tensor(by_e(prob), by_e(prob), row8(tot), ALU.mult))
                S(dve.tensor_reduce(top, by_e(prob), AX.X, ALU.max))
                first_of(first1, prob, top)
                S(dve.scalar_tensor_tensor(out=rest, in0=first1, scalar=-2.0, in1=prob, op0=ALU.mult, op1=ALU.add))
                S(dve.tensor_reduce(top2, by_e(rest), AX.X, ALU.max))
                first_of(first2, rest, top2)
                S(dve.tensor_tensor(tot, top, top2, ALU.add))
                S(dve.reciprocal(tot, tot))
                S(dve.tensor_tensor(by_e(prob), by_e(prob), row8(tot), ALU.mult), rt_gate)
                dve.wait_ge(rt_tr.sem, rt_tr.at(1))
                for n, dst in enumerate((F1T, F2T)):
                    S(dve.tensor_copy(dst, ps[1 + n][0:8, 0:T]))
                S(dve.tensor_tensor(FT, F1T, F2T, ALU.add))
                S(dve.tensor_tensor_scan(CUM, FT, FT, 0.0, ALU.add, ALU.max))
                S(dve.tensor_copy(n_e, CUM[:, T - 1:T]))
                S(dve.tensor_scalar(block5, parts["iota"][0:8, 0:5], float(P), n_e, ALU.mult, ALU.is_lt))
                S(dve.tensor_reduce(blocks, block5, AX.X, ALU.add), nb_ready)
                dve.wait_ge(bs_mm.sem, bs_mm.at(1))
                S(dve.tensor_tensor(end_e, ps[0][0:8, 40:41], blocks, ALU.add))
                S(dve.tensor_scalar(start128, ps[0][0:8, 40:41], float(P), None, ALU.mult))
                S(dve.tensor_scalar(block_cmp, parts["iota"][0:8, 0:MAXB], end_e, None, ALU.is_ge), nb_ready)
                S(dve.tensor_scalar(POS, CUM, start128, -1.0, ALU.add, ALU.add))
                S(dve.tensor_tensor(R0, F1T, POS, ALU.mult))
                S(dve.tensor_tensor(R1, F2T, POS, ALU.mult))
                dve.wait_ge(gt_cp.sem, gt_cp.at(1))
                S(dve.tensor_tensor(R2, F1T, GTT, ALU.mult))
                S(dve.tensor_tensor(R3, F2T, GTT, ALU.mult), rows_ready)
                S(dve.tensor_copy(slot_id, parts["index"]))
                dve.wait_ge(ek_mm.sem, ek_mm.at(1))
                S(dve.tensor_scalar(expert_of[0:1, 0:MAXB], ps[0][0:1, 64:80], float(NEXP - 1), None, ALU.min))
                S(dve.tensor_copy(expert_of[0:1, MAXB:MAXB + 1], ps[0][0:1, 80:81]))
                for n in range(2):
                    S(dve.tensor_copy(token_pos[n][:, 0:4], ps[0][:, 96 + 5 * n:100 + 5 * n]))
                    S(dve.tensor_copy(token_pos[n][0:NS, 4:5], ps[0][0:NS, 100 + 5 * n:101 + 5 * n]))
                build_places(dve, S, pk_ready)
        end_of_block()

        def moe_src(n, e):
            if n < 2 * KE:
                return i["w_moe_gu"][bass.ds(e * (2 * KE * P) + n * P, P), :]
            return i["w_moe_dn"][bass.ds(e * (KD * P) + (n - 2 * KE) * P, P), :]

        scatter_pt = lambda m: pt((0, 1, 3)[m % 3])
        hid_psum = lambda m, s: ps[m % 2][:, 512 * s:512 * s + P]
        N_PK = 2 * NT + 4
        def skip(e, counts):
            for s, n in counts:
                e.sem_inc(s.sem, n)

        with nc.Block() as block:
            @block.sync
            def _(sp):
                used = sp.value_load(expert_of[0:1, MAXB:MAXB + 1], min_val=1, max_val=MAXB)
                with sp.Fori(0, MAXB) as k:
                    with sp.If(k < used):
                        e = sp.value_load(expert_of[0:1, bass.ds(k, 1)], min_val=0, max_val=NEXP - 1)
                        for n in range(PER_E):
                            load_slab(sp, Q_MOE + n, moe_src(n, e), (k, PER_E))
                    with sp.Else():
                        sp.wait_ge(slab_used.sem, Q_MOE + PER_E * k)
                        skip(sp, [(s, 16 * (PER_E // RING)) for s in slab_in])
                prefetch(sp, Q_PLE1, "w_ple1")

            @block.tensor
            def _(pe):
                used = pe.value_load(expert_of[0:1, MAXB:MAXB + 1], min_val=1, max_val=MAXB)
                with pe.Fori(0, MAXB) as k:
                    with pe.If(k < used):
                        turn = (k, PER_E)
                        pe.wait_ge(pk_ready.sem, pk_ready.at(0) + k)
                        for m in range(KD):
                            for tt in range(NT):
                                w = tile_w(tt)
                                mm = pe.matmul(ps[2][:, m * P:(m + 1) * P], U_TOK(tt)[0:w, m * P:(m + 1) * P],
                                               PK[0:w, tt * P:(tt + 1) * P], start=tt == 0, stop=tt == NT - 1)
                            if m % 4 == 3:
                                mm.then_inc(xg_mm.sem, 1)
                        pe.wait_ge(evac.sem, evac.at(0) + KD * k)
                        for m in range(KE):
                            if m >= 2:
                                pe.wait_ge(hid_done.sem, hid_done.at(m - 1) + KE * k)
                            for s in range(2):
                                wait_slab(pe, Q_MOE + 2 * m + s, turn)
                                for f in range(KD):
                                    if m == 0 and s == 0 and f % 4 == 0:
                                        pe.wait_ge(xg_cp.sem, xg_cp.at(f // 4 + 1) + 2 * k)
                                    mm = pe.matmul(hid_psum(m, s), slot(Q_MOE + 2 * m + s)[:, f * P:(f + 1) * P],
                                                   XG[:, f * P:(f + 1) * P], start=f == 0, stop=f == KD - 1)
                                mm.then_inc(slab_used.sem, 1)
                        for m in range(KD):
                            wait_slab(pe, Q_MOE + 2 * KE + m, turn)
                            for f in range(KE):
                                if m == 0 and f in (0, KE - 1):
                                    pe.wait_ge(hid_done.sem, hid_done.at(KE - 1 if f == 0 else KE) + KE * k)
                                mm = pe.matmul(ps[2][:, m * P:(m + 1) * P], HK(f), slot(Q_MOE + 2 * KE + m)[:, f * P:(f + 1) * P],
                                               start=f == 0, stop=f == KE - 1)
                            mm.then_inc(slab_used.sem, 1)
                        pe.wait_ge(g_ready.sem, g_ready.at(1) + k)
                        for m in range(KD):
                            if m % 4 == 0:
                                pe.wait_ge(y_cp.sem, y_cp.at(m // 4 + 1) + 2 * k)
                            if m >= 3:
                                pe.wait_ge(evac.sem, evac.at(m - 2) + KD * k)
                            product(pe, scatter_pt(m), YS[:, m * P:(m + 1) * P], 1, lambda _: GK).then_inc(sc_mm.sem, 1)
                    with pe.Else():
                        pe.drain()
                        skip(pe, [(xg_mm, 2), (slab_used, PER_E), (sc_mm, KD)])

            @block.scalar
            def _(act):
                used = act.value_load(expert_of[0:1, MAXB:MAXB + 1], min_val=1, max_val=MAXB)
                with act.Fori(0, MAXB) as k:
                    with act.If(k < used):
                        for n in range(2):
                            act.wait_ge(xg_mm.sem, xg_mm.at(n + 1) + 2 * k)
                            act.activation(XG[:, 512 * n:512 * n + 512], ps[2][:, 512 * n:512 * n + 512],
                                           ACT.Copy).then_inc(xg_cp.sem, 1)
                        for m in range(KE):
                            act.wait_ge(slab_used.sem, Q_MOE + 2 * m + 1 + PER_E * k)
                            if m != 1:
                                act.wait_ge(hid_done.sem, hid_done.at(max(m - 1, 0)) + KE * k)
                            act.activation(TMPH(m), hid_psum(m, 0), ACT.Silu).then_inc(silu_done.sem, 1)
                        for n in range(2):
                            act.wait_ge(slab_used.sem, Q_MOE + 2 * KE + 4 * n + 4 + PER_E * k)
                            act.activation(YS[:, 512 * n:512 * n + 512], ps[2][:, 512 * n:512 * n + 512],
                                           ACT.Copy).then_inc(y_cp.sem, 1)
                    with act.Else():
                        act.drain()
                        skip(act, [(xg_cp, 2), (silu_done, KE), (y_cp, 2)])

            @block.vector
            def _(dve):
                used = dve.value_load(expert_of[0:1, MAXB:MAXB + 1], min_val=1, max_val=MAXB)
                with dve.Fori(0, MAXB) as k:
                    with dve.If(k < used):
                        step = [0]

                        def S(ins, signal=None):
                            if signal:
                                ins.then_inc(signal.sem, 1)
                                dve.wait_ge(signal.sem, signal.at(1) + k)
                            else:
                                step[0] += 1
                                ins.then_inc(dve_step.sem, 1)
                                dve.wait_ge(dve_step.sem, dve_step.at(step[0]) + N_PK * k)

                        S(dve.scalar_tensor_tensor(out=GK, in0=place[0], scalar=slot_id, in1=gate[0], op0=ALU.is_equal, op1=ALU.mult))
                        S(dve.scalar_tensor_tensor(out=GT1, in0=place[1], scalar=slot_id, in1=gate[1], op0=ALU.is_equal, op1=ALU.mult))
                        S(dve.tensor_tensor(GK, GK, GT1, ALU.add), g_ready)
                        S(dve.tensor_scalar(slot_id, slot_id, float(P), None, ALU.add))
                        for n in range(2):
                            S(dve.tensor_scalar(token_pos[n], token_pos[n], -float(P), None, ALU.add))
                        dve.wait_ge(xg_mm.sem, xg_mm.at(2) + 2 * k)
                        build_places(dve, S, pk_ready)
                        assert step[0] == N_PK
                        for m in range(KE):
                            dve.wait_ge(silu_done.sem, silu_done.at(m + 1) + KE * k)
                            dve.wait_ge(slab_used.sem, Q_MOE + 2 * m + 2 + PER_E * k)
                            dve.tensor_tensor(HK(m), TMPH(m), hid_psum(m, 1), ALU.mult).then_inc(hid_done.sem, 1)
                        for m in range(KD):
                            dve.wait_ge(sc_mm.sem, sc_mm.at(m + 1) + KD * k)
                            if m == 0:
                                dve.wait_ge(evac.sem, evac.at(0) + KD * k)
                            dve.tensor_tensor(h3[:, m, :], scatter_pt(m), h3[:, m, :], ALU.add).then_inc(evac.sem, 1)
                    with dve.Else():
                        dve.drain()
                        skip(dve, [(g_ready, 1), (dve_step, N_PK), (pk_ready, 1), (hid_done, KE), (evac, KD)])
        slab_used.add(MAXB * PER_E)
        for n in range(RING):
            slab_in[n].add(16 * (PER_E // RING) * MAXB)
        for s, n in ((silu_done, KE), (hid_done, KE), (dve_step, N_PK), (evac, KD), (sc_mm, KD), (g_ready, 1),
                     (pk_ready, 1), (y_cp, 2), (xg_cp, 2), (xg_mm, 2)):
            s.add(n * MAXB)
        end_of_block()

        square_block()
        ple_block(Q_PLE1, 1, None, "norm_ple1")
        with nc.Block() as block:
            @block.sync
            def _(sp):
                for n in range(4):
                    sp.wait_ge(u_ready.sem, u_ready.at(2 * n + 2))
                    stored.on(sp.dma_start(o["y"][:, 2 * T * n:2 * T * (n + 1)], u_sb[:, 2 * T * n:2 * T * (n + 1)]), 16)
                sp.wait_ge(stored.sem, stored.count)

            @block.tensor
            def _(pe):
                norm_pe(pe)

            @block.scalar
            def _(act):
                norm_act(act)

            @block.vector
            def _(dve):
                norm_dve(dve, "norm_final")


def slabs(w, tiles=None):
    k, m = w.shape
    return np.ascontiguousarray(w.reshape(k // P, P, m // P, P).transpose(2, 1, 0, 3).reshape(m // P, P, k))


def fm(a):
    return a.reshape(a.shape[0], -1, P).transpose(2, 1, 0)


def col(a):
    return a.reshape(-1, P).T


def shape_constants():
    eye = np.eye(P, dtype=np.float32)
    one = np.ones((P, P), np.float32)
    blk = np.kron(np.eye(2, dtype=np.float32), np.ones((64, 64), np.float32))
    out = {"consts": np.concatenate([eye, one, blk], 1)}
    r64 = np.ones((P, SEQ), np.float32)
    r64[:, ::64] = 0
    out["reset64"] = r64
    s, t = np.meshgrid(np.arange(64), np.arange(64), indexing="ij")
    incl, strict = (s <= t).astype(np.float32), (s < t).astype(np.float32)
    rwmask = np.block([[-incl, 0 * strict], [incl, strict]])
    levels = []
    r = np.arange(P)
    for l in range(6):
        m = 1 << l
        ti, si = r[:, None], r[None, :]
        levels.append(((ti // (2 * m) == si // (2 * m)) & ((ti // m) % 2 == 1) & ((si // m) % 2 == 0)).astype(np.float32))
    sign = np.where(np.arange(P) < 64, -1.0, 1.0).astype(np.float32)[:, None]
    i64 = np.tile(np.eye(64, dtype=np.float32), (2, 1))
    out["ph_rw"] = np.concatenate([rwmask] + levels + [sign, i64], 1)
    sel8 = np.zeros((P, 8, P), np.float32)
    selp = np.zeros((P, 4, P), np.float32)
    for n in range(8):
        sel8[n, n] = 1
        selp[n, n // 2, 64 * (n % 2):64 * (n % 2) + 64] = 1
    last = np.zeros((P, P), np.float32)
    last[P - 1] = 1
    j, t = np.meshgrid(np.arange(P), np.arange(P), indexing="ij")
    ssdmask = np.where(j <= t, 0.0, -1e30)
    glamask = ((j <= t) & (j // 32 == t // 32)).astype(np.float32)
    rs = lambda n, w: np.where(np.arange(w) % n == 0, 0.0, 1.0)[None].repeat(P, 0)
    out["cd"] = (np.concatenate([sel8.reshape(P, -1), selp.reshape(P, -1), last, ssdmask, glamask,
                                 rs(128, SEQ), rs(32, SEQ)], 1), 
                 np.concatenate([rs(8, 40), np.tile(np.arange(P), (P, 1)), np.arange(P)[:, None],
                                 np.triu(np.ones((P, P)), 1)[:, 0:NEXP]], 1))
    return {k: np.ascontiguousarray(a, np.float32) if k != "cd" else [y.astype(np.float32) for y in a] for k, a in out.items()}


def pack(x):
    c = shape_constants()
    a = {}
    a["x"] = fm(np.concatenate([x["x_prompt"][0], x["x_sample"][:, 0]], 0))
    z = lambda n: np.zeros(n, np.float32)
    pad1 = lambda y: np.concatenate([y.reshape(-1), z(P - y.size)])[:, None]
    vecs = {
        "norm_mix0": col(x["norm_mix"][0]), "norm_mix1": col(x["norm_mix"][1]),
        "norm_ffn0": col(x["norm_ffn"][0]), "norm_ffn1": col(x["norm_ffn"][1]),
        "norm_ple0": col(x["norm_ple"][0]), "norm_ple1": col(x["norm_ple"][1]), "norm_final": col(x["norm_final"]),
        "lru_w": col(x["lru_conv_w"][0]), "lru_b": col(x["lru_conv_b"][0]), "b_r": col(x["lru_b_r"][0]),
        "b_i": col(x["lru_b_i"][0]), "lam": col(x["lru_lambda"][0]), "mu": col(x["rwkv_mu"][0]),
        "w0": col(x["rwkv_w0"][0]), "a0": col(x["rwkv_a0"][0]), "k_k": col(x["rwkv_k_k"][0]),
        "k_a": col(x["rwkv_k_a"][0]), "r_k": col(x["rwkv_r_k"][0]), "ln_w": col(x["rwkv_ln_w"][0]),
        "ln_b": col(x["rwkv_ln_b"][0]), "ssd_w": col(x["ssd_conv_w"][0]), "ssd_b": col(x["ssd_conv_b"][0]),
        "ssd_norm": col(x["ssd_norm_w"][0]), "ssd_d": col(np.repeat(x["ssd_d"][0], 64)),
        "alpha_b": col(x["gla_alpha_b"][0]), "gla_norm": col(x["gla_norm_w"][0]),
        "dt_bias": pad1(x["ssd_dt_bias"][0]), "a_log": pad1(x["ssd_a_log"][0]),
    }
    a["vecs"] = np.concatenate([vecs[n] for n, _ in VECS], 1)
    a["consts"] = c["consts"]

    bd = np.zeros((2, P, 4, P), np.float32)
    for n, w in enumerate((x["lru_w_r"][0], x["lru_w_i"][0])):
        for t in range(4):
            bd[n, 0:64, t, 0:64] = w[2 * t]
            bd[n, 64:, t, 64:] = w[2 * t + 1]
    a["ph_ab"] = np.concatenate([bd[0].reshape(P, 512), bd[1].reshape(P, 512),
                                 np.concatenate([x["rwkv_w2"][0], x["rwkv_a2"][0]], 0), x["rwkv_g2"][0],
                                 c["reset64"]], 1)
    hist = x["state_lru_conv"][0].reshape(NS, 3, 4, P).transpose(3, 2, 0, 1)
    shift = x["state_rwkv_shift"][0].reshape(NS, 14, P).transpose(2, 1, 0)
    h0 = x["state_lru_h"][0].reshape(NS, 4, P).transpose(2, 1, 0)
    a["st_ab"] = np.concatenate([hist.reshape(P, 96), shift.reshape(P, 112), h0.reshape(P, 32)], 1)
    w = x["w_in_ab"][0]
    order = [n if k == "xa" else 4 + n if k == "ga" else 8 + n for k, n in AB_TILES]
    a["w_in_ab"] = slabs(w)[order]
    a["w_out_ab"] = slabs(x["w_out_ab"][0])
    a["ph_rw"] = c["ph_rw"]
    a["s_rw"] = x["state_rwkv_wkv"][0].reshape(NS, 4, 2 * 64, 64).transpose(2, 0, 1, 3).reshape(P, 2048)
    flat = lambda y: y.reshape(-1, y.shape[-1])
    for n in ("w_in_ab", "w_out_ab"):
        a[n] = flat(a[n])
    g, u = slabs(x["ffn_w_gate"][0]), slabs(x["ffn_w_up"][0])
    a["w_gu"] = flat(np.stack([g, u], 1))
    a["w_dn"] = slabs(x["ffn_w_down"][0]).reshape(KD * P, 2, SLAB).reshape(KD, P, 2, SLAB).transpose(0, 2, 1, 3).reshape(-1, SLAB)
    for l in range(2):
        a[f"w_ple{l}"] = flat(np.concatenate([slabs(x["w_ple_gate"][l]), slabs(x["w_ple_proj"][l])], 2))
    a["p"] = np.stack([fm(np.concatenate([x["p_prompt"][l, 0], x["p_sample"][l, :, 0]], 0)) for l in range(2)])
    w = x["w_in_cd"][0]
    z_, xbc, dt, q, k, v_, g, al = np.split(w, np.cumsum([512, 1024, 8, 256, 256, 512, 512]), 1)
    tail = np.concatenate([dt, np.zeros((D, 24), np.float32), al], 1)
    body = slabs(np.concatenate([xbc, q, k, v_, z_, g], 1))
    tail = tail.reshape(KD, P, 48).transpose(1, 0, 2).reshape(1, P, KD * 48)
    a["w_in_cd"] = flat(np.concatenate([np.concatenate([tail, np.zeros((1, P, D - KD * 48), np.float32)], 2), body], 0))
    alpha = np.zeros((P, 256), np.float32)
    alpha[32:48] = x["gla_alpha_up"][0]
    router = x["moe_router"][0].reshape(KD, P, NEXP).transpose(1, 0, 2).reshape(P, -1)
    a["ph_cd"] = np.concatenate([c["cd"][0], alpha, router, c["cd"][1]], 1)
    a["st_cd"] = x["state_ssd_conv"][0].reshape(NS, 3, 8, P).transpose(3, 2, 0, 1).reshape(P, -1)
    a["s_ssd"] = x["state_ssd"][0].reshape(NS, 4, P, P).transpose(2, 0, 1, 3).reshape(P, -1)
    a["s_gla"] = x["state_gla"][0].reshape(NS, 2, P, P).transpose(2, 0, 1, 3).reshape(P, -1)
    a["w_out_cd"] = flat(slabs(x["w_out_cd"][0]))
    g, u = [x[n][0].reshape(NEXP, KD, P, KE, P).transpose(0, 3, 2, 1, 4).reshape(NEXP, KE, P, D)
            for n in ("moe_w_gate", "moe_w_up")]
    a["w_moe_gu"] = np.stack([g, u], 2).reshape(-1, D)
    a["w_moe_dn"] = x["moe_w_down"][0].reshape(NEXP, KE, P, KD, P).transpose(0, 3, 2, 1, 4).reshape(-1, FFE)
    return {k: np.ascontiguousarray(y) for k, y in a.items()}


def unpack(r):
    tok = lambda a, f: a.reshape(P, f, -1).transpose(2, 1, 0).reshape(a.size // (P * f), f * P)
    y = tok(r["y"], KD)
    small = r["ab_small"]
    conv_p, conv_s = small[:, 0:12].reshape(P, 4, 3), small[:, 12:108].reshape(P, 4, NS, 3)
    shift, lru_h = tok(small[:, 108:234], 14), tok(small[:, 234:270], 4)
    wkv_p = r["wkv_p"].reshape(2, 64, 4, 64).transpose(2, 0, 3, 1).reshape(8, 64, 64)
    wkv_s = r["wkv_s"].reshape(2, 64, NS, 4, 64).transpose(2, 3, 0, 1, 4).reshape(NS, 8, 64, 64)
    c2 = r["cd_small"]
    conv2_p, conv2_s = c2[:, 0:24].reshape(P, 8, 3), c2[:, 24:216].reshape(P, 8, NS, 3)
    ssd_p = r["ssd_p"].reshape(P, 8, 64).transpose(1, 2, 0)
    ssd_s = r["ssd_s"].reshape(P, NS, 4, P).transpose(1, 2, 0, 3).reshape(NS, 8, 64, P)
    gla_p = r["gla_p"].reshape(2, 64, 2, P).transpose(2, 0, 1, 3).reshape(4, 64, P)
    gla_s = r["gla_s"].reshape(2, 64, NS, 2, P).transpose(2, 3, 0, 1, 4).reshape(NS, 4, 64, P)
    hist_p = lambda c: c.transpose(2, 1, 0).reshape(3, -1)
    hist_s = lambda c: c.transpose(2, 3, 1, 0).reshape(NS, 3, -1)
    outs = (y[:SEQ][None], y[SEQ:][:, None],
            hist_p(conv_p)[None, None], lru_h[0:1][None], shift[0:1][None], wkv_p[None, None],
            hist_p(conv2_p)[None, None], ssd_p[None, None], gla_p[None, None],
            hist_s(conv_s)[None], lru_h[1:][None], shift[1:][None], wkv_s[None],
            hist_s(conv2_s)[None], ssd_s[None], gla_s[None])
    return tuple(np.ascontiguousarray(a) for a in outs)


OUTPUTS = {"wkv_p": 256, "wkv_s": 2048, "ab_small": 270, "ssd_p": 512, "cd_small": 216, "ssd_s": 4096,
           "gla_p": 256, "gla_s": 2048, "y": KD * T}


def kernel(**inputs):
    import concourse.bacc as _bacc
    from concourse.bass_utils import run_bass_kernel_spmd as _run

    arrays = pack({k: np.asarray(a) for k, a in inputs.items()})
    nc = _bacc.Bacc("TRN2", target_bir_lowering=False, num_devices=1)
    i = {k: nc.dram_tensor("in_" + k, a.shape, F32, kind="ExternalInput").ap() for k, a in arrays.items()}
    o = {k: nc.dram_tensor("out_" + k, [P, c], F32, kind="ExternalOutput").ap() for k, c in OUTPUTS.items()}
    build_program(nc, i, o)
    r = _run(nc, [{"in_" + k: a for k, a in arrays.items()}], core_ids=[0])
    return unpack({k: r.results[0]["out_" + k] for k in OUTPUTS})
```
